# Optimizing a Trainium2 kernel written in Bass

```python
import jax, jax.numpy as jnp
from jax import lax
import numpy as np

D_MODEL = 1024
BATCH = 1
SEQ = 2048
DEPTH = 1

D_MIX = D_MODEL
D_CONV = D_MIX // 2
D_REC = D_MIX - D_CONV
CONV_WIDTH = 31
REC_EXPAND = 128
REC_HEADS = D_REC // REC_EXPAND
REC_DK = REC_EXPAND
REC_DV = D_REC // REC_HEADS
CHUNK = 64
D_IN = 2 * D_CONV + 4 * D_REC
IN_SPLITS = (D_CONV, 2 * D_CONV, 2 * D_CONV + D_REC, 2 * D_CONV + 2 * D_REC, 2 * D_CONV + 3 * D_REC)
N_GROUPS = 4
EXPERTS_PER_GROUP = 8
N_EXPERTS = N_GROUPS * EXPERTS_PER_GROUP
TOP_K = 2
D_EXPERT = D_MODEL // 4
EXPERT_BLOCK = 128
EPS = 1e-6

kernel_name = "hybrid_conv_hgrn2_hmoe_adaln"

def rms_norm(x, gain):
    xf = x.astype(jnp.float32)
    y = xf * lax.rsqrt(jnp.mean(xf * xf, axis=-1, keepdims=True) + EPS)
    return (y * gain.astype(jnp.float32)).astype(x.dtype)

def layer_norm(x, gain, bias):
    xf = x.astype(jnp.float32)
    mu = jnp.mean(xf, axis=-1, keepdims=True)
    xc = xf - mu
    y = xc * lax.rsqrt(jnp.mean(xc * xc, axis=-1, keepdims=True) + EPS)
    return (y * gain.astype(jnp.float32) + bias.astype(jnp.float32)).astype(x.dtype)

def conv_module(val, gate, dw_kernel, dw_bias, ln_gain, ln_bias):
    u = val * jax.nn.sigmoid(gate)
    u = lax.conv_general_dilated(
        u, dw_kernel[:, None, :].astype(u.dtype), window_strides=(1,),
        padding=[(CONV_WIDTH - 1, 0)],
        dimension_numbers=('NWC', 'WIO', 'NWC'),
        feature_group_count=D_CONV) + dw_bias.astype(u.dtype)
    u = layer_norm(u, ln_gain, ln_bias)
    return jax.nn.silu(u)

def hgrn2(q, f_logit, i, g, lb, norm_gain):
    B, S, _ = q.shape
    N = S // CHUNK
    out_dtype = q.dtype
    f32 = jnp.float32
    qf = jax.nn.silu(q.astype(f32))
    forget = lb + (1.0 - lb) * jax.nn.sigmoid(f_logit.astype(f32))
    k = 1.0 - forget
    log_f = jnp.log(forget)

    def heads(t, d):
        return t.reshape(B, N, CHUNK, REC_HEADS, d).transpose(0, 3, 1, 2, 4)

    qh, kh, lfh = heads(qf, REC_DK), heads(k, REC_DK), heads(log_f, REC_DK)
    vh = heads(i.astype(f32), REC_DV)
    b = jnp.cumsum(lfh, axis=3)
    b_last = b[:, :, :, -1:, :]
    q_dec = qh * jnp.exp(b)
    k_inv = kh * jnp.exp(-b)
    scores = jnp.einsum('bhncd,bhnsd->bhncs', q_dec, k_inv)
    causal = jnp.tril(jnp.ones((CHUNK, CHUNK), dtype=bool))
    scores = jnp.where(causal, scores, 0.0)
    o_intra = jnp.einsum('bhncs,bhnse->bhnce', scores, vh)

    k_end = kh * jnp.exp(b_last - b)
    chunk_state = jnp.einsum('bhncd,bhnce->nbhde', k_end, vh)
    chunk_decay = jnp.exp(b_last[:, :, :, 0, :]).transpose(2, 0, 1, 3)

    def step(state, inp):
        d_state, a = inp
        return state * a[..., None] + d_state, state

    s0 = jnp.zeros((B, REC_HEADS, REC_DK, REC_DV), f32)
    _, s_prev = lax.scan(step, s0, (chunk_state, chunk_decay))
    o_inter = jnp.einsum('bhncd,nbhde->bhnce', q_dec, s_prev)
    o = rms_norm(o_intra + o_inter, norm_gain)
    o = o.transpose(0, 2, 3, 1, 4).reshape(B, S, D_REC)
    return (o * jax.nn.silu(g.astype(f32))).astype(out_dtype)

def hier_moe(h, w_rg, b_rg, w_re, b_re, w_gate, w_up, w_down):
    B, S, D = h.shape
    T = B * S
    dt = h.dtype
    ht = h.reshape(T, D)
    f32 = jnp.float32
    group_p = jax.nn.softmax((ht @ w_rg).astype(f32) + b_rg.astype(f32), axis=-1)
    g_prob, g_idx = lax.top_k(group_p, 1)
    e_logit = ((ht @ w_re).astype(f32) + b_re.astype(f32)).reshape(T, N_GROUPS, EXPERTS_PER_GROUP)
    e_logit = jnp.take_along_axis(e_logit, g_idx[:, :, None], axis=1)[:, 0]
    e_p = jax.nn.softmax(e_logit, axis=-1)
    e_prob, e_local = lax.top_k(e_p, TOP_K)
    e_prob = e_prob / jnp.sum(e_prob, axis=-1, keepdims=True)
    weights = (g_prob * e_prob).reshape(-1)
    expert_ids = (g_idx * EXPERTS_PER_GROUP + e_local).reshape(-1)
    A = T * TOP_K
    token_ids = jnp.arange(A) // TOP_K

    order = jnp.argsort(expert_ids)
    sorted_e = expert_ids[order]
    sorted_tok = token_ids[order]
    counts = jnp.bincount(expert_ids, length=N_EXPERTS)
    padded = (counts + EXPERT_BLOCK - 1) // EXPERT_BLOCK * EXPERT_BLOCK
    pad_end = jnp.cumsum(padded)
    pad_start = pad_end - padded
    start = jnp.cumsum(counts) - counts
    dest = pad_start[sorted_e] + (jnp.arange(A) - start[sorted_e])
    n_rows = -(-A // EXPERT_BLOCK) * EXPERT_BLOCK + N_EXPERTS * EXPERT_BLOCK
    n_blocks = n_rows // EXPERT_BLOCK
    x_pad = jnp.zeros((n_rows, D), dt).at[dest].set(ht[sorted_tok])
    block_start = jnp.arange(n_blocks) * EXPERT_BLOCK
    block_expert = jnp.minimum(jnp.sum(block_start[:, None] >= pad_end[None, :], axis=1), N_EXPERTS - 1)

    def expert_block(args):
        xb, e = args
        hb = jax.nn.silu(xb @ w_gate[e]) * (xb @ w_up[e])
        return hb @ w_down[e]

    y_pad = lax.map(expert_block, (x_pad.reshape(n_blocks, EXPERT_BLOCK, D), block_expert))
    y_sorted = y_pad.reshape(n_rows, D)[dest] * weights[order][:, None].astype(dt)
    out = jnp.zeros((T, D), dt).at[sorted_tok].add(y_sorted)
    return out.reshape(B, S, D)

def setup_inputs(seed: int = 0) -> dict:
    key = jax.random.key(seed)
    ks = jax.random.split(key, 24)
    nrm = jax.random.normal
    f32 = jnp.float32
    L, D = DEPTH, D_MODEL
    return {
        "x": nrm(ks[0], (BATCH, SEQ, D), f32),
        "c": nrm(ks[1], (BATCH, D), f32),
        "w_ada": nrm(ks[2], (L, D, 6 * D), f32) * (0.5 * D ** -0.5),
        "b_ada": nrm(ks[3], (L, 6 * D), f32) * 0.01,
        "g_pre_mix": 1.0 + 0.01 * nrm(ks[4], (L, D), f32),
        "g_post_mix": 1.0 + 0.01 * nrm(ks[5], (L, D), f32),
        "w_in": nrm(ks[6], (L, D, D_IN), f32) * D ** -0.5,
        "dw_kernel": nrm(ks[7], (L, CONV_WIDTH, D_CONV), f32) * CONV_WIDTH ** -0.5,
        "dw_bias": nrm(ks[8], (L, D_CONV), f32) * 0.01,
        "conv_ln_gain": 1.0 + 0.01 * nrm(ks[9], (L, D_CONV), f32),
        "conv_ln_bias": nrm(ks[10], (L, D_CONV), f32) * 0.01,
        "lb_logits": nrm(ks[11], (L + 1, D_REC), f32) * 0.1,
        "rec_norm_gain": 1.0 + 0.01 * nrm(ks[12], (L, REC_DV), f32),
        "w_out": nrm(ks[13], (L, D_MIX, D), f32) * D_MIX ** -0.5,
        "g_pre_ffn": 1.0 + 0.01 * nrm(ks[14], (L, D), f32),
        "g_post_ffn": 1.0 + 0.01 * nrm(ks[15], (L, D), f32),
        "w_router_group": nrm(ks[16], (L, D, N_GROUPS), f32) * D ** -0.5,
        "b_router_group": nrm(ks[17], (L, N_GROUPS), f32) * 0.01,
        "w_router_expert": nrm(ks[18], (L, D, N_EXPERTS), f32) * D ** -0.5,
        "b_router_expert": nrm(ks[19], (L, N_EXPERTS), f32) * 0.01,
        "w_gate": nrm(ks[20], (L, N_EXPERTS, D, D_EXPERT), f32) * D ** -0.5,
        "w_up": nrm(ks[21], (L, N_EXPERTS, D, D_EXPERT), f32) * D ** -0.5,
        "w_down": nrm(ks[22], (L, N_EXPERTS, D_EXPERT, D), f32) * D_EXPERT ** -0.5,
    }

def reference(x, c, w_ada, b_ada, g_pre_mix, g_post_mix, w_in, dw_kernel, dw_bias,
              conv_ln_gain, conv_ln_bias, lb_logits, rec_norm_gain, w_out, g_pre_ffn,
              g_post_ffn, w_router_group, b_router_group, w_router_expert, b_router_expert,
              w_gate, w_up, w_down):
    cond = jax.nn.silu(c)
    lb_table = jnp.cumsum(jax.nn.softmax(lb_logits.astype(jnp.float32), axis=0), axis=0)
    for l in range(DEPTH):
        mod = (cond @ w_ada[l] + b_ada[l])[:, None, :]
        sh1, sc1, gt1, sh2, sc2, gt2 = jnp.split(mod, 6, axis=-1)

        h = rms_norm(x, g_pre_mix[l]) * (1.0 + sc1) + sh1
        proj = h @ w_in[l]
        cv, cg, q, f, i, g = jnp.split(proj, IN_SPLITS, axis=-1)
        y_conv = conv_module(cv, cg, dw_kernel[l], dw_bias[l], conv_ln_gain[l], conv_ln_bias[l])
        y_rec = hgrn2(q, f, i, g, lb_table[l], rec_norm_gain[l])
        y = jnp.concatenate([y_conv, y_rec], axis=-1) @ w_out[l]
        x = x + gt1 * rms_norm(y, g_post_mix[l])

        h = rms_norm(x, g_pre_ffn[l]) * (1.0 + sc2) + sh2
        y = hier_moe(h, w_router_group[l], b_router_group[l], w_router_expert[l],
                     b_router_expert[l], w_gate[l], w_up[l], w_down[l])
        x = x + gt2 * rms_norm(y, g_post_ffn[l])
    return x


_drawn_inputs = setup_inputs


def setup_inputs(seed=0):
    import zlib

    import numpy as np

    out = dict(_drawn_inputs(seed))
    spreads = {}
    factors = {'g_post_mix': 3.306,
     'dw_bias': 2.996,
     'conv_ln_gain': 3.862,
     'conv_ln_bias': 3.623,
     'lb_logits': 3.434,
     'rec_norm_gain': 3.389,
     'g_post_ffn': 8.0,
     'b_router_expert': 2.958}
    for name, (base, spread) in spreads.items():
        noise = np.random.default_rng([zlib.crc32(name.encode()), seed]).standard_normal(out[name].shape)
        drawn = base * np.exp(spread * noise) if base else spread * noise
        out[name] = __import__('jax').numpy.asarray(drawn.astype(out[name].dtype))
    for name, factor in factors.items():
        out[name] = (out[name] * factor).astype(out[name].dtype)
    return out
```

```python
import concourse.bass as bass
from concourse import mybir
from contextlib import ExitStack

F32 = mybir.dt.float32
I32 = mybir.dt.int32
U32 = mybir.dt.uint32
BF16 = mybir.dt.bfloat16
ALU = mybir.AluOpType
ACT = mybir.ActivationFunctionType
AX = mybir.AxisListType

P = 128
D = 1024
KD = D // P
SEQ = 2048
DC = 512
NCH = DC // P
NH = 4
CW = 31
HALO = CW - 1
T = 512
NB = SEQ // T
NT = T // P
CH = 64
NTILES = SEQ // P
NG, NEG = 4, 8
NE = NG * NEG
FE = 256
NR = NG + NE
EPS = 1e-6
NBLK = 64
MINBLK = 2 * SEQ // P
WSLOTS = 4
TAB = NBLK + 2

VEC = {}
_at = 0
for _name, _n in (("c", 8), ("b_ada", 48), ("g_pre_mix", 8), ("g_post_mix", 8), ("g_pre_ffn", 8),
                  ("g_post_ffn", 8), ("dw_bias", 4), ("conv_ln_gain", 4), ("conv_ln_bias", 4),
                  ("lb_logits", 8), ("rec_norm_gain", 1)):
    VEC[_name] = (_at, _at + _n)
    _at += _n
NVEC = _at


def wait(eng, sem, value):
    if isinstance(value, int) and value <= 0:
        return
    eng.wait_ge(sem, value)


def wait_apart(eng, sem, value, passed):
    eng.wait_ge(sem, value)
    eng.sem_inc(passed, 1)


class Chain:

    def __init__(self, eng, sem, base=0):
        self.eng, self.sem, self.base, self.n = eng, sem, base, 0

    def step(self, ins):
        ins.then_inc(self.sem, 1)
        self.n += 1

    def sync(self):
        wait(self.eng, self.sem, self.base + self.n)

    def link(self, ins):
        self.step(ins)
        self.sync()


def constants_phase(nc, ap, c):
    with ExitStack() as ctx:
        sb = lambda n, s, d=F32: ctx.enter_context(nc.sbuf_tensor(n, s, d))
        sem = lambda n: ctx.enter_context(nc.semaphore(n))
        vrows = sb("vrows", [NVEC, P])
        dwrows = sb("dwrows", [CW, DC])
        wada = sb("wada", [P, 2, KD, D])
        cond = sb("cond", [P, KD])
        mod = sb("mod", [P, 6 * KD])
        lbt = sb("lbt", [P, 4, NCH])
        diag = sb("diag", [P, 2, 4, P])
        pv = ctx.enter_context(nc.psum_tensor("pv", [P, 512], F32))
        pk = ctx.enter_context(nc.psum_tensor("pk", [P, 512], F32))
        pm = ctx.enter_context(nc.psum_tensor("pm", [P, 512], F32))
        pg = [ctx.enter_context(nc.psum_tensor(f"pg{i}", [P, 512], F32)) for i in range(2)]
        pr = ctx.enter_context(nc.psum_tensor("pr", [P, 512], F32))
        vec_in, wada_in0, wada_in1 = sem("vec_in"), sem("wada_in0"), sem("wada_in1")
        wada_in = [wada_in0, wada_in1]
        pool_step, masks_ready = sem("pool_step"), sem("masks_ready")
        turned, cols_ready, cond_ready = sem("turned"), sem("cols_ready"), sem("cond_ready")
        mod_done, mod_ready, diag_ready, row_done = sem("mod_done"), sem("mod_ready"), sem("diag_ready"), sem("row_done")
        dve_step, lb_in, lb_exp = sem("dve_step0"), sem("lb_in"), sem("lb_exp")
        rbias_done = sem("rbias_done")
        block = ctx.enter_context(nc.Block())
        NLOAD = len(VEC) + 5
        MODS = 6

        @block.sync
        def _(sp):
            for name, (a, b) in VEC.items():
                src = ap[name]
                src = src.rearrange("a (k p) -> (a k) p", p=P)
                sp.dma_start(vrows[a:b, :], src).then_inc(vec_in, 16)
            sp.dma_start(dwrows[:, :], ap["dw_kernel"][0]).then_inc(vec_in, 16)
            sp.dma_start(c.wroute[:, :, 0:NG], ap["w_router_group"][0].rearrange("(k p) n -> p k n", p=P),
                         allow_slow_non_contiguous=True).then_inc(vec_in, 16)
            sp.dma_start(c.wroute[:, :, NG:NR],
                         ap["w_router_expert"][0].rearrange("(k p) n -> p k n", p=P)).then_inc(vec_in, 16)
            sp.dma_start(c.brow[0:1, 0:NG], ap["b_router_group"]).then_inc(vec_in, 16)
            sp.dma_start(c.brow[0:1, NG:NR], ap["b_router_expert"]).then_inc(vec_in, 16)
            for m in range(MODS):
                if m >= 2:
                    sp.wait_ge(mod_done, m - 1)
                sp.dma_start(wada[:, m % 2], ap["w_ada"][0, :, m * D:(m + 1) * D]
                             .rearrange("(k p) n -> p k n", p=P)).then_inc(wada_in[m % 2], 16)

        @block.gpsimd
        def _(pool):
            ch = Chain(pool, pool_step)
            ch.step(nc.gpsimd.memset(c.ident[:], 0.0))
            ch.step(nc.gpsimd.memset(c.ones[:], 1.0))
            ch.step(nc.gpsimd.memset(c.causal[:], 1.0))
            ch.step(nc.gpsimd.memset(c.restart[:], 1.0))
            ch.step(nc.gpsimd.memset(c.epsc[:], EPS))
            ch.sync()
            ch.step(nc.gpsimd.affine_select(out=c.ident[:], in_=c.ident[:], compare_op=ALU.not_equal, fill=1.0,
                                            base=0, pattern=[[-1, P]], channel_multiplier=1))
            ch.step(nc.gpsimd.affine_select(out=c.causal[:], in_=c.causal[:], compare_op=ALU.is_ge, fill=0.0,
                                            base=0, pattern=[[1, P]], channel_multiplier=-1))
            ch.sync()
            ch.step(nc.gpsimd.memset(c.causal[0:CH, CH:P], 0.0))
            ch.step(nc.gpsimd.memset(c.restart[:].rearrange("p (n k) -> p n k", k=CH)[:, :, 0:1], 0.0))
            ch.sync()
            nc.gpsimd.memset(c.halo0[:], 0.0).then_inc(masks_ready, 1)

        @block.tensor
        def _(pe):
            pe.wait_ge(masks_ready, 1)
            pe.wait_ge(vec_in, 16 * NLOAD)
            nc.tensor.transpose(pv[:, 0:NVEC], vrows[:, :], c.ident[0:NVEC, 0:NVEC])
            for k in range(NCH):
                last = nc.tensor.transpose(pk[:, k * CW:(k + 1) * CW], dwrows[:, k * P:(k + 1) * P],
                                           c.ident[0:CW, 0:CW])
            last.then_inc(turned, 1)
            pe.wait_ge(cond_ready, 1)
            for m in range(MODS):
                pe.wait_ge(wada_in[m % 2], 16 * (m // 2 + 1))
                for j in range(KD):
                    for k in range(KD):
                        last = nc.tensor.matmul(pm[:, m * KD + j:m * KD + j + 1], wada[:, m % 2, k, j * P:(j + 1) * P],
                                                cond[:, k:k + 1], start=(k == 0), stop=(k == KD - 1))
                last.then_inc(mod_done, 1)
            for r in range(2):
                pe.wait_ge(diag_ready, r + 1)
                nc.tensor.matmul(pg[r % 2][:], c.ones[:], diag[:, r % 2].rearrange("p a b -> p (a b)"),
                                 start=True, stop=True).then_inc(row_done, 1)
            pe.wait_ge(mod_ready, 1)
            for k in range(KD):
                last = nc.tensor.matmul(pr[0:1, 0:NR], c.shift2[:, k:k + 1], c.wroute[:, k, :],
                                        start=(k == 0), stop=(k == KD - 1))
            last.then_inc(rbias_done, 1)

        @block.scalar
        def _(act):
            act.wait_ge(cols_ready, 1)
            nc.scalar.activation(cond[:], c.cols[:, VEC["c"][0]:VEC["c"][1]], ACT.Silu).then_inc(cond_ready, 1)
            act.wait_ge(lb_in, 1)
            nc.scalar.activation(lbt[:, 1:3], lbt[:, 1:3], ACT.Exp).then_inc(lb_exp, 1)

        @block.vector
        def _(dve):
            col = lambda n: c.cols[:, VEC[n][0]:VEC[n][1]]
            ch = Chain(dve, dve_step)
            dve.wait_ge(turned, 1)
            nc.vector.tensor_copy(c.taps[:], pk[:, 0:NCH * CW])
            ch.step(nc.vector.tensor_copy(c.cols[:], pv[:, 0:NVEC]))
            ch.sync()
            dve.sem_inc(cols_ready, 1)
            lb0 = VEC["lb_logits"][0]
            l0, l1 = c.cols[:, lb0:lb0 + NCH], c.cols[:, lb0 + NCH:lb0 + 2 * NCH]
            ch.link(nc.vector.tensor_tensor(lbt[:, 0], l0, l1, ALU.max))
            ch.step(nc.vector.tensor_tensor(lbt[:, 1], l0, lbt[:, 0], ALU.subtract))
            nc.vector.tensor_tensor(lbt[:, 2], l1, lbt[:, 0], ALU.subtract).then_inc(lb_in, 1)
            dve.wait_ge(lb_exp, 1)
            ch.link(nc.vector.tensor_tensor(lbt[:, 3], lbt[:, 1], lbt[:, 2], ALU.add))
            ch.link(nc.vector.reciprocal(lbt[:, 0], lbt[:, 3]))
            ch.link(nc.vector.tensor_tensor(c.lb[:], lbt[:, 1], lbt[:, 0], ALU.mult))
            ch.step(nc.vector.tensor_scalar(c.oneless[:], c.lb[:], -1.0, 1.0, ALU.mult, ALU.add))
            dve.wait_ge(mod_done, MODS)
            ch.link(nc.vector.tensor_tensor(mod[:], pm[:, 0:6 * KD], col("b_ada"), ALU.add))
            m = lambda i: mod[:, i * KD:(i + 1) * KD]
            ch.step(nc.vector.scalar_tensor_tensor(out=c.scale1[:], in0=m(1), scalar=1.0, in1=col("g_pre_mix"),
                                                   op0=ALU.add, op1=ALU.mult))
            ch.step(nc.vector.scalar_tensor_tensor(out=c.scale2[:], in0=m(4), scalar=1.0, in1=col("g_pre_ffn"),
                                                   op0=ALU.add, op1=ALU.mult))
            ch.step(nc.vector.tensor_tensor(c.gcol[:, 0:KD], m(2), col("g_post_mix"), ALU.mult))
            ch.step(nc.vector.tensor_tensor(c.gcol[:, KD:2 * KD], m(5), col("g_post_ffn"), ALU.mult))
            ch.step(nc.vector.tensor_copy(c.shift1[:], m(0)))
            nc.vector.tensor_copy(c.shift2[:], m(3)).then_inc(mod_ready, 1)
            ch.sync()
            for r in range(2):
                for j in range(4):
                    last = nc.vector.tensor_scalar(diag[:, r, j], c.ident[:], c.gcol[:, r * 4 + j:r * 4 + j + 1],
                                                   None, ALU.mult)
                last.then_inc(diag_ready, 1)
            for r in range(2):
                dve.wait_ge(row_done, r + 1)
                nc.vector.tensor_copy(c.grow[:, r * 512:(r + 1) * 512], pg[r][:])
            dve.wait_ge(rbias_done, 1)
            ch.link(nc.vector.tensor_tensor(c.brow[:], c.brow[:], pr[0:1, 0:NR], ALU.add))
            for k in range(KD):
                ch.step(nc.vector.tensor_scalar(c.wroute[:, k, :], c.wroute[:, k, :], c.scale2[:, k:k + 1],
                                                None, ALU.mult))
            ch.step(nc.vector.memset(c.state[:], 0.0))
            ch.step(nc.vector.memset(c.scoreT[:], 0.0))


def mixer_phase(nc, ap, c):
    with ExitStack() as ctx:
        sb = lambda n, s, d=F32: ctx.enter_context(nc.sbuf_tensor(n, s, d))
        sem = lambda n: ctx.enter_context(nc.semaphore(n))
        col = lambda n, k: c.cols[:, VEC[n][0] + k:VEC[n][0] + k + 1]

        xt = sb("xt", [P, 2, D])
        hT = sb("hT", [P, KD, T])
        NSLOT = 3
        win = sb("win", [P, NSLOT, KD, 256])
        wo = sb("wo", [P, KD, D])
        u = sb("u", [P, NCH, HALO + T])
        cv = sb("cv", [P, NCH, T])
        yT = sb("yT", [P, KD, T])
        qd = sb("qd", [P, NH, T])
        ki = sb("ki", [P, NH, T])
        ke = sb("ke", [P, NH, T])
        v = sb("v", [P, NT, DC])
        gs = sb("gs", [P, NT, DC])
        ob = sb("ob", [P, NT, DC])
        scr = sb("scr", [P, D])
        yt = sb("yt", [P, 2, D])
        xres = sb("xres", [P, 2, D])
        tmp = sb("tmp", [P, 512])
        decay = sb("decay", [P, NH, T // CH])
        sums = sb("sums", [P, 64])
        bank = [ctx.enter_context(nc.psum_tensor(f"bank{i}", [P, 512], F32)) for i in range(4)]
        pS = ctx.enter_context(nc.psum_tensor("pS", [P, 512], F32))
        pO = ctx.enter_context(nc.psum_tensor("pO", [P, 512], F32))
        pD = ctx.enter_context(nc.psum_tensor("pD", [P, 512], F32))
        pT = ctx.enter_context(nc.psum_tensor("pT", [P, 512], F32))

        x_in = [sem("x_in0"), sem("x_in1")]
        win_in = [sem(f"win_in{i}") for i in range(NSLOT)]
        wo_in = sem("wo_in")
        res_in = [sem("res_in0"), sem("res_in1")]
        x_rstd, x_normed, xT_ready, hT_ready = sem("x_rstd"), sem("x_normed"), sem("xT_ready"), sem("hT_ready")
        proj_ready = sem("proj_ready")
        gate_sig, u_ready = sem("gate_sig"), sem("u_ready")
        q_parts, g_parts, v_ready = sem("q_parts"), sem("g_parts"), sem("v_ready")
        forget_ready, logf_ready, b_ready = sem("forget_ready"), sem("logf_ready"), sem("b_ready")
        exp_ready, exp_used = sem("exp_ready"), sem("exp_used")
        y_ready, y_rstd, x1_ready, x1_rstd, xn_ready = sem("y_ready"), sem("y_rstd"), sem("x1_ready"), sem("x1_rstd"), sem("xn_ready")
        y_cleared = sem("y_cleared")
        res_free, pool_passed, dve_passed, sp_passed = sem("res_free"), sem("pool_passed"), sem("dve_passed"), sem("sp_passed")
        rT_ready, rin_ready, logit_ready, logit_saved = sem("rT_ready"), sem("rin_ready"), sem("logit_ready"), sem("logit_saved")
        x1_stored, xn_stored = [sem("x1_stored0"), sem("x1_stored1")], [sem("xn_stored0"), sem("xn_stored1")]
        mean_ready, centred, squared, var_ready, ln_rstd, ln_normed, ln_sig = (
            sem("mean_ready"), sem("centred"), sem("squared"), sem("var_ready"), sem("ln_rstd"), sem("ln_normed"), sem("ln_sig"))
        score_ready, masked, keT_psum, keT_ready = sem("score_ready"), sem("masked"), sem("keT_psum"), sem("keT_ready")
        dstate_ready, state_ready, o_ready, o_saved = sem("dstate_ready"), sem("state_ready"), sem("o_ready"), sem("o_saved")
        o_squared, o_ms, o_rstd, o_gated = sem("o_squared"), sem("o_ms"), sem("o_rstd"), sem("o_gated")
        oT_psum, yT_rec, yT_conv = sem("oT_psum"), sem("yT_rec"), sem("yT_conv")
        a_norm, a_out, a_head, a_rec, a_ln = (sem(n) for n in ("a_norm", "a_out", "a_head", "a_rec", "a_ln"))
        conv_step, v_head, y_normed, v_rec, v_ln, g_done, diff_ready = (
            sem(n) for n in ("conv_step", "v_head", "y_normed", "v_rec", "v_ln", "g_done", "diff_ready"))
        CONV_STEPS = NCH * CW + NCH
        block = ctx.enter_context(nc.Block())

        x_d, x1_d, xn_d = ap["x"][0], ap["x1"], ap["xn"]
        w_d = ap["w_in"][0].rearrange("(k p) n -> p k n", p=P)
        NPIECE = 12
        GATE, Q, FG, VI, GG = DC, 2 * DC, 3 * DC, 4 * DC, 5 * DC
        PIECES = [((j * P, P), (GATE + j * P, P)) for j in range(NCH)]
        PIECES += [((Q + j * P, P), (FG + j * P, P)) for j in range(NH)]
        PIECES += [((GG + j * 256, 256),) for j in range(2)] + [((VI + j * 256, 256),) for j in range(2)]
        TU, AU, OU = 8, 24, 16

        def win_bytes(t, j):
            per_block = sum(16 * len(PIECES[i]) for i in range(NPIECE) if i % NSLOT == j % NSLOT)
            return t * per_block + sum(16 * len(PIECES[i]) for i in range(j + 1) if i % NSLOT == j % NSLOT)

        ORDER = [("y", 0), ("y", 1), ("r", 0), ("y", 2), ("r", 1), ("y", 3), ("r", 2), ("r", 3)]
        BANKS = {step: 2 * n for n, step in enumerate(ORDER)}

        def reader(stage, n, t):
            if stage == "T":
                return hT_ready, t * TU + n + 1
            if stage == "A":
                if n < 8:
                    return u_ready, t * NCH + n // 2 + 1
                if n < 16:
                    return q_parts, (t * NH + (n - 8) // 2) * 3 + 2 + n % 2
                if n < 20:
                    return g_parts, t * 8 + 2 * (n - 16) + 2
                return v_ready, t * 4 + (n - 20) + 1
            kind, i = ORDER[n // 2]
            return (y_normed if kind == "y" else rin_ready), t * 8 + 2 * i + n % 2 + 1

        @block.sync
        def _(sp):
            sp.dma_start(wo[:], ap["w_out"][0].rearrange("(k p) n -> p k n", p=P)).then_inc(wo_in, 16)

            def load(t):
                for i in range(NT):
                    wait(sp, xT_ready, t * TU + 2 * (i - 2) + 2)
                    sp.sem_inc(sp_passed, 1)
                    sp.dma_start(xt[:, i % 2], x_d[bass.ds(t * T + i * P, P), :]).then_inc(x_in[i % 2], 16)
                for j, cols in enumerate(PIECES):
                    wait(sp, proj_ready, t * AU + 2 * (j - NSLOT) + 2)
                    sp.sem_inc(sp_passed, 1)
                    at = 0
                    for a, n in cols:
                        sp.dma_start(win[:, j % NSLOT, :, at:at + n], w_d[:, :, a:a + n]).then_inc(win_in[j % NSLOT], 16)
                        at += n

            def load_residual(t):
                for i in range(NT):
                    wait_apart(sp, res_free, t * NT + i + 1, sp_passed)
                    sp.wait_ge(xn_stored[i % 2], t * 32 + 16 * (i // 2))
                    sp.sem_inc(sp_passed, 1)
                    sp.dma_start(xres[:, i % 2], x_d[bass.ds(t * T + i * P, P), :]).then_inc(res_in[i % 2], 16)

            load(0)
            with sp.Fori(1, NB) as t:
                load(t)
                load_residual(t - 1)
            load_residual(NB - 1)

        @block.gpsimd
        def _(pool):
            def store(t):
                for i in range(NT):
                    rows = bass.ds(t * T + i * P, P)
                    wait_apart(pool, x1_ready, t * NT + i + 1, pool_passed)
                    pool.dma_start(x1_d[rows, :], yt[:, i % 2]).then_inc(x1_stored[i % 2], 16)
                    wait_apart(pool, xn_ready, t * NT + i + 1, pool_passed)
                    pool.dma_start(xn_d[rows, :], xres[:, i % 2]).then_inc(xn_stored[i % 2], 16)

            with pool.Fori(MINBLK, NBLK) as b:
                pool.dma_start(ap["y"][bass.ds(b * P, P), :], c.scoreT[:].rearrange("p a n -> p (a n)")).then_inc(y_cleared, 16)
            with pool.Fori(0, NB) as t:
                store(t)
            for s in x1_stored + xn_stored:
                pool.wait_ge(s, NB * 32)

        @block.tensor
        def _(pe):
            def claim(stage, n, t):
                if n >= 4:
                    wait(pe, *reader(stage, n - 4, t))
                elif stage == "A":
                    wait(pe, *reader("T", n + 4, t))
                elif stage == "O":
                    wait(pe, *reader("A", n + AU - 4, t + 1))
                elif stage == "tail":
                    wait(pe, *reader("O", n + OU - 4, t - 1))
                elif not isinstance(t, int):
                    wait(pe, *reader("A", n + AU - 4, t - 1))
                    wait(pe, rin_ready, (t - 1) * 8)
                return bank[n % 4]

            def transposes_in(t):
                for i in range(NT):
                    pe.wait_ge(x_normed, t * NT + i + 1)
                    for half in range(2):
                        n = 2 * i + half
                        out = claim("T", n, t)
                        for j in range(4):
                            k = half * 4 + j
                            last = nc.tensor.transpose(out[:, j * P:(j + 1) * P], xt[:, i % 2, k * P:(k + 1) * P], c.ident[:])
                        last.then_inc(xT_ready, 1)

            def project(t):
                for j in range(NPIECE):
                    w = win[:, j % NSLOT]
                    pe.wait_ge(win_in[j % NSLOT], win_bytes(t, j))
                    if j == 0:
                        pe.wait_ge(hT_ready, t * TU + TU)
                    for half in range(2):
                        n = 2 * j + half
                        out = claim("A", n, t)
                        if j < 8:
                            for k in range(KD):
                                last = nc.tensor.matmul(out[:], w[:, k, half * P:(half + 1) * P], hT[:, k, :],
                                                        start=(k == 0), stop=(k == KD - 1))
                        else:
                            for s in range(2):
                                i = 2 * half + s
                                for k in range(KD):
                                    last = nc.tensor.matmul(out[:, s * 256:(s + 1) * 256], hT[:, k, i * P:(i + 1) * P],
                                                            w[:, k, :], start=(k == 0), stop=(k == KD - 1))
                        last.then_inc(proj_ready, 1)

            def output(t, stage):
                def y_tile(i, n):
                    for half in range(2):
                        out = claim(stage if n < 4 else "O", n + half, t)
                        for k in range(KD):
                            last = nc.tensor.matmul(out[:], yT[:, k, i * P:(i + 1) * P], wo[:, k, half * 512:(half + 1) * 512],
                                                    start=(k == 0), stop=(k == KD - 1))
                        last.then_inc(y_ready, 1)

                def router_tile(i, n):
                    pe.wait_ge(xn_ready, t * NT + i + 1)
                    for half in range(2):
                        out = claim(stage if n < 4 else "O", n + half, t)
                        for j in range(4):
                            k = half * 4 + j
                            last = nc.tensor.transpose(out[:, j * P:(j + 1) * P], xres[:, i % 2, k * P:(k + 1) * P], c.ident[:])
                        last.then_inc(rT_ready, 1)
                    pe.wait_ge(rT_ready, t * 8 + 2 * i + 2)
                    pe.sem_inc(res_free, 1)
                    pe.wait_ge(rin_ready, t * 8 + 2 * i + 2)
                    wait(pe, logit_saved, t * NT + i)
                    for k in range(KD):
                        nc.tensor.matmul(pS[:, 0:NR], scr[:, k * P:(k + 1) * P], c.wroute[:, k, :], start=(k == 0), stop=False)
                    nc.tensor.matmul(pS[:, 0:NR], c.ones[0:1, :], c.brow[:], start=False, stop=True).then_inc(logit_ready, 1)

                pe.wait_ge(wo_in, 16)
                pe.wait_ge(yT_rec, (t + 1) * NT)
                pe.wait_ge(yT_conv, (t + 1) * NCH)
                for n, (kind, i) in enumerate(ORDER):
                    (y_tile if kind == "y" else router_tile)(i, 2 * n)

            def layer_norm_sums(t):
                pe.wait_ge(conv_step, (t + 1) * CONV_STEPS)
                wait(pe, logit_saved, t * NT)
                for k in range(NCH):
                    last = nc.tensor.matmul(pS[:], c.ones[:], cv[:, k, :], start=(k == 0), stop=(k == NCH - 1))
                last.then_inc(mean_ready, 1)
                wait(pe, o_saved, t * NT)
                for k in range(NCH):
                    pe.wait_ge(squared, t * NCH + k + 1)
                    last = nc.tensor.matmul(pO[:], c.ones[:], hT[:, k, :], start=(k == 0), stop=(k == NCH - 1))
                last.then_inc(var_ready, 1)

            def recurrence(t):
                pe.wait_ge(exp_used, (t + 1) * 3 * NH)
                pe.wait_ge(v_ready, (t + 1) * 4)
                pe.wait_ge(centred, (t + 1) * NCH)
                wait(pe, yT_rec, t * NT)
                for i in range(NT):
                    tok = slice(i * P, (i + 1) * P)
                    wait(pe, masked, t * NT + i)
                    for h in range(NH):
                        last = nc.tensor.matmul(pS[:, h * P:(h + 1) * P], ki[:, h, tok], qd[:, h, tok], start=True, stop=True)
                    last.then_inc(score_ready, 1)
                    wait(pe, keT_ready, t * NT + i)
                    for h in range(NH):
                        last = nc.tensor.transpose(pT[:, h * P:(h + 1) * P], ke[:, h, tok], c.ident[:])
                    last.then_inc(keT_psum, 1)
                    pe.wait_ge(keT_ready, t * NT + i + 1)
                    for s in range(2):
                        rows = slice(s * CH, (s + 1) * CH)
                        n = 2 * i + s
                        wait(pe, state_ready, t * 2 * NT + n)
                        for h in range(NH):
                            last = nc.tensor.matmul(pD[:, h * P:(h + 1) * P], scr[rows, (i % 2) * 512 + h * P:(i % 2) * 512 + (h + 1) * P],
                                                    v[rows, i, h * P:(h + 1) * P], start=True, stop=True)
                        last.then_inc(dstate_ready, 1)
                    pe.wait_ge(masked, t * NT + i + 1)
                    pe.wait_ge(state_ready, t * 2 * NT + 2 * i + 1)
                    if i == 0:
                        pe.wait_ge(ln_rstd, t + 1)
                    wait(pe, o_saved, t * NT + i)
                    for h in range(NH):
                        hc = slice(h * P, (h + 1) * P)
                        nc.tensor.matmul(pO[:, hc], c.scoreT[:, i % 2, hc], v[:, i, hc], start=True, stop=False, skip_group_check=True)
                        for s in range(2):
                            at = i * P + s * CH
                            last = nc.tensor.matmul(pO[s * CH:(s + 1) * CH, hc], qd[:, h, at:at + CH],
                                                    c.state[:, (2 * i + s) % 4, hc], start=False, stop=(s == 1), skip_group_check=True)
                    last.then_inc(o_ready, 1)
                pe.wait_ge(o_gated, t + 1)
                for i in range(NT):
                    wait(pe, yT_rec, t * NT + i)
                    for h in range(NH):
                        last = nc.tensor.transpose(pT[:, h * P:(h + 1) * P], ob[:, i, h * P:(h + 1) * P], c.ident[:])
                    last.then_inc(oT_psum, 1)

            pe.sem_inc(res_free, 2)
            transposes_in(0)
            project(0)
            layer_norm_sums(0)
            recurrence(0)
            with pe.Fori(1, NB) as t:
                transposes_in(t)
                project(t)
                output(t - 1, "O")
                layer_norm_sums(t)
                recurrence(t)
            output(NB - 1, "tail")

        @block.scalar
        def _(act):
            A = nc.scalar.activation

            def rstd(ch, out, in_, width):
                ch.link(A(out, in_, ACT.Ln, bias=c.epsc[:], scale=1.0 / width))
                return A(out, out, ACT.Exp, scale=-0.5)

            def norm_in(t):
                ch = Chain(act, a_norm, t * (2 * NT))
                act.preload_act_table_set("natural_log_exp_and_others")

                def evacuate(i):
                    for half in range(2):
                        n = 2 * i + half
                        act.wait_ge(xT_ready, t * TU + n + 1)
                        if n == 0:
                            wait(act, proj_ready, t * AU)
                            wait(act, yT_conv, t * NCH)
                        for j in range(4):
                            k = half * 4 + j
                            last = A(hT[:, k, i * P:(i + 1) * P], bank[n % 4][:, j * P:(j + 1) * P], ACT.Identity,
                                     scale=c.scale1[:, k:k + 1], bias=c.shift1[:, k:k + 1])
                        last.then_inc(hT_ready, 1)

                for i in range(NT):
                    act.wait_ge(x_in[i % 2], t * 32 + 16 * (i // 2 + 1))
                    if i == 0:
                        wait(act, xT_ready, t * TU)
                    ch.link(A(scr[:], xt[:, i % 2], ACT.Square, accum_out=sums[:, i:i + 1]))
                    ch.link(A(sums[:, i:i + 1], sums[:, i:i + 1], ACT.Ln, bias=c.epsc[:], scale=1.0 / D))
                    A(sums[:, i:i + 1], sums[:, i:i + 1], ACT.Exp, scale=-0.5).then_inc(x_rstd, 1)
                    if i >= 1:
                        evacuate(i - 1)
                evacuate(NT - 1)

            def gates(t):
                for j in range(NCH):
                    act.wait_ge(proj_ready, t * AU + 2 * j + 2)
                    if j == 0:
                        wait(act, yT_conv, t * NCH)
                    A(cv[:, j], bank[(2 * j + 1) % 4][:], ACT.Sigmoid).then_inc(gate_sig, 1)
                for h in range(NH):
                    n = 8 + 2 * h
                    act.wait_ge(proj_ready, t * AU + n + 1)
                    if h == 0:
                        wait(act, o_ready, t * NT)
                        wait(act, keT_psum, t * NT)
                    A(ke[:, h], bank[n % 4][:], ACT.Sigmoid).then_inc(q_parts, 1)
                    A(qd[:, h], bank[n % 4][:], ACT.Copy).then_inc(q_parts, 1)
                    act.wait_ge(proj_ready, t * AU + n + 2)
                    A(ki[:, h], bank[(n + 1) % 4][:], ACT.Sigmoid).then_inc(q_parts, 1)
                for j in range(2):
                    for half in range(2):
                        n = 16 + 2 * j + half
                        act.wait_ge(proj_ready, t * AU + n + 1)
                        if n == 16:
                            wait(act, oT_psum, t * NT)
                        src = bank[n % 4][:].rearrange("p (a b) -> p a b", a=2)
                        cols = slice(j * 256, (j + 1) * 256)
                        A(ob[:, 2 * half:2 * half + 2, cols], src, ACT.Sigmoid).then_inc(g_parts, 1)
                        A(gs[:, 2 * half:2 * half + 2, cols], src, ACT.Copy).then_inc(g_parts, 1)

            def values(t, n0, n1):
                for n in range(n0, n1):
                    j, half = (n - 20) // 2, n % 2
                    act.wait_ge(proj_ready, t * AU + n + 1)
                    src = bank[n % 4][:].rearrange("p (a b) -> p a b", a=2)
                    A(v[:, 2 * half:2 * half + 2, j * 256:(j + 1) * 256], src, ACT.Copy).then_inc(v_ready, 1)

            def heads(t):
                bb, ee = scr[:, 0:T], scr[:, T:2 * T]
                act.preload_act_table_set("natural_log_exp_and_others")
                for h in range(NH):
                    n = t * NH + h
                    act.wait_ge(forget_ready, n + 1)
                    if h > 0:
                        act.wait_ge(diff_ready, n)
                    A(bb, ki[:, h], ACT.Ln).then_inc(logf_ready, 1)
                    act.wait_ge(b_ready, n + 1)
                    A(ee, bb, ACT.Exp).then_inc(exp_ready, 1)
                    A(decay[:, h], bb[:, CH - 1::CH], ACT.Exp).then_inc(exp_ready, 1)
                    act.wait_ge(exp_used, 3 * n + 1)
                    A(ee, bb, ACT.Exp, scale=-1.0).then_inc(exp_ready, 1)
                    act.wait_ge(diff_ready, n + 1)
                    A(tmp[:], tmp[:], ACT.Exp).then_inc(exp_ready, 1)
                    values(t, 20 + h, 21 + h)
                    act.wait_ge(exp_used, 3 * n + 3)

            def output(t):
                ch = Chain(act, a_out, t * (7 * NT))

                def y_sums(i):
                    n = BANKS["y", i]
                    s = sums[:, 8 + 2 * (i % 2):10 + 2 * (i % 2)]
                    r = sums[:, 12 + i % 2:13 + i % 2]
                    if i >= 2:
                        act.wait_ge(x1_ready, t * NT + i - 1)
                    for half in range(2):
                        act.wait_ge(y_ready, t * 8 + 2 * i + half + 1)
                        ch.link(A(tmp[:], bank[(n + half) % 4][:], ACT.Square, accum_out=s[:, half:half + 1]))
                    ch.link(A(r, s[:, 0:1], ACT.Identity, bias=s[:, 1:2]))
                    ch.link(A(r, r, ACT.Ln, bias=c.epsc[:], scale=1.0 / D))
                    A(r, r, ACT.Exp, scale=-0.5).then_inc(y_rstd, 1)

                def x1_sums(i):
                    r = sums[:, 14 + i % 2:15 + i % 2]
                    act.wait_ge(x1_ready, t * NT + i + 1)
                    for half in range(2):
                        ch.link(A(tmp[:], yt[:, i % 2, half * 512:(half + 1) * 512], ACT.Square,
                                  accum_out=sums[:, 16 + half:17 + half]))
                    ch.link(A(r, sums[:, 16:17], ACT.Identity, bias=sums[:, 17:18]))
                    A(r, r, ACT.Ln, bias=c.epsc[:], scale=1.0 / D).then_inc(x1_rstd, 1)
                    act.wait_ge(x1_rstd, (t * NT + i) * 2 + 1)
                    A(r, r, ACT.Exp, scale=-0.5).then_inc(x1_rstd, 1)

                def router_in(i):
                    n = BANKS["r", i]
                    wait(act, logit_ready, t * NT + i)
                    for half in range(2):
                        act.wait_ge(rT_ready, t * 8 + 2 * i + half + 1)
                        A(scr[:, half * 512:(half + 1) * 512], bank[(n + half) % 4][:], ACT.Copy).then_inc(rin_ready, 1)

                y_sums(0)
                for n in range(1, len(ORDER)):
                    kind, i = ORDER[n]
                    if kind == "y":
                        y_sums(i)
                    else:
                        x1_sums(i)
                        router_in(i)
                assert ch.n == 7 * NT, ch.n

            def layer_norm(t):
                act.wait_ge(centred, (t + 1) * NCH)
                act.wait_ge(proj_ready, (t + 1) * AU)
                for k in range(NCH):
                    A(hT[:, k, :], cv[:, k], ACT.Square).then_inc(squared, 1)
                act.wait_ge(var_ready, t + 1)
                A(hT[:, 4, :], pO[:], ACT.Ln, bias=c.epsc[:], scale=1.0 / DC).then_inc(a_ln, 1)
                act.wait_ge(a_ln, t + 1)
                A(hT[:, 4, :], hT[:, 4, :], ACT.Exp, scale=-0.5).then_inc(ln_rstd, 1)

            def layer_norm_gate(t):
                for k in range(NCH):
                    act.wait_ge(ln_normed, t * NCH + k + 1)
                    A(hT[:, k, :], cv[:, k], ACT.Sigmoid, scale=col("conv_ln_gain", k), bias=col("conv_ln_bias", k)).then_inc(ln_sig, 1)

            def recurrence(t):
                ch = Chain(act, a_rec, t)
                wait(act, logit_ready, t * NT)
                for i in range(NT):
                    act.wait_ge(keT_psum, t * NT + i + 1)
                    if i >= 2:
                        act.wait_ge(dstate_ready, t * 2 * NT + 2 * (i - 1))
                    A(scr[:, (i % 2) * 512:(i % 2 + 1) * 512], pT[:], ACT.Copy).then_inc(keT_ready, 1)
                    if i >= 1:
                        o_square(t, i - 1)
                o_square(t, NT - 1)
                act.wait_ge(o_ms, (t + 1) * NT)
                ch.link(A(sums[:, 32:48], sums[:, 32:48], ACT.Ln, bias=c.epsc[:], scale=1.0 / P))
                A(sums[:, 32:48], sums[:, 32:48], ACT.Exp, scale=-0.5).then_inc(o_rstd, 1)
                for i in range(NT):
                    act.wait_ge(oT_psum, t * NT + i + 1)
                    A(yT[:, NH:, i * P:(i + 1) * P], pT[:].rearrange("p (h n) -> p h n", h=NH), ACT.Copy,
                      scale=col("rec_norm_gain", 0)).then_inc(yT_rec, 1)

            def o_square(t, i):
                act.wait_ge(o_saved, t * NT + i + 1)
                wait(act, o_ms, t * NT + i)
                A(tmp[:], ob[:, i], ACT.Square).then_inc(o_squared, 1)

            def block_of(t):
                norm_in(t)
                gates(t)
                heads(t)

            block_of(0)
            layer_norm(0)
            recurrence(0)
            layer_norm_gate(0)
            with act.Fori(1, NB) as t:
                block_of(t)
                output(t - 1)
                layer_norm(t)
                recurrence(t)
                layer_norm_gate(t)
            output(NB - 1)

        @block.vector
        def _(dve):
            V = nc.vector

            def norm_in(t):
                for i in range(NT):
                    dve.wait_ge(x_rstd, t * NT + i + 1)
                    V.tensor_scalar(xt[:, i % 2], xt[:, i % 2], sums[:, i:i + 1], None, ALU.mult).then_inc(x_normed, 1)

            def conv(t):
                ch = Chain(dve, conv_step, t * CONV_STEPS)
                for k in range(NCH):
                    if isinstance(t, int):
                        ch.step(V.tensor_copy(u[:, k, 0:HALO], c.halo0[:]))
                    else:
                        ch.step(V.tensor_copy(u[:, k, 0:HALO], u[:, k, T:T + HALO]))
                ch.sync()
                for j in range(NCH):
                    dve.wait_ge(gate_sig, t * NCH + j + 1)
                    V.tensor_tensor(u[:, j, HALO:], bank[(2 * j) % 4][:], cv[:, j], ALU.mult).then_inc(u_ready, 1)
                dve.wait_ge(u_ready, (t + 1) * NCH)
                for w in range(CW):
                    for j in range(NCH):
                        tap = c.taps[:, j * CW + w:j * CW + w + 1]
                        if w == 0:
                            ins = V.tensor_scalar(cv[:, j], u[:, j, 0:T], tap, col("dw_bias", j), ALU.mult, ALU.add)
                        else:
                            dve.wait_ge(conv_step, ch.base + ch.n - NCH + 1)
                            ins = V.scalar_tensor_tensor(out=cv[:, j], in0=u[:, j, w:w + T], scalar=tap, in1=cv[:, j],
                                                         op0=ALU.mult, op1=ALU.add)
                        ch.step(ins)
                ch.sync()
                assert ch.n == CONV_STEPS

            def heads(t):
                ch = Chain(dve, v_head, t * 2 * NH)
                bb, ee = scr[:, 0:T], scr[:, T:2 * T]
                for h in range(NH):
                    dve.wait_ge(q_parts, (t * NH + h) * 3 + 3)
                    ch.step(V.tensor_tensor(qd[:, h], qd[:, h], ke[:, h], ALU.mult))
                    V.tensor_scalar(ki[:, h], ki[:, h], c.oneless[:, h:h + 1], c.lb[:, h:h + 1], ALU.mult, ALU.add).then_inc(forget_ready, 1)
                for h in range(NH):
                    n = t * NH + h
                    dve.wait_ge(forget_ready, n + 1)
                    dve.wait_ge(v_head, ch.base + NH)
                    ch.step(V.tensor_scalar(ke[:, h], ki[:, h], -1.0, 1.0, ALU.mult, ALU.add))
                    dve.wait_ge(logf_ready, n + 1)
                    V.tensor_tensor_scan(bb, c.restart[:], bb, 0.0, ALU.mult, ALU.add).then_inc(b_ready, 1)
                    dve.wait_ge(b_ready, n + 1)
                    b3 = bb.rearrange("p (n k) -> p n k", k=CH)
                    V.tensor_tensor(tmp[:].rearrange("p (n k) -> p n k", k=CH),
                                    b3[:, :, CH - 1:CH].to_broadcast([P, T // CH, CH]), b3, ALU.subtract).then_inc(diff_ready, 1)
                    dve.wait_ge(exp_ready, 4 * n + 2)
                    V.tensor_tensor(qd[:, h], qd[:, h], ee, ALU.mult).then_inc(exp_used, 1)
                    dve.wait_ge(exp_ready, 4 * n + 3)
                    ch.sync()
                    V.tensor_tensor(ki[:, h], ke[:, h], ee, ALU.mult).then_inc(exp_used, 1)
                    dve.wait_ge(exp_ready, 4 * n + 4)
                    V.tensor_tensor(ke[:, h], ke[:, h], tmp[:], ALU.mult).then_inc(exp_used, 1)
                assert ch.n == 2 * NH, ch.n

            def gate_values(t):
                dve.wait_ge(g_parts, (t + 1) * 8)
                V.tensor_tensor(gs[:], gs[:], ob[:], ALU.mult).then_inc(g_done, 1)
                dve.wait_ge(g_done, t + 1)

            def output(t):
                def y_norm(i):
                    n = BANKS["y", i]
                    dve.wait_ge(y_rstd, t * NT + i + 1)
                    wait(dve, x1_stored[i % 2], t * 32 + 16 * (i // 2))
                    for half in range(2):
                        cols = slice(half * 512, (half + 1) * 512)
                        V.scalar_tensor_tensor(out=yt[:, i % 2, cols], in0=bank[(n + half) % 4][:],
                                               scalar=sums[:, 12 + i % 2:13 + i % 2], in1=c.grow[:, cols],
                                               op0=ALU.mult, op1=ALU.mult).then_inc(y_normed, 1)
                    dve.wait_ge(y_normed, t * 8 + 2 * i + 2)
                    dve.wait_ge(res_in[i % 2], t * 32 + 16 * (i // 2 + 1))
                    V.tensor_tensor(yt[:, i % 2], yt[:, i % 2], xres[:, i % 2], ALU.add).then_inc(x1_ready, 1)

                def x1_norm(i):
                    dve.wait_ge(x1_rstd, (t * NT + i + 1) * 2)
                    V.tensor_scalar(xres[:, i % 2], yt[:, i % 2], sums[:, 14 + i % 2:15 + i % 2], None, ALU.mult).then_inc(xn_ready, 1)

                def save_logits(i):
                    dve.wait_ge(logit_ready, t * NT + i + 1)
                    V.tensor_copy(c.logits[:, bass.ds(t * NT + i, 1), :].rearrange("p a n -> p (a n)"), pS[:, 0:NR]).then_inc(logit_saved, 1)

                y_norm(0)
                for n in range(1, len(ORDER)):
                    kind, i = ORDER[n]
                    if kind == "y":
                        y_norm(i)
                    else:
                        x1_norm(i)
                        save_logits(i)

            def layer_norm(t):
                dve.wait_ge(mean_ready, t + 1)
                for k in range(NCH):
                    V.scalar_tensor_tensor(out=cv[:, k], in0=pS[:], scalar=-1.0 / DC, in1=cv[:, k],
                                           op0=ALU.mult, op1=ALU.add).then_inc(centred, 1)
                dve.wait_ge(centred, (t + 1) * NCH)
                dve.wait_ge(ln_rstd, t + 1)
                for k in range(NCH):
                    V.tensor_tensor(cv[:, k], cv[:, k], hT[:, 4, :], ALU.mult).then_inc(ln_normed, 1)

            def layer_norm_out(t):
                ch = Chain(dve, v_ln, t * NCH)
                for k in range(NCH):
                    dve.wait_ge(ln_sig, t * NCH + k + 1)
                    ch.step(V.tensor_scalar(cv[:, k], cv[:, k], col("conv_ln_gain", k), col("conv_ln_bias", k), ALU.mult, ALU.add))
                ch.sync()
                for k in range(NCH):
                    V.tensor_tensor(yT[:, k, :], cv[:, k], hT[:, k, :], ALU.mult).then_inc(yT_conv, 1)

            def recurrence(t):
                for i in range(NT):
                    n = t * NT + i
                    wait_apart(dve, score_ready, n + 1, dve_passed)
                    V.copy_predicated(c.scoreT[:, i % 2].rearrange("p (h n) -> p h n", h=NH),
                                      c.causal[:].bitcast(I32).unsqueeze(1).to_broadcast([P, NH, P]),
                                      pS[:].rearrange("p (h n) -> p h n", h=NH)).then_inc(masked, 1)
                    for s in range(2):
                        m = 2 * i + s
                        dve.wait_ge(dstate_ready, t * 2 * NT + m + 1)
                        wait(dve, state_ready, t * 2 * NT + m)
                        for h in range(NH):
                            hc = slice(h * P, (h + 1) * P)
                            last = V.scalar_tensor_tensor(out=c.state[:, (m + 1) % 4, hc], in0=c.state[:, m % 4, hc],
                                                          scalar=decay[:, h, m:m + 1], in1=pD[:, hc], op0=ALU.mult, op1=ALU.add)
                        last.then_inc(state_ready, 1)
                    dve.wait_ge(o_ready, n + 1)
                    V.tensor_copy(ob[:, i], pO[:]).then_inc(o_saved, 1)
                    dve.wait_ge(o_squared, n + 1)
                    V.tensor_reduce(sums[:, 32 + 4 * i:36 + 4 * i], tmp[:].rearrange("p (h n) -> p h n", h=NH), axis=AX.X, op=ALU.add).then_inc(o_ms, 1)
                dve.wait_ge(o_rstd, t + 1)
                o3 = ob[:].rearrange("p i (h n) -> p (i h) n", h=NH)
                V.tensor_tensor(o3, o3, sums[:, 32:48].unsqueeze(2).to_broadcast([P, NT * NH, P]), ALU.mult).then_inc(v_rec, 1)
                dve.wait_ge(v_rec, t + 1)
                V.tensor_tensor(ob[:], ob[:], gs[:], ALU.mult).then_inc(o_gated, 1)

            def block_of(t, with_output):
                norm_in(t)
                conv(t)
                heads(t)
                gate_values(t)
                if with_output:
                    output(t - 1)
                layer_norm(t)
                recurrence(t)
                layer_norm_out(t)

            dve.wait_ge(y_cleared, (NBLK - MINBLK) * 16)
            block_of(0, False)
            with dve.Fori(1, NB) as t:
                block_of(t, True)
            output(NB - 1)


def routing_phase(nc, ap, c):
    with ExitStack() as ctx:
        sb = lambda n, s, d=F32: ctx.enter_context(nc.sbuf_tensor(n, s, d))
        sem = lambda n: ctx.enter_context(nc.semaphore(n))
        BIG = 1e30
        NA = 2 * NTILES
        lane, blk = sb("lane", [P, P]), sb("blk", [P, TAB])
        token, blkrow = sb("token", [P, NTILES]), sb("blkrow", [P, 16])
        tri, one16 = sb("tri16", [P, P], BF16), sb("one16", [P, P], BF16)
        trif = sb("trif", [P, P])
        t16 = [sb(f"t16_{i}", [P, NTILES]) for i in range(12)]
        g4 = [sb(f"g4_{i}", [P, NTILES, NG]) for i in range(3)]
        e8 = [sb(f"e8_{i}", [P, NTILES, NEG]) for i in range(6)]
        big = [sb(f"big{i}", [P, NTILES, NE]) for i in range(4)]
        hot = sb("hot", [P, NTILES, NE], BF16)
        cum = sb("cum", [P, NTILES + 1, NE], BF16)
        x32 = [sb(f"x32_{i}", [P, NE]) for i in range(4)]
        cmp_ = sb("cmp", [P, TAB, NE])
        destf, rowi, blki = sb("destf", [P, NA]), sb("rowi", [P, NA], I32), sb("blki", [P, NA], I32)
        rowf, blkf = sb("rowf", [P, NA]), sb("blkf", [P, NA])
        RING = 4
        at_row, at_blk = sb("at_row", [P, RING, P]), sb("at_blk", [P, RING, TAB])
        etab = sb("etab", [P, TAB])
        pr = ctx.enter_context(nc.psum_tensor("prank", [P, 512], F32))
        pc = ctx.enter_context(nc.psum_tensor("pcount", [P, 512], F32))
        pi = ctx.enter_context(nc.psum_tensor("pindex", [P, 512], F32))
        iota_done, tri_done, dve_step = sem("iota_done"), sem("tri_done"), sem("route_step")
        group_in, group_exp, expert_in, expert_exp = sem("group_in"), sem("group_exp"), sem("expert_in"), sem("expert_exp")
        hot_ready, rank_ready, onehot_ready, onehot_used = sem("hot_ready"), sem("rank_ready"), sem("onehot_ready"), sem("onehot_used")
        block = ctx.enter_context(nc.Block())

        @block.gpsimd
        def _(pool):
            io = lambda out, n, **k: nc.gpsimd.iota(out, [[1, n]], base=0, allow_small_or_imprecise_dtypes=True, **k)
            io(lane[:], P, channel_multiplier=0)
            io(blk[:], TAB, channel_multiplier=0)
            nc.gpsimd.iota(blkrow[:], [[P, 16]], base=0, channel_multiplier=0, allow_small_or_imprecise_dtypes=True)
            nc.gpsimd.iota(token[:], [[P, NTILES]], base=0, channel_multiplier=1, allow_small_or_imprecise_dtypes=True)
            nc.gpsimd.memset(trif[:], 1.0).then_inc(tri_done, 1)
            pool.wait_ge(tri_done, 1)
            nc.gpsimd.affine_select(out=trif[:], in_=trif[:], compare_op=ALU.is_gt, fill=0.0,
                                    base=0, pattern=[[1, P]], channel_multiplier=-1).then_inc(iota_done, 1)

        @block.scalar
        def _(act):
            act.wait_ge(group_in, 1)
            nc.scalar.activation(g4[1][:], g4[0][:], ACT.Exp).then_inc(group_exp, 1)
            act.wait_ge(expert_in, 1)
            nc.scalar.activation(e8[2][:], e8[1][:], ACT.Exp)
            nc.scalar.activation(t16[5][:], t16[4][:], ACT.Exp).then_inc(expert_exp, 1)

        @block.tensor
        def _(pe):
            pe.wait_ge(hot_ready, 1)
            flat = lambda a: a.rearrange("p t e -> p (t e)")
            nc.tensor.matmul(pr[:], tri[:], flat(hot[:]), start=True, stop=False)
            nc.tensor.matmul(pr[:], one16[:], flat(cum[:, 0:NTILES]), start=False, stop=True)
            nc.tensor.matmul(pc[:, 0:NE], one16[:], cum[:, NTILES], start=True, stop=True).then_inc(rank_ready, 1)
            for n in range(NA):
                pe.wait_ge(onehot_ready, n + 1)
                nc.tensor.matmul(pi[:, 0:TAB], at_row[:, n % RING], at_blk[:, n % RING],
                                 start=(n == 0), stop=(n == NA - 1)).then_inc(onehot_used, 1)

        @block.vector
        def _(dve):
            V = nc.vector
            L = Chain(dve, dve_step).link
            bc = lambda a, n: a.unsqueeze(2).to_broadcast([P, a.shape[1], n])
            dve.wait_ge(iota_done, 1)
            L(V.tensor_copy(tri[:], trif[:]))
            L(V.tensor_copy(one16[:], c.ones[:]))

            def first_max(vals, best, diff, cand, index, onehot, n):
                L(V.tensor_reduce(best[:], vals, axis=AX.X, op=ALU.max))
                ins = V.tensor_tensor(diff[:], vals, bc(best[:], n), ALU.subtract)
                L(ins)
                L(V.tensor_scalar(cand[:], diff[:], 0.0, -64.0, ALU.is_ge, ALU.mult))
                L(V.tensor_tensor(cand[:], cand[:], lane[:, 0:n].unsqueeze(1).to_broadcast([P, NTILES, n]), ALU.add))
                L(V.tensor_reduce(index[:], cand[:], axis=AX.X, op=ALU.min))
                L(V.tensor_tensor(onehot[:], cand[:], bc(index[:], n), ALU.is_equal))

            gl = c.logits[:, :, 0:NG]
            first_max(gl, t16[0], g4[0], g4[1], t16[1], g4[2], NG)
            dve.sem_inc(group_in, 1)
            dve.wait_ge(group_exp, 1)
            L(V.tensor_reduce(t16[2][:], g4[1][:], axis=AX.X, op=ALU.add))
            L(V.reciprocal(t16[2][:], t16[2][:]))
            el = c.logits[:, :, NG:NR].rearrange("p t (g e) -> p t g e", g=NG)
            b4 = big[0][:].rearrange("p t (g e) -> p t g e", g=NG)
            L(V.tensor_tensor(b4, el, g4[2][:].unsqueeze(3).to_broadcast([P, NTILES, NG, NEG]), ALU.mult))
            L(V.tensor_reduce(e8[0][:], big[0][:].rearrange("p t (g e) -> p t e g", g=NG), axis=AX.X, op=ALU.add))
            first_max(e8[0][:], t16[3], e8[1], e8[2], t16[1], e8[3], NEG)
            L(V.scalar_tensor_tensor(out=e8[0][:], in0=e8[3][:], scalar=-BIG, in1=e8[0][:], op0=ALU.mult, op1=ALU.add))
            first_max(e8[0][:], t16[6], e8[5], e8[2], t16[1], e8[4], NEG)
            L(V.tensor_tensor(t16[4][:], t16[6][:], t16[3][:], ALU.subtract))
            dve.sem_inc(expert_in, 1)
            dve.wait_ge(expert_exp, 1)
            L(V.tensor_reduce(t16[7][:], e8[2][:], axis=AX.X, op=ALU.add))
            L(V.reciprocal(t16[7][:], t16[7][:]))
            L(V.tensor_tensor(t16[8][:], t16[5][:], t16[7][:], ALU.mult))
            L(V.tensor_tensor(t16[9][:], t16[8][:], t16[7][:], ALU.add))
            L(V.reciprocal(t16[9][:], t16[9][:]))
            L(V.tensor_tensor(t16[9][:], t16[9][:], t16[2][:], ALU.mult))
            L(V.tensor_tensor(c.weight[:, 0], t16[7][:], t16[9][:], ALU.mult))
            L(V.tensor_tensor(c.weight[:, 1], t16[8][:], t16[9][:], ALU.mult))
            for k in range(2):
                L(V.tensor_tensor(big[k][:].rearrange("p t (g e) -> p t g e", g=NG),
                                  g4[2][:].unsqueeze(3).to_broadcast([P, NTILES, NG, NEG]),
                                  e8[3 + k][:].unsqueeze(2).to_broadcast([P, NTILES, NG, NEG]), ALU.mult))
            L(V.tensor_tensor(hot[:], big[0][:], big[1][:], ALU.add))
            L(V.memset(cum[:, 0], 0.0))
            for i in range(NTILES):
                L(V.tensor_tensor(cum[:, i + 1], cum[:, i], hot[:, i], ALU.add))
            dve.sem_inc(hot_ready, 1)
            dve.wait_ge(rank_ready, 1)
            L(V.tensor_copy(x32[0][:], pc[:, 0:NE]))
            c3 = cmp_[:].rearrange("p a b -> p (a b)")[:, 0:NE * 16].rearrange("p (e m) -> p e m", e=NE)
            L(V.tensor_tensor(c3, bc(x32[0][:], 16), blkrow[:].unsqueeze(1).to_broadcast([P, NE, 16]), ALU.is_gt))
            L(V.tensor_reduce(x32[1][:], c3, axis=AX.X, op=ALU.add))
            L(V.tensor_tensor_scan(x32[2][:], c.ones[:, 0:NE], x32[1][:], 0.0, ALU.mult, ALU.add))
            L(V.tensor_copy(c.block_end[:], x32[2][:]))
            L(V.tensor_tensor(x32[3][:], x32[2][:], x32[1][:], ALU.subtract))
            L(V.tensor_scalar(x32[3][:], x32[3][:], float(P), None, ALU.mult))
            L(V.tensor_tensor(big[2][:], pr[:].rearrange("p (t e) -> p t e", e=NE),
                              x32[3][:].unsqueeze(1).to_broadcast([P, NTILES, NE]), ALU.add))
            for k in range(2):
                L(V.tensor_tensor(big[3][:], big[2][:], big[k][:], ALU.mult))
                L(V.tensor_reduce(destf[:, k * NTILES:(k + 1) * NTILES], big[3][:], axis=AX.X, op=ALU.add))
            L(V.tensor_copy(c.dest[:].rearrange("p k t -> p (k t)"), destf[:]))
            di = c.dest[:].rearrange("p k t -> p (k t)")
            L(V.tensor_scalar(blki[:], di, 7, None, ALU.arith_shift_right))
            L(V.tensor_scalar(rowi[:], di, P - 1, None, ALU.bitwise_and))
            L(V.tensor_copy(blkf[:], blki[:]))
            L(V.tensor_copy(rowf[:], rowi[:]))
            for n in range(NA):
                if n >= RING:
                    dve.wait_ge(onehot_used, n - RING + 1)
                V.tensor_scalar(at_row[:, n % RING], lane[:], rowf[:, n:n + 1], None, ALU.is_equal)
                i = n % NTILES
                V.tensor_scalar(at_blk[:, n % RING], blk[:], blkf[:, n:n + 1], token[:, i:i + 1],
                                ALU.is_equal, ALU.mult).then_inc(onehot_ready, 1)
            L(V.tensor_tensor(cmp_[:], x32[2][:].unsqueeze(1).to_broadcast([P, TAB, NE]), bc(blk[:], NE), ALU.is_le))
            L(V.tensor_reduce(etab[:], cmp_[:], axis=AX.X, op=ALU.add))
            L(V.tensor_scalar(etab[:], etab[:], float(NE - 1), 1.0, ALU.min, ALU.add))
            L(V.tensor_copy(c.expert_no[:], etab[:]))
            L(V.tensor_scalar(etab[:], etab[:], -1.0, None, ALU.add))
            L(V.tensor_copy(c.expert_slot[:], etab[:]))
            L(V.tensor_scalar(c.expert_slot[:], c.expert_slot[:], WSLOTS - 1, None, ALU.bitwise_and))
            L(V.tensor_scalar(x32[0][:, 0:1], x32[2][:, NE - 1:NE], 1.0, None, ALU.add))
            L(V.tensor_copy(c.pairs[:], x32[0][:, 0:1]))
            L(V.tensor_scalar(c.pairs[:], c.pairs[:], 1, None, ALU.arith_shift_right))
            dve.wait_ge(onehot_used, NA)
            L(V.tensor_copy(c.block_token[:], pi[:, 0:TAB]))


def expert_phase(nc, ap, c):
    with ExitStack() as ctx:
        sb = lambda n, s, d=F32: ctx.enter_context(nc.sbuf_tensor(n, s, d))
        sem = lambda n: ctx.enter_context(nc.semaphore(n))
        psum = lambda n: ctx.enter_context(nc.psum_tensor(n, [P, 512], F32))
        wgu = sb("wgu", [P, WSLOTS, KD, 2 * FE])
        wd = sb("wd", [P, WSLOTS, FE // P, D])
        xg = sb("xg", [P, 2, D])
        xT = sb("xTe", [P, KD, P])
        sg, hh = sb("sg", [P, FE]), sb("hh", [P, FE])
        hT = sb("hTe", [P, FE // P, P])
        yb = sb("yb", [P, 2, D])
        rows = sb("rows", [P, 2], I32)
        pt = [psum("pt0"), psum("pt1")]
        pgate, pup, ph = psum("pgate"), psum("pup"), psum("ph")
        py = [psum("py0"), psum("py1")]
        w_in = [sem(f"w_in{i}") for i in range(WSLOTS)]
        experts_loaded, blocks_done = sem("experts_loaded"), sem("blocks_done")
        row_copied, xg_in = sem("row_copied"), [sem("xg_in0"), sem("xg_in1")]
        x_turned, xT_act, xT_dve = sem("x_turned"), sem("xT_act"), sem("xT_dve")
        gate_ready, up_ready, silu_ready, hh_ready = sem("gate_ready"), sem("up_ready"), sem("silu_ready"), sem("hh_ready")
        h_turned, hT_ready, y_ready, y_act, y_dve = sem("h_turned"), sem("hT_e"), sem("y_e"), sem("y_act"), sem("y_dve")
        y_stored = [sem("y_stored0"), sem("y_stored1")]
        pool_passed, sp_passed = sem("pool_passed_e"), sem("sp_passed_e")
        block = ctx.enter_context(nc.Block())

        def load_pairs(eng):
            return eng.value_load(c.pairs[0:1, 0:1], min_val=1, max_val=NBLK // 2)

        @block.sync
        def _(sp):
            def load(e, s):
                wk = lambda name: ap[name][0][bass.ds(e, 1)]
                sp.dma_start(wgu[:, s, :, 0:FE], wk("w_gate").rearrange("a (k p) n -> p (a k) n", p=P)).then_inc(w_in[s], 16)
                sp.dma_start(wgu[:, s, :, FE:2 * FE], wk("w_up").rearrange("a (k p) n -> p (a k) n", p=P)).then_inc(w_in[s], 16)
                sp.dma_start(wd[:, s], wk("w_down").rearrange("a (k p) n -> p (a k) n", p=P)).then_inc(w_in[s], 16)

            def announce(s, turn):
                sp.wait_ge(w_in[s], 48 * turn)
                sp.sem_inc(experts_loaded, 1)

            for s in range(WSLOTS):
                load(s, s)
                if s > 0:
                    announce(s - 1, 1)
            with sp.Fori(1, NE // WSLOTS) as g:
                for s in range(WSLOTS):
                    last = sp.value_load(c.block_end[0:1, bass.ds((g - 1) * WSLOTS + s, 1)], min_val=0, max_val=NBLK)
                    wait_apart(sp, blocks_done, last, sp_passed)
                    load(g * WSLOTS + s, s)
                    if s == 0:
                        announce(WSLOTS - 1, g)
                    else:
                        announce(s - 1, g + 1)
            announce(WSLOTS - 1, NE // WSLOTS)

        @block.gpsimd
        def _(pool):
            def fetch(b, s, n):
                nc.gpsimd.tensor_copy(rows[:, s:s + 1], c.block_token[:, bass.ds(b, 1)]).then_inc(row_copied, 1)
                wait_apart(pool, row_copied, n, pool_passed)
                pool.indirect_dma_start(xg[:, s], None, ap["xn"], bass.IndirectOffsetOnAxis(rows[:, s:s + 1], 0)).then_inc(xg_in[s], 16)

            fetch(0, 0, 1)
            fetch(1, 1, 2)
            n_pairs = load_pairs(pool)
            with pool.Fori(0, n_pairs) as q:
                for s in range(2):
                    b = 2 * q + s
                    wait_apart(pool, x_turned, 2 * b + 2, pool_passed)
                    fetch(b + 2, s, b + 3)
                    pool.wait_ge(y_act, b + 1)
                    wait_apart(pool, y_dve, b + 1, pool_passed)
                    pool.dma_start(ap["y"][bass.ds(b * P, P), :], yb[:, s]).then_inc(y_stored[s], 16)
            for s in range(2):
                wait_apart(pool, y_stored[s], n_pairs * 16, pool_passed)
                wait_apart(pool, xg_in[s], n_pairs * 16 + 16, pool_passed)

        @block.tensor
        def _(pe):
            def turn(b, s, times):
                pe.wait_ge(xg_in[s], 16 * times)
                for half in range(2):
                    for j in range(4):
                        k = 4 * half + j
                        last = nc.tensor.transpose(pt[half][:, j * P:(j + 1) * P], xg[:, s, k * P:(k + 1) * P], c.ident[:])
                    last.then_inc(x_turned, 1)

            turn(0, 0, 1)
            with pe.Fori(0, load_pairs(pe)) as q:
                for s in range(2):
                    b = 2 * q + s
                    number = pe.value_load(c.expert_no[0:1, bass.ds(b, 1)], min_val=1, max_val=NE)
                    slot = pe.value_load(c.expert_slot[0:1, bass.ds(b, 1)], min_val=0, max_val=WSLOTS - 1)
                    pe.wait_ge(experts_loaded, number)
                    pe.wait_ge(xT_act, b + 1)
                    pe.wait_ge(xT_dve, b + 1)
                    for out, cols, done in ((pgate, 0, gate_ready), (pup, FE, up_ready)):
                        for k in range(KD):
                            last = nc.tensor.matmul(out[:, 0:FE], xT[:, k, :],
                                                    wgu[:, bass.ds(slot, 1), k, cols:cols + FE].rearrange("p a n -> p (a n)"),
                                                    start=(k == 0), stop=(k == KD - 1))
                        last.then_inc(done, 1)
                    turn(b + 1, 1 - s, q + 1 + s)
                    pe.wait_ge(hh_ready, b + 1)
                    for k in range(FE // P):
                        last = nc.tensor.transpose(ph[:, k * P:(k + 1) * P], hh[:, k * P:(k + 1) * P], c.ident[:])
                    last.then_inc(h_turned, 1)
                    pe.wait_ge(hT_ready, b + 1)
                    pe.wait_ge(y_act, b)
                    pe.wait_ge(y_dve, b)
                    for half in range(2):
                        for k in range(FE // P):
                            last = nc.tensor.matmul(py[half][:], hT[:, k, :],
                                                    wd[:, bass.ds(slot, 1), k, half * 512:(half + 1) * 512].rearrange("p a n -> p (a n)"),
                                                    start=(k == 0), stop=(k == FE // P - 1))
                        last.then_inc(y_ready, 1)
                    pe.wait_ge(y_ready, 2 * b + 2)
                    pe.sem_inc(blocks_done, 1)

        @block.scalar
        def _(act):
            A = nc.scalar.activation

            def evacuate(b):
                act.wait_ge(x_turned, 2 * b + 1)
                wait(act, up_ready, b)
                for k in range(4):
                    last = A(xT[:, k, :], pt[0][:, k * P:(k + 1) * P], ACT.Identity, scale=c.scale2[:, k:k + 1], bias=c.shift2[:, k:k + 1])
                last.then_inc(xT_act, 1)

            evacuate(0)
            with act.Fori(0, load_pairs(act)) as q:
                for s in range(2):
                    b = 2 * q + s
                    act.wait_ge(gate_ready, b + 1)
                    act.wait_ge(hh_ready, b)
                    A(sg[:], pgate[:, 0:FE], ACT.Silu).then_inc(silu_ready, 1)
                    evacuate(b + 1)
                    act.wait_ge(y_ready, 2 * b + 1)
                    act.wait_ge(y_stored[s], q * 16)
                    A(yb[:, s, 0:512], py[0][:], ACT.Copy).then_inc(y_act, 1)

        @block.vector
        def _(dve):
            V = nc.vector

            def evacuate(b):
                dve.wait_ge(x_turned, 2 * b + 2)
                wait(dve, up_ready, b)
                for j in range(4):
                    k = 4 + j
                    last = V.tensor_scalar(xT[:, k, :], pt[1][:, j * P:(j + 1) * P], c.scale2[:, k:k + 1], c.shift2[:, k:k + 1], ALU.mult, ALU.add)
                last.then_inc(xT_dve, 1)

            evacuate(0)
            with dve.Fori(0, load_pairs(dve)) as q:
                for s in range(2):
                    b = 2 * q + s
                    dve.wait_ge(silu_ready, b + 1)
                    dve.wait_ge(up_ready, b + 1)
                    dve.wait_ge(h_turned, b)
                    V.tensor_tensor(hh[:], pup[:, 0:FE], sg[:], ALU.mult).then_inc(hh_ready, 1)
                    dve.wait_ge(h_turned, b + 1)
                    dve.wait_ge(y_ready, 2 * b)
                    V.tensor_copy(hT[:].rearrange("p a b -> p (a b)"), ph[:, 0:FE]).then_inc(hT_ready, 1)
                    evacuate(b + 1)
                    dve.wait_ge(y_ready, 2 * b + 2)
                    dve.wait_ge(y_stored[s], q * 16)
                    V.tensor_copy(yb[:, s, 512:D], py[1][:]).then_inc(y_dve, 1)


def combine_phase(nc, ap, c, out):
    with ExitStack() as ctx:
        sb = lambda n, s, d=F32: ctx.enter_context(nc.sbuf_tensor(n, s, d))
        sem = lambda n: ctx.enter_context(nc.semaphore(n))
        diag, grow = sb("diag2", [P, KD, P]), sb("grow2", [P, D])
        ya, yb2, x1 = sb("ya", [P, 2, D]), sb("yb2", [P, 2, D]), sb("x1t", [P, 2, D])
        t1, junk = sb("t1", [P, 2, D]), sb("junk", [P, D])
        rows = sb("rows2", [P, 4], I32)
        ss = sb("ss", [P, 2])
        pg = [ctx.enter_context(nc.psum_tensor(f"pgrow{i}", [P, 512], F32)) for i in range(2)]
        diag_ready, row_done = sem("diag2_ready"), sem("row2_done")
        row_copied, ya_in, yb_in = sem("row2_copied"), [sem("ya_in0"), sem("ya_in1")], [sem("yb_in0"), sem("yb_in1")]
        x1_in, out_stored = [sem("x1_in0"), sem("x1_in1")], [sem("out_stored0"), sem("out_stored1")]
        scaled, y_sum, act_step, rstd_ready, gated, out_ready = (
            sem("scaled"), sem("y_sum"), sem("act_step2"), sem("rstd_ready"), sem("gated"), sem("out_ready"))
        pool_passed, sp_passed = sem("pool_passed2"), sem("sp_passed2")
        block = ctx.enter_context(nc.Block())
        HALF = NTILES // 2

        @block.sync
        def _(sp):
            with sp.Fori(0, HALF) as q:
                for s in range(2):
                    i = 2 * q + s
                    wait_apart(sp, out_stored[s], q * 16, sp_passed)
                    sp.dma_start(x1[:, s], ap["x1"][bass.ds(i * P, P), :]).then_inc(x1_in[s], 16)

        @block.gpsimd
        def _(pool):
            with pool.Fori(0, HALF) as q:
                for s in range(2):
                    i = 2 * q + s
                    wait_apart(pool, y_sum, i, pool_passed)
                    for k, (buf, done) in enumerate(((ya, ya_in), (yb2, yb_in))):
                        at = 2 * s + k
                        nc.gpsimd.tensor_copy(rows[:, at:at + 1], c.dest[:, k, bass.ds(i, 1)]).then_inc(row_copied, 1)
                        wait_apart(pool, row_copied, 2 * i + k + 1, pool_passed)
                        pool.indirect_dma_start(buf[:, s], None, ap["y"], bass.IndirectOffsetOnAxis(rows[:, at:at + 1], 0)).then_inc(done[s], 16)

        @block.tensor
        def _(pe):
            pe.wait_ge(diag_ready, 1)
            for r in range(2):
                nc.tensor.matmul(pg[r][:], c.ones[:], diag[:, 4 * r:4 * r + 4].rearrange("p a b -> p (a b)"),
                                 start=True, stop=True).then_inc(row_done, 1)

        @block.scalar
        def _(act):
            A = nc.scalar.activation
            act.preload_act_table_set("natural_log_exp_and_others")
            with act.Fori(0, HALF) as q:
                for s in range(2):
                    i = 2 * q + s
                    act.wait_ge(ya_in[s], 16 * q + 16)
                    A(ya[:, s], ya[:, s], ACT.Copy, scale=c.weight[:, 0, bass.ds(i, 1)]).then_inc(scaled, 1)
                    act.wait_ge(y_sum, i + 2)
                    A(junk[:], t1[:, s], ACT.Square, accum_out=ss[:, s:s + 1]).then_inc(act_step, 1)
                    act.wait_ge(act_step, 2 * i + 1)
                    A(ss[:, s:s + 1], ss[:, s:s + 1], ACT.Ln, bias=c.epsc[:], scale=1.0 / D).then_inc(act_step, 1)
                    act.wait_ge(act_step, 2 * i + 2)
                    A(ss[:, s:s + 1], ss[:, s:s + 1], ACT.Exp, scale=-0.5).then_inc(rstd_ready, 1)
                    act.wait_ge(out_ready, i + 1)
                    act.dma_start(out[bass.ds(i * P, P), :], x1[:, s]).then_inc(out_stored[s], 16)
            for s in range(2):
                act.wait_ge(out_stored[s], HALF * 16)

        @block.vector
        def _(dve):
            V = nc.vector
            for k in range(KD):
                last = V.tensor_scalar(diag[:, k], c.ident[:], c.gcol[:, KD + k:KD + k + 1], None, ALU.mult)
            last.then_inc(diag_ready, 1)
            for r in range(2):
                dve.wait_ge(row_done, r + 1)
                V.tensor_copy(grow[:, r * 512:(r + 1) * 512], pg[r][:])
            dve.sem_inc(y_sum, 1)
            with dve.Fori(0, HALF) as q:
                for s in range(2):
                    i = 2 * q + s
                    dve.wait_ge(scaled, i + 1)
                    dve.wait_ge(yb_in[s], 16 * q + 16)
                    V.scalar_tensor_tensor(out=t1[:, s], in0=yb2[:, s], scalar=c.weight[:, 1, bass.ds(i, 1)], in1=ya[:, s],
                                           op0=ALU.mult, op1=ALU.add).then_inc(y_sum, 1)
                    dve.wait_ge(rstd_ready, i + 1)
                    V.scalar_tensor_tensor(out=t1[:, s], in0=t1[:, s], scalar=ss[:, s:s + 1], in1=grow[:],
                                           op0=ALU.mult, op1=ALU.mult).then_inc(gated, 1)
                    dve.wait_ge(gated, i + 1)
                    dve.wait_ge(x1_in[s], 16 * q + 16)
                    V.tensor_tensor(x1[:, s], x1[:, s], t1[:, s], ALU.add).then_inc(out_ready, 1)


INPUTS = ["x", "c", "w_ada", "b_ada", "g_pre_mix", "g_post_mix", "w_in", "dw_kernel", "dw_bias",
          "conv_ln_gain", "conv_ln_bias", "lb_logits", "rec_norm_gain", "w_out", "g_pre_ffn", "g_post_ffn",
          "w_router_group", "b_router_group", "w_router_expert", "b_router_expert", "w_gate", "w_up", "w_down"]


class Kept:
    pass


def build(nc, ap, out):
    c = Kept()
    with ExitStack() as ctx:
        sb = lambda n, s, d=F32: ctx.enter_context(nc.sbuf_tensor(n, s, d))
        c.ident, c.ones, c.causal = (sb(n, [P, P]) for n in ("ident", "ones", "causal"))
        c.cols = sb("cols", [P, NVEC])
        c.epsc = sb("epsc", [P, 1])
        c.scale1, c.shift1, c.scale2, c.shift2 = (sb(n, [P, KD]) for n in ("scale1", "shift1", "scale2", "shift2"))
        c.gcol = sb("gcol", [P, 2 * KD])
        c.logits = sb("logits", [P, NTILES, NR])
        ap["x1"] = nc.dram_tensor("x1_dram", (SEQ, D), F32, kind=DEBUG_KIND).ap()
        ap["xn"] = nc.dram_tensor("xn_dram", (SEQ, D), F32, kind=DEBUG_KIND).ap()
        ap["y"] = nc.dram_tensor("y_dram", (NBLK * P, D), F32, kind="Internal").ap()
        with ExitStack() as mix:
            mb = lambda n, s, d=F32: mix.enter_context(nc.sbuf_tensor(n, s, d))
            c.restart = mb("restart", [P, T])
            c.halo0 = mb("halo0", [P, HALO])
            c.wroute = mb("wroute", [P, KD, NR])
            c.brow = mb("brow", [1, NR])
            c.taps = mb("taps", [P, NCH * CW])
            c.lb, c.oneless = mb("lb", [P, NCH]), mb("oneless", [P, NCH])
            c.grow = mb("grow", [P, D])
            c.state = mb("state", [P, 4, DC])
            c.scoreT = mb("scoreT", [P, 2, DC])
            constants_phase(nc, ap, c)
            mixer_phase(nc, ap, c)
        c.weight = sb("weight", [P, 2, NTILES])
        c.dest = sb("dest", [P, 2, NTILES], I32)
        c.block_token = sb("block_token", [P, TAB], I32)
        c.expert_no, c.expert_slot = sb("expert_no", [P, TAB], I32), sb("expert_slot", [P, TAB], I32)
        c.block_end, c.pairs = sb("block_end", [P, NE], I32), sb("pairs", [P, 1], I32)
        routing_phase(nc, ap, c)
        expert_phase(nc, ap, c)
        combine_phase(nc, ap, c, out[0])


DEBUG_KIND = "Internal"


def kernel(**inputs):
    import numpy as np
    import concourse.bacc as bacc
    from concourse.bass_utils import run_bass_kernel_spmd

    nc = bacc.Bacc("TRN2", target_bir_lowering=False, num_devices=1)
    arrays, ap = {}, {}
    for name in INPUTS:
        a = np.ascontiguousarray(inputs[name])
        arrays[f"{name}_in"] = a
        ap[name] = nc.dram_tensor(f"{name}_in", a.shape, mybir.dt.from_np(a.dtype), kind="ExternalInput").ap()
    out = nc.dram_tensor("out", (1, SEQ, D), F32, kind="ExternalOutput").ap()
    build(nc, ap, out)
    r = run_bass_kernel_spmd(nc, [arrays], core_ids=[0])
    return r.results[0]["out"]
```

```python
import concourse.bass as bass
from concourse import mybir
from contextlib import ExitStack

F32 = mybir.dt.float32
I32 = mybir.dt.int32
U32 = mybir.dt.uint32
BF16 = mybir.dt.bfloat16
ALU = mybir.AluOpType
ACT = mybir.ActivationFunctionType
AX = mybir.AxisListType

P = 128
D = 1024
KD = D // P
SEQ = 2048
DC = 512
NCH = DC // P
NH = 4
CW = 31
HALO = CW - 1
T = 512
NB = SEQ // T
NT = T // P
CH = 64
NTILES = SEQ // P
NG, NEG = 4, 8
NE = NG * NEG
FE = 256
NR = NG + NE
EPS = 1e-6
NBLK = 64
MINBLK = 2 * SEQ // P
WSLOTS = 4
TAB = NBLK + 2

VEC = {}
_at = 0
for _name, _n in (("c", 8), ("b_ada", 48), ("g_pre_mix", 8), ("g_post_mix", 8), ("g_pre_ffn", 8),
                  ("g_post_ffn", 8), ("dw_bias", 4), ("conv_ln_gain", 4), ("conv_ln_bias", 4),
                  ("lb_logits", 8), ("rec_norm_gain", 1)):
    VEC[_name] = (_at, _at + _n)
    _at += _n
NVEC = _at


def wait(eng, sem, value):
    if isinstance(value, int) and value <= 0:
        return
    eng.wait_ge(sem, value)


def wait_apart(eng, sem, value, passed):
    eng.wait_ge(sem, value)
    eng.sem_inc(passed, 1)


class Chain:

    def __init__(self, eng, sem, base=0):
        self.eng, self.sem, self.base, self.n = eng, sem, base, 0

    def step(self, ins):
        ins.then_inc(self.sem, 1)
        self.n += 1

    def sync(self):
        wait(self.eng, self.sem, self.base + self.n)

    def link(self, ins):
        self.step(ins)
        self.sync()


def mixer_phase(nc, ap, c):
    with ExitStack() as ctx:
        sb = lambda n, s, d=F32: ctx.enter_context(nc.sbuf_tensor(n, s, d))
        sem = lambda n: ctx.enter_context(nc.semaphore(n))
        col = lambda n, k: c.cols[:, VEC[n][0] + k:VEC[n][0] + k + 1]

        xt = sb("xt", [P, 2, D])
        hT = sb("hT", [P, KD, T])
        NSLOT = 3
        win = sb("win", [P, NSLOT, KD, 256])
        wo = sb("wo", [P, KD, D])
        u = sb("u", [P, NCH, HALO + T])
        cv = sb("cv", [P, NCH, T])
        yT = sb("yT", [P, KD, T])
        heads_buf = sb("heads_buf", [P, 4, NH * T])
        by_head = lambda m: heads_buf[:, m].rearrange("p (h n) -> p h n", h=NH)
        qd, ki, ke = by_head(0), by_head(1), by_head(2)
        v = heads_buf[:, 3].rearrange("p (i n) -> p i n", i=NT)
        gs = sb("gs", [P, NT, DC])
        ob = sb("ob", [P, NT, DC])
        scr = sb("scr", [P, D])
        yt = sb("yt", [P, 2, D])
        xres = sb("xres", [P, 2, D])
        tmp = sb("tmp", [P, 512])
        decay = sb("decay", [P, NH, T // CH])
        sums = sb("sums", [P, 48])
        cond, mod, lbt = sb("cond", [P, KD]), sb("mod", [P, 6 * KD]), sb("lbt", [P, 4, NCH])
        bank = [ctx.enter_context(nc.psum_tensor(f"bank{i}", [P, 512], F32)) for i in range(4)]
        pS = ctx.enter_context(nc.psum_tensor("pS", [P, 512], F32))
        pO = ctx.enter_context(nc.psum_tensor("pO", [P, 512], F32))
        pD = ctx.enter_context(nc.psum_tensor("pD", [P, 512], F32))
        pT = ctx.enter_context(nc.psum_tensor("pT", [P, 512], F32))

        vec_in, masks_ready, mask_step, turned, cols_ready, cond_ready = (
            sem(n) for n in ("vec_in", "masks_ready", "mask_step", "turned", "cols_ready", "cond_ready"))
        lb_in, lb_exp = sem("lb_in"), sem("lb_exp")
        ada_in = [sem(f"ada_in{i}") for i in range(4)] + [sem(f"ada_late_in{i}") for i in range(2)]
        route_in, act_passed = sem("route_in"), sem("act_passed")
        ada_used, ada_cols_done, scale1_ready, mod_ready = (
            sem(n) for n in ("ada_used", "ada_cols_done", "scale1_ready", "mod_ready"))
        mod_step, diag_ready, row_done, grow_ready = (
            sem(n) for n in ("mod_step", "diag_ready", "row_done", "grow_ready"))
        x_in = [sem("x_in0"), sem("x_in1")]
        win_in = [sem(f"win_in{i}") for i in range(NSLOT)]
        wo_in = sem("wo_in")
        res_in = [sem("res_in0"), sem("res_in1")]
        x_rstd, x_normed, xT_ready, hT_ready = sem("x_rstd"), sem("x_normed"), sem("xT_ready"), sem("hT_ready")
        proj_ready = sem("proj_ready")
        gate_sig, u_ready = sem("gate_sig"), sem("u_ready")
        q_parts, g_parts, v_ready = sem("q_parts"), sem("g_parts"), sem("v_ready")
        forget_ready, logf_ready, b_ready = sem("forget_ready"), sem("logf_ready"), sem("b_ready")
        exp_ready, exp_used = sem("exp_ready"), sem("exp_used")
        y_ready, y_rstd, x1_ready, x1_rstd, xn_ready = sem("y_ready"), sem("y_rstd"), sem("x1_ready"), sem("x1_rstd"), sem("xn_ready")
        y_cleared = sem("y_cleared")
        res_free, pool_passed, dve_passed, sp_passed = sem("res_free"), sem("pool_passed"), sem("dve_passed"), sem("sp_passed")
        rT_ready, rin_ready, logit_ready, logit_saved = sem("rT_ready"), sem("rin_ready"), sem("logit_ready"), sem("logit_saved")
        x1_stored, xn_stored = [sem("x1_stored0"), sem("x1_stored1")], [sem("xn_stored0"), sem("xn_stored1")]
        mean_ready, centred, squared, var_ready, ln_rstd, ln_normed, ln_sig, ln_out = (
            sem(n) for n in ("mean_ready", "centred", "squared", "var_ready", "ln_rstd", "ln_normed", "ln_sig", "ln_out"))
        score_ready, masked, keT_psum, keT_ready = sem("score_ready"), sem("masked"), sem("keT_psum"), sem("keT_ready")
        dstate_ready, state_ready, o_ready, o_saved = sem("dstate_ready"), sem("state_ready"), sem("o_ready"), sem("o_saved")
        o_squared, o_ms, o_rstd, o_gated = sem("o_squared"), sem("o_ms"), sem("o_rstd"), sem("o_gated")
        oT_psum, yT_rec, yT_conv = sem("oT_psum"), sem("yT_rec"), sem("yT_conv")
        a_norm, a_out, a_rec, a_ln = (sem(n) for n in ("a_norm", "a_out", "a_rec", "a_ln"))
        conv_step, v_head, y_normed, v_rec, v_ln, g_done, diff_ready = (
            sem(n) for n in ("conv_step", "v_head", "y_normed", "v_rec", "v_ln", "g_done", "diff_ready"))
        CONV_STEPS = NCH * CW + NCH
        block = ctx.enter_context(nc.Block())

        x_d, x1_d, xn_d = ap["x"][0], ap["x1"], ap["xn"]
        w_d = ap["w_in"][0].rearrange("(k p) n -> p k n", p=P)
        NPIECE = 12
        GATE, Q, FG, VI, GG = DC, 2 * DC, 3 * DC, 4 * DC, 5 * DC
        PIECES = [((j * P, P), (GATE + j * P, P)) for j in range(NCH)]
        PIECES += [((Q + j * P, P), (FG + j * P, P)) for j in range(NH)]
        PIECES += [((GG + j * 256, 256),) for j in range(2)] + [((VI + j * 256, 256),) for j in range(2)]
        AU = 2 * NPIECE

        MODS, ADA_PIECES = 6, 12
        ada_slot = [wo[:, 0:4], wo[:, 4:8]] + [heads_buf[:, 2 * i:2 * i + 2].rearrange("p a (b n) -> p (a b) n", n=D) for i in range(2)]
        slot_of = lambda p: p if p < 4 else p % 2
        ada_load = lambda p: (ada_in[p], 16) if p < 4 else (ada_in[4 + p % 2], 16 * (p // 2 - 1))
        ada_acc = [yt[:, 0], yt[:, 1], xres[:, 0], xres[:, 1], yt[:, 0], yt[:, 1]]

        def load_ada(eng, p):
            m, half = p // 2, p % 2
            eng.dma_start(ada_slot[slot_of(p)], ap["w_ada"][0, half * 512:(half + 1) * 512, m * D:(m + 1) * D]
                          .rearrange("(k p) n -> p k n", p=P)).then_inc(ada_load(p)[0], 16)

        def load_vectors(eng, part):
            if part == 0:
                eng.dma_start(scr[0:CW, 0:DC], ap["dw_kernel"][0]).then_inc(vec_in, 16)
            for name in list(VEC)[part::2]:
                a, b = VEC[name]
                eng.dma_start(tmp[a:b, 0:P], ap[name].rearrange("a (k p) -> (a k) p", p=P)).then_inc(vec_in, 16)

        def win_bytes(t, j):
            per_block = sum(16 * len(PIECES[i]) for i in range(NPIECE) if i % NSLOT == j % NSLOT)
            return t * per_block + sum(16 * len(PIECES[i]) for i in range(j + 1) if i % NSLOT == j % NSLOT)

        STEPS = [("mean",), ("y", 0, 0), ("var",), ("y", 0, 1), ("A", 0), ("y", 1, 0), ("B", 0), ("r", 0), ("O", 0),
                 ("A", 1), ("y", 1, 1), ("B", 1), ("l", 0), ("O", 1),
                 ("A", 2), ("y", 2, 0), ("B", 2), ("r", 1), ("O", 2),
                 ("A", 3), ("y", 2, 1), ("B", 3), ("l", 1), ("O", 3),
                 ("y", 3, 0), ("y", 3, 1), ("r", 2), ("T", 0), ("T", 1), ("l", 2), ("oT", 0), ("oT", 1),
                 ("r", 3), ("oT", 2), ("oT", 3), ("l", 3), ("T", 2), ("T", 3)]
        USES = {"y": 1, "r": 2, "l": 1, "T": 2}

        TAIL = [("y", 0, 0), ("y", 0, 1), ("y", 1, 0), ("y", 1, 1), ("r", 0), ("y", 2, 0), ("y", 2, 1), ("l", 0), ("r", 1),
                ("y", 3, 0), ("y", 3, 1), ("l", 1), ("r", 2), ("l", 2), ("r", 3), ("l", 3)]
        tail_bank = [pS, pO, pD, pT] + bank

        def stage_units(kinds, steps=STEPS):
            return [(s[0], s[1], s[2] if s[0] == "y" else h) for s in steps if s[0] in kinds for h in range(USES.get(s[0], 0))]

        def stage_banks(mix, out, nxt):
            units = stage_units(kinds_of(out, nxt), STEPS if mix else TAIL)
            return {unit: bank[n % 4] if mix else tail_bank[n % 8] for n, unit in enumerate(units)}

        def reader(kind, i, half, t):
            if kind == "T":
                return hT_ready, t * 2 * NT + 2 * i + half + 1
            if kind == "y":
                return y_normed, t * 2 * NT + 2 * i + half + 1
            if kind == "r":
                return rin_ready, t * 2 * NT + 2 * i + half + 1
            if kind == "l":
                return logit_saved, t * NT + i + 1
            n = i
            if n < 8:
                return u_ready, t * NCH + n // 2 + 1
            if n < 16:
                return q_parts, (t * NH + (n - 8) // 2) * 3 + 2 + n % 2
            if n < 20:
                return g_parts, t * 8 + 2 * (n - 16) + 2
            return v_ready, t * 4 + (n - 20) + 1

        def kinds_of(out, nxt):
            return ("y", "r", "l") * out + ("T",) * nxt

        @block.sync
        def _(sp):
            def load_x(t, i):
                wait(sp, xT_ready, t * 2 * NT + 2 * (i - 2) + 2)
                sp.sem_inc(sp_passed, 1)
                sp.dma_start(xt[:, i % 2], x_d[bass.ds(t * T + i * P, P), :]).then_inc(x_in[i % 2], 16)

            def load_piece(t, j):
                wait(sp, proj_ready, t * AU + 2 * (j - NSLOT) + 2)
                sp.sem_inc(sp_passed, 1)
                at = 0
                for a, n in PIECES[j]:
                    sp.dma_start(win[:, j % NSLOT, :, at:at + n], w_d[:, :, a:a + n]).then_inc(win_in[j % NSLOT], 16)
                    at += n

            load_vectors(sp, 0)
            load_x(0, 0)
            load_x(0, 1)
            for p in range(4):
                load_ada(sp, p)
            for j in range(NSLOT):
                load_piece(0, j)
            load_x(0, 2)
            load_x(0, 3)
            with sp.Fori(0, NB - 1) as t:
                for j in range(NSLOT, NPIECE):
                    load_piece(t, j)
                load_x(t + 1, 0)
                load_x(t + 1, 1)
                for j in range(NSLOT):
                    load_piece(t + 1, j)
                load_x(t + 1, 2)
                load_x(t + 1, 3)
            for j in range(NSLOT, NPIECE):
                load_piece(NB - 1, j)

        @block.gpsimd
        def _(pool):
            def store(t, n_residual):
                for i in range(NT):
                    rows = bass.ds(t * T + i * P, P)
                    wait_apart(pool, x1_ready, t * NT + i + 1, pool_passed)
                    pool.dma_start(x1_d[rows, :], yt[:, i % 2]).then_inc(x1_stored[i % 2], 16)
                    wait_apart(pool, xn_ready, t * NT + i + 1, pool_passed)
                    pool.dma_start(xn_d[rows, :], xres[:, i % 2]).then_inc(xn_stored[i % 2], 16)
                    if i < n_residual:
                        wait_apart(pool, res_free, t * NT + i + 3, pool_passed)
                        wait_apart(pool, xn_stored[i % 2], t * 32 + 16 * (i // 2 + 1), pool_passed)
                        pool.dma_start(xres[:, i % 2], x_d[bass.ds(t * T + (i + 2) * P, P), :]).then_inc(res_in[i % 2], 16)

            ch = Chain(pool, mask_step)
            ch.step(nc.gpsimd.memset(c.ident[:], 0.0))
            ch.step(nc.gpsimd.memset(c.ones[:], 1.0))
            ch.step(nc.gpsimd.memset(c.causal[:], 1.0))
            ch.step(nc.gpsimd.memset(c.restart[:], 1.0))
            ch.step(nc.gpsimd.memset(c.epsc[:], EPS))
            ch.sync()
            ch.step(nc.gpsimd.affine_select(out=c.ident[:], in_=c.ident[:], compare_op=ALU.not_equal, fill=1.0,
                                            base=0, pattern=[[-1, P]], channel_multiplier=1))
            ch.step(nc.gpsimd.affine_select(out=c.causal[:], in_=c.causal[:], compare_op=ALU.is_ge, fill=0.0,
                                            base=0, pattern=[[1, P]], channel_multiplier=-1))
            ch.sync()
            ch.step(nc.gpsimd.memset(c.causal[0:CH, CH:P], 0.0))
            ch.step(nc.gpsimd.memset(c.restart[:].rearrange("p (n k) -> p n k", k=CH)[:, :, 0:1], 0.0))
            ch.step(nc.gpsimd.memset(c.zeros[:], 0.0))
            ch.sync()
            pool.sem_inc(masks_ready, 1)
            pool.dma_start(c.wroute[:, :, 0:NG], ap["w_router_group"][0].rearrange("(k p) n -> p k n", p=P),
                           allow_slow_non_contiguous=True).then_inc(route_in, 16)
            pool.dma_start(c.wroute[:, :, NG:NR],
                           ap["w_router_expert"][0].rearrange("(k p) n -> p k n", p=P)).then_inc(route_in, 16)
            pool.dma_start(c.brow[0:1, 0:NG], ap["b_router_group"]).then_inc(route_in, 16)
            pool.dma_start(c.brow[0:1, NG:NR], ap["b_router_expert"]).then_inc(route_in, 16)
            for p in range(4, ADA_PIECES):
                pool.wait_ge(ada_used, p - 3 if p < 6 else p - 1)
                load_ada(pool, p)
            pool.wait_ge(ada_used, ADA_PIECES)
            pool.dma_start(wo[:], ap["w_out"][0].rearrange("(k p) n -> p k n", p=P)).then_inc(wo_in, 16)
            pool.wait_ge(grow_ready, 1)
            for i in range(2):
                pool.dma_start(xres[:, i], x_d[i * P:(i + 1) * P, :]).then_inc(res_in[i], 16)
            with pool.Fori(MINBLK, NBLK) as b:
                pool.dma_start(ap["y"][bass.ds(b * P, P), :].rearrange("p (a n) -> p a n", n=P),
                               c.zeros[:].unsqueeze(1).to_broadcast([P, KD, P])).then_inc(y_cleared, 16)
            with pool.Fori(0, NB - 1) as t:
                store(t, NT)
            store(NB - 1, 2)
            pool.wait_ge(y_cleared, (NBLK - MINBLK) * 16)
            for s in x1_stored + xn_stored:
                pool.wait_ge(s, NB * 32)

        @block.tensor
        def _(pe):
            def ring(units, before, banks=bank):
                size = len(banks)
                for n in range(len(units)):
                    if n >= size:
                        wait(pe, *reader(*units[n - size]))
                    elif before and n >= size - 4:
                        wait(pe, *reader(*before[n - size + 4]))
                    yield banks[n % size]

            def turn_in(t, i, banks):
                pe.wait_ge(x_normed, t * NT + i + 1)
                for half in range(2):
                    out = next(banks)
                    for j in range(4):
                        k = half * 4 + j
                        last = nc.tensor.transpose(out[:, j * P:(j + 1) * P], xt[:, i % 2, k * P:(k + 1) * P], c.ident[:])
                    last.then_inc(xT_ready, 1)

            def ada_columns(m):
                pe.wait_ge(ada_used, 2 * m + 2)
                for j in range(KD):
                    last = nc.tensor.matmul(pT[:, m * KD + j:m * KD + j + 1], ada_acc[m][:, j * P:(j + 1) * P],
                                            c.ones[:, 0:1], start=True, stop=True)
                last.then_inc(ada_cols_done, 1)

            def project(t, with_ada=False):
                banks = ring([("A", n, 0, t) for n in range(AU)], [("T", 2 + n // 2, n % 2, t) for n in range(4)])
                for j in range(NPIECE):
                    w = win[:, j % NSLOT]
                    pe.wait_ge(win_in[j % NSLOT], win_bytes(t, j))
                    if j == 0:
                        pe.wait_ge(hT_ready, (t + 1) * 2 * NT)
                    for half in range(2):
                        out = next(banks)
                        if j < 8:
                            for k in range(KD):
                                last = nc.tensor.matmul(out[:], w[:, k, half * P:(half + 1) * P], hT[:, k, :],
                                                        start=(k == 0), stop=(k == KD - 1))
                        else:
                            for s in range(2):
                                i = 2 * half + s
                                for k in range(KD):
                                    last = nc.tensor.matmul(out[:, s * 256:(s + 1) * 256], hT[:, k, i * P:(i + 1) * P],
                                                            w[:, k, :], start=(k == 0), stop=(k == KD - 1))
                        last.then_inc(proj_ready, 1)
                    if with_ada and 4 <= j < 8:
                        ada_columns(j - 2)

            def y_half(t, i, half, banks):
                if i == 0 and half == 0:
                    pe.wait_ge(wo_in, 16)
                    pe.wait_ge(yT_rec, (t + 1) * NT)
                    pe.wait_ge(yT_conv, (t + 1) * NCH)
                out = next(banks)
                for k in range(KD):
                    last = nc.tensor.matmul(out[:], yT[:, k, i * P:(i + 1) * P], wo[:, k, half * 512:(half + 1) * 512],
                                            start=(k == 0), stop=(k == KD - 1))
                last.then_inc(y_ready, 1)

            def router_turn(t, i, banks):
                pe.wait_ge(xn_ready, t * NT + i + 1)
                for half in range(2):
                    out = next(banks)
                    for j in range(4):
                        k = half * 4 + j
                        last = nc.tensor.transpose(out[:, j * P:(j + 1) * P], xres[:, i % 2, k * P:(k + 1) * P], c.ident[:])
                    last.then_inc(rT_ready, 1)
                pe.wait_ge(rT_ready, t * 2 * NT + 2 * i + 2)
                pe.sem_inc(res_free, 1)

            def logits(t, i, banks):
                pe.wait_ge(rin_ready, t * 2 * NT + 2 * i + 2)
                out = next(banks)
                for k in range(KD):
                    nc.tensor.matmul(out[:, 0:NR], yt[:, i % 2, k * P:(k + 1) * P], c.wroute[:, k, :], start=(k == 0), stop=False)
                nc.tensor.matmul(out[:, 0:NR], c.ones[0:1, :], c.brow[:], start=False, stop=True).then_inc(logit_ready, 1)

            def mean(t):
                pe.wait_ge(conv_step, (t + 1) * CONV_STEPS)
                wait(pe, masked, t * NT)
                for k in range(NCH):
                    last = nc.tensor.matmul(pS[:], c.ones[:], cv[:, k, :], start=(k == 0), stop=(k == NCH - 1))
                last.then_inc(mean_ready, 1)

            def variance(t):
                wait(pe, o_saved, t * NT)
                for k in range(NCH):
                    pe.wait_ge(squared, t * NCH + k + 1)
                    last = nc.tensor.matmul(pO[:], c.ones[:], hT[:, k, :], start=(k == 0), stop=(k == NCH - 1))
                last.then_inc(var_ready, 1)

            def scores(t, i):
                tok = slice(i * P, (i + 1) * P)
                if i == 0:
                    pe.wait_ge(exp_used, (t + 1) * 3 * NH)
                    pe.wait_ge(centred, (t + 1) * NCH)
                    wait(pe, yT_rec, t * NT)
                else:
                    pe.wait_ge(masked, t * NT + i)
                for h in range(NH):
                    last = nc.tensor.matmul(pS[:, h * P:(h + 1) * P], ki[:, h, tok], qd[:, h, tok], start=True, stop=True)
                last.then_inc(score_ready, 1)
                if i > 0:
                    pe.wait_ge(state_ready, t * 2 * NT + 2 * i)
                for h in range(NH):
                    last = nc.tensor.transpose(pT[:, h * P:(h + 1) * P], ke[:, h, tok], c.ident[:])
                last.then_inc(keT_psum, 1)

            def state_sums(t, i):
                pe.wait_ge(keT_ready, t * NT + i + 1)
                if i == 0:
                    pe.wait_ge(v_ready, (t + 1) * 4)
                for s, out in ((0, pD), (1, pT)):
                    rows = slice(s * CH, (s + 1) * CH)
                    for h in range(NH):
                        last = nc.tensor.matmul(out[:, h * P:(h + 1) * P], scr[rows, (i % 2) * 512 + h * P:(i % 2) * 512 + (h + 1) * P],
                                                v[rows, i, h * P:(h + 1) * P], start=True, stop=True)
                    last.then_inc(dstate_ready, 1)

            def outputs(t, i):
                pe.wait_ge(masked, t * NT + i + 1)
                pe.wait_ge(state_ready, t * 2 * NT + 2 * i + 1)
                if i == 0:
                    pe.wait_ge(ln_rstd, t + 1)
                else:
                    pe.wait_ge(o_saved, t * NT + i)
                for h in range(NH):
                    hc = slice(h * P, (h + 1) * P)
                    nc.tensor.matmul(pO[:, hc], c.scoreT[:, i % 2, hc], v[:, i, hc], start=True, stop=False, skip_group_check=True)
                    for s in range(2):
                        at = i * P + s * CH
                        last = nc.tensor.matmul(pO[s * CH:(s + 1) * CH, hc], qd[:, h, at:at + CH],
                                                c.state[:, (2 * i + s) % 4, hc], start=False, stop=(s == 1), skip_group_check=True)
                last.then_inc(o_ready, 1)

            def turn_outputs(t, i):
                if i == 0:
                    pe.wait_ge(o_gated, t + 1)
                if i >= 2:
                    pe.wait_ge(yT_rec, t * NT + i - 1)
                out = (pT, pD)[i % 2]
                for h in range(NH):
                    last = nc.tensor.transpose(out[:, h * P:(h + 1) * P], ob[:, i, h * P:(h + 1) * P], c.ident[:])
                last.then_inc(oT_psum, 1)

            def steps(t, mix, out, nxt, before):
                block_of_kind = {"T": t + 1, "y": t - 1, "r": t - 1, "l": t - 1}
                order = STEPS if mix else TAIL
                banks = ring([(k, i, h, block_of_kind[k]) for k, i, h in stage_units(kinds_of(out, nxt), order)], before,
                             bank if mix else tail_bank)
                for kind, *at in order:
                    if kind in ("y", "r", "l"):
                        if out:
                            {"y": y_half, "r": router_turn, "l": logits}[kind](t - 1, *at, banks)
                    elif kind == "T":
                        if nxt:
                            turn_in(t + 1, *at, banks)
                    elif mix:
                        {"mean": mean, "var": variance, "A": scores, "B": state_sums, "O": outputs, "oT": turn_outputs}[kind](t, *at)

            after_project = lambda t: [("A", AU - 4 + n, 0, t) for n in range(4)]

            pe.wait_ge(masks_ready, 1)
            pe.wait_ge(vec_in, 16 * (len(VEC) + 1))
            nc.tensor.transpose(pS[:, 0:NVEC], tmp[0:NVEC, 0:P], c.ident[0:NVEC, 0:NVEC])
            for k in range(NCH):
                last = nc.tensor.transpose(pO[:, k * CW:(k + 1) * CW], scr[0:CW, k * P:(k + 1) * P], c.ident[0:CW, 0:CW])
            last.then_inc(turned, 1)
            first = ring([("T", n // 2, n % 2, 0) for n in range(2 * NT)], None)
            turn_in(0, 0, first)
            turn_in(0, 1, first)
            ada_columns(0)
            ada_columns(1)
            turn_in(0, 2, first)
            turn_in(0, 3, first)
            project(0, with_ada=True)
            for r, out in ((0, pD), (1, pO)):
                pe.wait_ge(diag_ready, r + 1)
                nc.tensor.matmul(out[:], c.ones[:], xres[:, 0, r * 512:(r + 1) * 512], start=True, stop=True).then_inc(row_done, 1)
            pe.wait_ge(mod_ready, 1)
            pe.wait_ge(route_in, 64)
            for k in range(KD):
                last = nc.tensor.matmul(pT[0:1, 64:64 + NR], c.shift2[:, k:k + 1], c.wroute[:, k, :],
                                        start=(k == 0), stop=(k == KD - 1))
            last.then_inc(row_done, 1)
            pe.sem_inc(res_free, 2)
            steps(0, True, False, True, after_project(0))
            with pe.Fori(1, NB - 1) as t:
                project(t)
                steps(t, True, True, True, after_project(t))
            project(NB - 1)
            steps(NB - 1, True, True, False, after_project(NB - 1))
            ended = [(k, i, h, NB - 2) for k, i, h in stage_units(kinds_of(True, False))[-4:]]
            steps(NB, False, True, False, ended)

        @block.scalar
        def _(act):
            A = nc.scalar.activation
            logs = lambda: act.preload_act_table_set("natural_log_exp_and_others")

            def x_sums(t, i, junk):
                ch = Chain(act, a_norm, t * 2 * NT + 2 * i)
                act.wait_ge(x_in[i % 2], t * 32 + 16 * (i // 2 + 1))
                ch.link(A(junk, xt[:, i % 2], ACT.Square, accum_out=sums[:, i:i + 1]))
                ch.link(A(sums[:, i:i + 1], sums[:, i:i + 1], ACT.Ln, bias=c.epsc[:], scale=1.0 / D))
                A(sums[:, i:i + 1], sums[:, i:i + 1], ACT.Exp, scale=-0.5).then_inc(x_rstd, 1)

            def modulate(t, i, banks):
                for half in range(2):
                    act.wait_ge(xT_ready, t * 2 * NT + 2 * i + half + 1)
                    for j in range(4):
                        k = half * 4 + j
                        last = A(hT[:, k, i * P:(i + 1) * P], banks[half][:, j * P:(j + 1) * P], ACT.Identity,
                                 scale=c.scale1[:, k:k + 1], bias=c.shift1[:, k:k + 1])
                    last.then_inc(hT_ready, 1)

            def gates(t):
                for j in range(NCH):
                    act.wait_ge(proj_ready, t * AU + 2 * j + 2)
                    if j == 0:
                        wait(act, yT_conv, t * NCH)
                    A(cv[:, j], bank[(2 * j + 1) % 4][:], ACT.Sigmoid).then_inc(gate_sig, 1)
                for h in range(NH):
                    n = 8 + 2 * h
                    act.wait_ge(proj_ready, t * AU + n + 1)
                    if h == 0:
                        wait(act, o_ready, t * NT)
                        wait(act, keT_psum, t * NT)
                    A(ke[:, h], bank[n % 4][:], ACT.Sigmoid).then_inc(q_parts, 1)
                    A(qd[:, h], bank[n % 4][:], ACT.Copy).then_inc(q_parts, 1)
                    act.wait_ge(proj_ready, t * AU + n + 2)
                    A(ki[:, h], bank[(n + 1) % 4][:], ACT.Sigmoid).then_inc(q_parts, 1)
                for j in range(2):
                    for half in range(2):
                        n = 16 + 2 * j + half
                        act.wait_ge(proj_ready, t * AU + n + 1)
                        if n == 16:
                            wait(act, oT_psum, t * NT)
                        src = bank[n % 4][:].rearrange("p (a b) -> p a b", a=2)
                        cols = slice(j * 256, (j + 1) * 256)
                        A(ob[:, 2 * half:2 * half + 2, cols], src, ACT.Sigmoid).then_inc(g_parts, 1)
                        A(gs[:, 2 * half:2 * half + 2, cols], src, ACT.Copy).then_inc(g_parts, 1)

            def values(t, n0, n1):
                for n in range(n0, n1):
                    j, half = (n - 20) // 2, n % 2
                    act.wait_ge(proj_ready, t * AU + n + 1)
                    src = bank[n % 4][:].rearrange("p (a b) -> p a b", a=2)
                    A(v[:, 2 * half:2 * half + 2, j * 256:(j + 1) * 256], src, ACT.Copy).then_inc(v_ready, 1)

            def heads(t):
                bb, ee = scr[:, 0:T], scr[:, T:2 * T]
                act.preload_act_table_set("natural_log_exp_and_others")
                for h in range(NH):
                    n = t * NH + h
                    act.wait_ge(forget_ready, n + 1)
                    if h > 0:
                        act.wait_ge(diff_ready, n)
                    A(bb, ki[:, h], ACT.Ln).then_inc(logf_ready, 1)
                    act.wait_ge(b_ready, n + 1)
                    A(ee, bb, ACT.Exp).then_inc(exp_ready, 1)
                    A(decay[:, h], bb[:, CH - 1::CH], ACT.Exp).then_inc(exp_ready, 1)
                    act.wait_ge(exp_used, 3 * n + 1)
                    A(ee, bb, ACT.Exp, scale=-1.0).then_inc(exp_ready, 1)
                    act.wait_ge(diff_ready, n + 1)
                    A(tmp[:], tmp[:], ACT.Exp).then_inc(exp_ready, 1)
                    values(t, 20 + h, 21 + h)
                    act.wait_ge(exp_used, 3 * n + 3)

            def y_sums(t, i, places):
                ch = Chain(act, a_out, t * 7 * NT + 7 * i)
                s = sums[:, 8 + 2 * (i % 2):10 + 2 * (i % 2)]
                r = sums[:, 12 + i % 2:13 + i % 2]
                wait(act, x1_ready, t * NT + max(i - 1, 0))
                wait(act, logit_ready, t * NT + max(i - 1, 0))
                for half in range(2):
                    act.wait_ge(y_ready, t * 2 * NT + 2 * i + half + 1)
                    ch.link(A(yt[:, i % 2, half * 512:(half + 1) * 512], places["y", i, half][:], ACT.Square,
                              accum_out=s[:, half:half + 1]))
                ch.link(A(r, s[:, 0:1], ACT.Identity, bias=s[:, 1:2]))
                ch.link(A(r, r, ACT.Ln, bias=c.epsc[:], scale=1.0 / D))
                A(r, r, ACT.Exp, scale=-0.5).then_inc(y_rstd, 1)

            def x1_sums(t, i):
                ch = Chain(act, a_out, t * 7 * NT + 7 * i + 4)
                r = sums[:, 14 + i % 2:15 + i % 2]
                act.wait_ge(x1_ready, t * NT + i + 1)
                for half in range(2):
                    cols = slice(half * 512, (half + 1) * 512)
                    ch.link(A(xres[:, i % 2, cols], yt[:, i % 2, cols], ACT.Square, accum_out=sums[:, 16 + half:17 + half]))
                ch.link(A(r, sums[:, 16:17], ACT.Identity, bias=sums[:, 17:18]))
                A(r, r, ACT.Ln, bias=c.epsc[:], scale=1.0 / D).then_inc(x1_rstd, 1)
                act.wait_ge(x1_rstd, (t * NT + i) * 2 + 1)
                A(r, r, ACT.Exp, scale=-0.5).then_inc(x1_rstd, 1)

            def router_in(t, i, places):
                act.wait_ge(x1_stored[i % 2], t * 32 + 16 * (i // 2 + 1))
                for half in range(2):
                    act.wait_ge(rT_ready, t * 2 * NT + 2 * i + half + 1)
                    A(yt[:, i % 2, half * 512:(half + 1) * 512], places["r", i, half][:], ACT.Copy).then_inc(rin_ready, 1)

            def squares(t):
                act.wait_ge(centred, (t + 1) * NCH)
                act.wait_ge(proj_ready, (t + 1) * AU)
                for k in range(NCH):
                    A(hT[:, k, :], cv[:, k], ACT.Square).then_inc(squared, 1)

            def variance(t):
                act.wait_ge(var_ready, t + 1)
                A(hT[:, 4, :], pO[:], ACT.Ln, bias=c.epsc[:], scale=1.0 / DC).then_inc(a_ln, 1)
                act.wait_ge(a_ln, t + 1)
                A(hT[:, 4, :], hT[:, 4, :], ACT.Exp, scale=-0.5).then_inc(ln_rstd, 1)

            def conv_gate(t):
                for k in range(NCH):
                    act.wait_ge(ln_normed, t * NCH + k + 1)
                    A(hT[:, k, :], cv[:, k], ACT.Sigmoid, scale=col("conv_ln_gain", k), bias=col("conv_ln_bias", k)).then_inc(ln_sig, 1)
                logs()

            def save_keys(t, i):
                act.wait_ge(keT_psum, t * NT + i + 1)
                if i >= 2:
                    act.wait_ge(dstate_ready, t * 2 * NT + 2 * (i - 1))
                A(scr[:, (i % 2) * 512:(i % 2 + 1) * 512], pT[:], ACT.Copy).then_inc(keT_ready, 1)

            def square_outputs(t, i):
                act.wait_ge(o_saved, t * NT + i + 1)
                wait(act, o_ms, t * NT + i)
                A(tmp[:], ob[:, i], ACT.Square).then_inc(o_squared, 1)

            def outputs_rstd(t):
                ch = Chain(act, a_rec, t)
                act.wait_ge(o_ms, (t + 1) * NT)
                ch.link(A(sums[:, 32:48], sums[:, 32:48], ACT.Ln, bias=c.epsc[:], scale=1.0 / P))
                A(sums[:, 32:48], sums[:, 32:48], ACT.Exp, scale=-0.5).then_inc(o_rstd, 1)

            def save_turned(t, i):
                act.wait_ge(oT_psum, t * NT + i + 1)
                A(yT[:, NH:, i * P:(i + 1) * P], (pT, pD)[i % 2][:].rearrange("p (h n) -> p h n", h=NH), ACT.Copy,
                  scale=col("rec_norm_gain", 0)).then_inc(yT_rec, 1)

            ORDER = [("sq",), ("var",), ("ysum", 0), ("key", 0), ("x1sum", 0), ("rin", 0), ("osq", 0), ("key", 1), ("ysum", 1),
                     ("x1sum", 1), ("osq", 1), ("xsum", 0), ("xsum", 1), ("key", 2), ("gate",), ("rin", 1), ("osq", 2), ("key", 3),
                     ("ysum", 2), ("x1sum", 2), ("osq", 3), ("orstd",), ("ysum", 3), ("x1sum", 3), ("rin", 2), ("T", 0), ("T", 1),
                     ("turned", 0), ("turned", 1), ("rin", 3), ("turned", 2), ("turned", 3), ("xsum", 2), ("xsum", 3),
                     ("T", 2), ("T", 3)]

            TAIL_ORDER = [("ysum", 0), ("x1sum", 0), ("ysum", 1), ("rin", 0), ("x1sum", 1), ("ysum", 2), ("rin", 1), ("x1sum", 2),
                          ("ysum", 3), ("rin", 2), ("x1sum", 3), ("rin", 3)]

            def steps(t, mix, out, nxt):
                places = stage_banks(mix, out, nxt)
                act.sem_inc(act_passed, 1)
                logs()
                for kind, *at in (ORDER if mix else TAIL_ORDER):
                    if kind in ("ysum", "x1sum", "rin"):
                        if out:
                            if kind == "x1sum":
                                x1_sums(t - 1, *at)
                            else:
                                {"ysum": y_sums, "rin": router_in}[kind](t - 1, *at, places)
                    elif kind == "xsum":
                        if nxt:
                            if at[0] == 2:
                                act.wait_ge(dstate_ready, (t + 1) * 2 * NT)
                            x_sums(t + 1, *at, hT[:, 5:7, :].rearrange("p a n -> p (a n)") if at[0] < 2 else scr[:])
                    elif kind == "T":
                        if nxt:
                            if at[0] == 0:
                                act.wait_ge(ln_out, (t + 1) * NCH)
                            modulate(t + 1, *at, (places["T", at[0], 0], places["T", at[0], 1]))
                    elif mix:
                        {"sq": squares, "var": variance, "key": save_keys, "gate": conv_gate, "osq": square_outputs,
                         "orstd": outputs_rstd, "turned": save_turned}[kind](t, *at)

            load_vectors(act, 1)
            act.wait_ge(cols_ready, 1)
            A(cond[:], c.cols[:, VEC["c"][0]:VEC["c"][1]], ACT.Silu).then_inc(cond_ready, 1)
            logs()
            act.wait_ge(lb_in, 1)
            A(lbt[:, 1:3], lbt[:, 1:3], ACT.Exp).then_inc(lb_exp, 1)
            x_sums(0, 0, scr[:])
            x_sums(0, 1, scr[:])
            act.wait_ge(scale1_ready, 1)
            for i in range(NT):
                modulate(0, i, bank[2 * (i % 2):2 * (i % 2) + 2])
                if i < 2:
                    x_sums(0, i + 2, scr[:])
            gates(0)
            heads(0)
            steps(0, True, False, True)
            with act.Fori(1, NB - 1) as t:
                gates(t)
                heads(t)
                steps(t, True, True, True)
            gates(NB - 1)
            heads(NB - 1)
            steps(NB - 1, True, True, False)
            steps(NB, False, True, False)

        @block.vector
        def _(dve):
            V = nc.vector

            def norm_in(t, i):
                dve.wait_ge(x_rstd, t * NT + i + 1)
                V.tensor_scalar(xt[:, i % 2], xt[:, i % 2], sums[:, i:i + 1], None, ALU.mult).then_inc(x_normed, 1)

            def ada_sums(m):
                for half in range(2):
                    p = 2 * m + half
                    dve.wait_ge(*ada_load(p))
                    for k in range(4):
                        w, factor = ada_slot[slot_of(p)][:, k], cond[:, 4 * half + k:4 * half + k + 1]
                        if half == 0 and k == 0:
                            ins = V.tensor_scalar(ada_acc[m], w, factor, None, ALU.mult)
                        else:
                            mod_chain.sync()
                            ins = V.scalar_tensor_tensor(out=ada_acc[m], in0=w, scalar=factor, in1=ada_acc[m],
                                                         op0=ALU.mult, op1=ALU.add)
                        mod_chain.step(ins)
                    mod_chain.sync()
                    dve.sem_inc(ada_used, 1)

            def conv(t, with_ada=False):
                ch = Chain(dve, conv_step, t * CONV_STEPS)
                for k in range(NCH):
                    if isinstance(t, int) and t == 0:
                        ch.step(V.tensor_copy(u[:, k, 0:HALO], c.zeros[:, 0:HALO]))
                    else:
                        ch.step(V.tensor_copy(u[:, k, 0:HALO], u[:, k, T:T + HALO]))
                ch.sync()
                for j in range(NCH):
                    if with_ada:
                        ada_sums(2 + j)
                    dve.wait_ge(gate_sig, t * NCH + j + 1)
                    V.tensor_tensor(u[:, j, HALO:], bank[(2 * j) % 4][:], cv[:, j], ALU.mult).then_inc(u_ready, 1)
                dve.wait_ge(u_ready, (t + 1) * NCH)
                for w in range(CW):
                    for j in range(NCH):
                        tap = c.taps[:, j * CW + w:j * CW + w + 1]
                        if w == 0:
                            ins = V.tensor_scalar(cv[:, j], u[:, j, 0:T], tap, col("dw_bias", j), ALU.mult, ALU.add)
                        else:
                            dve.wait_ge(conv_step, ch.base + ch.n - NCH + 1)
                            ins = V.scalar_tensor_tensor(out=cv[:, j], in0=u[:, j, w:w + T], scalar=tap, in1=cv[:, j],
                                                         op0=ALU.mult, op1=ALU.add)
                        ch.step(ins)
                ch.sync()
                assert ch.n == CONV_STEPS

            def heads(t):
                ch = Chain(dve, v_head, t * 2 * NH)
                bb, ee = scr[:, 0:T], scr[:, T:2 * T]
                for h in range(NH):
                    dve.wait_ge(q_parts, (t * NH + h) * 3 + 3)
                    ch.step(V.tensor_tensor(qd[:, h], qd[:, h], ke[:, h], ALU.mult))
                    V.tensor_scalar(ki[:, h], ki[:, h], c.oneless[:, h:h + 1], c.lb[:, h:h + 1], ALU.mult, ALU.add).then_inc(forget_ready, 1)
                for h in range(NH):
                    n = t * NH + h
                    dve.wait_ge(forget_ready, n + 1)
                    dve.wait_ge(v_head, ch.base + NH)
                    ch.step(V.tensor_scalar(ke[:, h], ki[:, h], -1.0, 1.0, ALU.mult, ALU.add))
                    dve.wait_ge(logf_ready, n + 1)
                    V.tensor_tensor_scan(bb, c.restart[:], bb, 0.0, ALU.mult, ALU.add).then_inc(b_ready, 1)
                    dve.wait_ge(b_ready, n + 1)
                    b3 = bb.rearrange("p (n k) -> p n k", k=CH)
                    V.tensor_tensor(tmp[:].rearrange("p (n k) -> p n k", k=CH),
                                    b3[:, :, CH - 1:CH].to_broadcast([P, T // CH, CH]), b3, ALU.subtract).then_inc(diff_ready, 1)
                    dve.wait_ge(exp_ready, 4 * n + 2)
                    V.tensor_tensor(qd[:, h], qd[:, h], ee, ALU.mult).then_inc(exp_used, 1)
                    dve.wait_ge(exp_ready, 4 * n + 3)
                    ch.sync()
                    V.tensor_tensor(ki[:, h], ke[:, h], ee, ALU.mult).then_inc(exp_used, 1)
                    dve.wait_ge(exp_ready, 4 * n + 4)
                    V.tensor_tensor(ke[:, h], ke[:, h], tmp[:], ALU.mult).then_inc(exp_used, 1)
                assert ch.n == 2 * NH, ch.n

            def gate_values(t):
                dve.wait_ge(g_parts, (t + 1) * 8)
                V.tensor_tensor(gs[:], gs[:], ob[:], ALU.mult).then_inc(g_done, 1)
                dve.wait_ge(g_done, t + 1)

            def y_norm(t, i, places):
                dve.wait_ge(y_rstd, t * NT + i + 1)
                wait(dve, x1_stored[i % 2], t * 32 + 16 * (i // 2))
                for half in range(2):
                    cols = slice(half * 512, (half + 1) * 512)
                    V.scalar_tensor_tensor(out=yt[:, i % 2, cols], in0=places["y", i, half][:],
                                           scalar=sums[:, 12 + i % 2:13 + i % 2], in1=c.grow[:, cols],
                                           op0=ALU.mult, op1=ALU.mult).then_inc(y_normed, 1)
                dve.wait_ge(y_normed, t * 2 * NT + 2 * i + 2)
                dve.wait_ge(res_in[i % 2], t * 32 + 16 * (i // 2 + 1))
                V.tensor_tensor(yt[:, i % 2], yt[:, i % 2], xres[:, i % 2], ALU.add).then_inc(x1_ready, 1)

            def x1_norm(t, i):
                dve.wait_ge(x1_rstd, (t * NT + i + 1) * 2)
                V.tensor_scalar(xres[:, i % 2], yt[:, i % 2], sums[:, 14 + i % 2:15 + i % 2], None, ALU.mult).then_inc(xn_ready, 1)

            def save_logits(t, i, places):
                dve.wait_ge(logit_ready, t * NT + i + 1)
                V.tensor_copy(c.logits[:, bass.ds(t * NT + i, 1), :].rearrange("p a n -> p (a n)"),
                              places["l", i, 0][:, 0:NR]).then_inc(logit_saved, 1)

            def centre(t):
                dve.wait_ge(mean_ready, t + 1)
                for k in range(NCH):
                    V.scalar_tensor_tensor(out=cv[:, k], in0=pS[:], scalar=-1.0 / DC, in1=cv[:, k],
                                           op0=ALU.mult, op1=ALU.add).then_inc(centred, 1)

            def scale_conv(t):
                dve.wait_ge(ln_rstd, t + 1)
                for k in range(NCH):
                    V.tensor_tensor(cv[:, k], cv[:, k], hT[:, 4, :], ALU.mult).then_inc(ln_normed, 1)

            def conv_out(t):
                ch = Chain(dve, v_ln, t * NCH)
                for k in range(NCH):
                    dve.wait_ge(ln_sig, t * NCH + k + 1)
                    ch.step(V.tensor_scalar(cv[:, k], cv[:, k], col("conv_ln_gain", k), col("conv_ln_bias", k), ALU.mult, ALU.add))
                ch.sync()
                for k in range(NCH):
                    V.tensor_tensor(cv[:, k], cv[:, k], hT[:, k, :], ALU.mult).then_inc(ln_out, 1)

            def place_conv(t):
                wait(dve, y_ready, t * 2 * NT)
                dve.wait_ge(ln_out, (t + 1) * NCH)
                for k in range(NCH):
                    V.tensor_copy(yT[:, k, :], cv[:, k]).then_inc(yT_conv, 1)

            def mask(t, i):
                wait_apart(dve, score_ready, t * NT + i + 1, dve_passed)
                V.copy_predicated(c.scoreT[:, i % 2].rearrange("p (h n) -> p h n", h=NH),
                                  c.causal[:].bitcast(I32).unsqueeze(1).to_broadcast([P, NH, P]),
                                  pS[:].rearrange("p (h n) -> p h n", h=NH)).then_inc(masked, 1)

            def states(t, i):
                for s in range(2):
                    m = 2 * i + s
                    dve.wait_ge(dstate_ready, t * 2 * NT + m + 1)
                    wait(dve, state_ready, t * 2 * NT + m)
                    for h in range(NH):
                        hc = slice(h * P, (h + 1) * P)
                        last = V.scalar_tensor_tensor(out=c.state[:, (m + 1) % 4, hc], in0=c.state[:, m % 4, hc],
                                                      scalar=decay[:, h, m:m + 1], in1=(pD, pT)[s][:, hc], op0=ALU.mult, op1=ALU.add)
                    last.then_inc(state_ready, 1)

            def save_outputs(t, i):
                dve.wait_ge(o_ready, t * NT + i + 1)
                V.tensor_copy(ob[:, i], pO[:]).then_inc(o_saved, 1)

            def output_squares(t, i):
                dve.wait_ge(o_squared, t * NT + i + 1)
                V.tensor_reduce(sums[:, 32 + 4 * i:36 + 4 * i], tmp[:].rearrange("p (h n) -> p h n", h=NH), axis=AX.X, op=ALU.add).then_inc(o_ms, 1)

            def gate_outputs(t):
                dve.wait_ge(o_rstd, t + 1)
                o3 = ob[:].rearrange("p i (h n) -> p (i h) n", h=NH)
                V.tensor_tensor(o3, o3, sums[:, 32:48].unsqueeze(2).to_broadcast([P, NT * NH, P]), ALU.mult).then_inc(v_rec, 1)
                dve.wait_ge(v_rec, t + 1)
                V.tensor_tensor(ob[:], ob[:], gs[:], ALU.mult).then_inc(o_gated, 1)

            ORDER = [("centre",), ("ynorm", 0), ("scale",), ("mask", 0), ("state", 0), ("x1norm", 0), ("osave", 0), ("oms", 0),
                     ("mask", 1), ("ynorm", 1), ("state", 1), ("x1norm", 1), ("logit", 0), ("osave", 1), ("oms", 1),
                     ("mask", 2), ("xnorm", 0), ("xnorm", 1), ("state", 2), ("osave", 2), ("conv",), ("oms", 2),
                     ("mask", 3), ("ynorm", 2), ("state", 3), ("x1norm", 2), ("logit", 1), ("osave", 3), ("oms", 3),
                     ("gate",), ("ynorm", 3), ("x1norm", 3), ("logit", 2), ("place",), ("xnorm", 2), ("xnorm", 3), ("logit", 3)]

            TAIL_ORDER = [("ynorm", 0), ("x1norm", 0), ("ynorm", 1), ("x1norm", 1), ("logit", 0), ("ynorm", 2), ("x1norm", 2), ("logit", 1),
                          ("ynorm", 3), ("x1norm", 3), ("logit", 2), ("logit", 3)]

            def steps(t, mix, out, nxt):
                places = stage_banks(mix, out, nxt)
                for kind, *at in (ORDER if mix else TAIL_ORDER):
                    if kind in ("ynorm", "x1norm", "logit"):
                        if out:
                            if kind == "x1norm":
                                x1_norm(t - 1, *at)
                            else:
                                {"ynorm": y_norm, "logit": save_logits}[kind](t - 1, *at, places)
                    elif kind == "xnorm":
                        if nxt:
                            norm_in(t + 1, *at)
                    elif mix:
                        {"centre": centre, "scale": scale_conv, "mask": mask, "state": states, "osave": save_outputs,
                         "oms": output_squares, "conv": conv_out, "gate": gate_outputs, "place": place_conv}[kind](t, *at)

            cols = lambda n: c.cols[:, VEC[n][0]:VEC[n][1]]
            m_of = lambda i: mod[:, i * KD:(i + 1) * KD]
            ch = mod_chain = Chain(dve, mod_step)
            ch.step(V.memset(c.state[:], 0.0))
            ch.step(V.memset(c.scoreT[:], 0.0))
            dve.wait_ge(turned, 1)
            ch.step(V.tensor_copy(c.taps[:], pO[:, 0:NCH * CW]))
            ch.step(V.tensor_copy(c.cols[:], pS[:, 0:NVEC]))
            ch.sync()
            dve.sem_inc(cols_ready, 1)
            lb0 = VEC["lb_logits"][0]
            l0, l1 = c.cols[:, lb0:lb0 + NCH], c.cols[:, lb0 + NCH:lb0 + 2 * NCH]
            ch.link(V.tensor_tensor(lbt[:, 0], l0, l1, ALU.max))
            ch.step(V.tensor_tensor(lbt[:, 1], l0, lbt[:, 0], ALU.subtract))
            ch.link(V.tensor_tensor(lbt[:, 2], l1, lbt[:, 0], ALU.subtract))
            dve.sem_inc(lb_in, 1)
            dve.wait_ge(lb_exp, 1)
            ch.link(V.tensor_tensor(lbt[:, 3], lbt[:, 1], lbt[:, 2], ALU.add))
            ch.link(V.reciprocal(lbt[:, 0], lbt[:, 3]))
            ch.link(V.tensor_tensor(c.lb[:], lbt[:, 1], lbt[:, 0], ALU.mult))
            ch.step(V.tensor_scalar(c.oneless[:], c.lb[:], -1.0, 1.0, ALU.mult, ALU.add))
            norm_in(0, 0)
            norm_in(0, 1)
            dve.wait_ge(cond_ready, 1)
            ada_sums(0)
            ada_sums(1)
            dve.wait_ge(ada_cols_done, 2)
            mod_chain.link(V.tensor_tensor(mod[:, 0:2 * KD], pT[:, 0:2 * KD], c.cols[:, VEC["b_ada"][0]:VEC["b_ada"][0] + 2 * KD], ALU.add))
            mod_chain.step(V.scalar_tensor_tensor(out=c.scale1[:], in0=m_of(1), scalar=1.0, in1=cols("g_pre_mix"),
                                                  op0=ALU.add, op1=ALU.mult))
            mod_chain.link(V.tensor_copy(c.shift1[:], m_of(0)))
            dve.sem_inc(scale1_ready, 1)
            norm_in(0, 2)
            norm_in(0, 3)
            conv(0, with_ada=True)
            heads(0)
            gate_values(0)
            dve.wait_ge(ada_cols_done, MODS)
            mod_chain.link(V.tensor_tensor(mod[:, 2 * KD:], pT[:, 2 * KD:6 * KD], c.cols[:, VEC["b_ada"][0] + 2 * KD:VEC["b_ada"][1]], ALU.add))
            mod_chain.step(V.scalar_tensor_tensor(out=c.scale2[:], in0=m_of(4), scalar=1.0, in1=cols("g_pre_ffn"),
                                                  op0=ALU.add, op1=ALU.mult))
            mod_chain.step(V.tensor_copy(c.shift2[:], m_of(3)))
            mod_chain.step(V.tensor_tensor(c.gcol[:, 0:KD], m_of(2), cols("g_post_mix"), ALU.mult))
            mod_chain.link(V.tensor_tensor(c.gcol[:, KD:2 * KD], m_of(5), cols("g_post_ffn"), ALU.mult))
            dve.sem_inc(mod_ready, 1)
            for r in range(2):
                for j in range(4):
                    k = 4 * r + j
                    last = V.tensor_scalar(xres[:, 0, k * P:(k + 1) * P], c.ident[:], c.gcol[:, k:k + 1], None, ALU.mult)
                last.then_inc(diag_ready, 1)
            for r, src in ((0, pD), (1, pO)):
                dve.wait_ge(row_done, r + 1)
                mod_chain.step(V.tensor_copy(c.grow[:, r * 512:(r + 1) * 512], src[:]))
            mod_chain.sync()
            dve.sem_inc(grow_ready, 1)
            dve.wait_ge(row_done, 3)
            mod_chain.step(V.tensor_tensor(c.brow[:], c.brow[:], pT[0:1, 64:64 + NR], ALU.add))
            for k in range(KD):
                mod_chain.step(V.tensor_scalar(c.wroute[:, k, :], c.wroute[:, k, :], c.scale2[:, k:k + 1], None, ALU.mult))
            mod_chain.sync()
            steps(0, True, False, True)
            with dve.Fori(1, NB - 1) as t:
                conv(t)
                heads(t)
                gate_values(t)
                steps(t, True, True, True)
            conv(NB - 1)
            heads(NB - 1)
            gate_values(NB - 1)
            steps(NB - 1, True, True, False)
            steps(NB, False, True, False)


def routing_phase(nc, ap, c):
    with ExitStack() as ctx:
        sb = lambda n, s, d=F32: ctx.enter_context(nc.sbuf_tensor(n, s, d))
        sem = lambda n: ctx.enter_context(nc.semaphore(n))
        BIG = 1e30
        NA = 2 * NTILES
        lane, blk = sb("lane", [P, P]), sb("blk", [P, TAB])
        token, blkrow = sb("token", [P, NTILES]), sb("blkrow", [P, 16])
        tri, one16 = sb("tri16", [P, P], BF16), sb("one16", [P, P], BF16)
        trif = sb("trif", [P, P])
        t16 = [sb(f"t16_{i}", [P, NTILES]) for i in range(12)]
        g4 = [sb(f"g4_{i}", [P, NTILES, NG]) for i in range(3)]
        e8 = [sb(f"e8_{i}", [P, NTILES, NEG]) for i in range(6)]
        big = [sb(f"big{i}", [P, NTILES, NE]) for i in range(4)]
        hot = sb("hot", [P, NTILES, NE], BF16)
        cum = sb("cum", [P, NTILES + 1, NE], BF16)
        x32 = [sb(f"x32_{i}", [P, NE]) for i in range(4)]
        cmp_ = sb("cmp", [P, TAB, NE])
        destf, rowi, blki = sb("destf", [P, NA]), sb("rowi", [P, NA], I32), sb("blki", [P, NA], I32)
        rowf, blkf = sb("rowf", [P, NA]), sb("blkf", [P, NA])
        RING = 8
        at_row, at_blk = sb("at_row", [P, RING, P]), sb("at_blk", [P, RING, TAB])
        etab = sb("etab", [P, TAB])
        pr = ctx.enter_context(nc.psum_tensor("prank", [P, 512], F32))
        pc = ctx.enter_context(nc.psum_tensor("pcount", [P, 512], F32))
        pi = ctx.enter_context(nc.psum_tensor("pindex", [P, 512], F32))
        iota_done, tri_done, dve_step = sem("iota_done"), sem("tri_done"), sem("route_step")
        group_in, group_exp, expert_in, expert_exp = sem("group_in"), sem("group_exp"), sem("expert_in"), sem("expert_exp")
        row_ready, onehot_ready, fourth_ready = sem("row_ready"), sem("onehot_ready"), sem("fourth_ready")
        hot_ready, rank_ready, onehot_used = sem("hot_ready"), sem("rank_ready"), sem("onehot_used")
        block = ctx.enter_context(nc.Block())

        @block.sync
        def _(sp):
            for e in range(WSLOTS):
                load_expert(sp, ap, c, e, e)

        @block.gpsimd
        def _(pool):
            io = lambda out, n, **k: nc.gpsimd.iota(out, [[1, n]], base=0, allow_small_or_imprecise_dtypes=True, **k)
            io(lane[:], P, channel_multiplier=0)
            io(blk[:], TAB, channel_multiplier=0)
            nc.gpsimd.iota(blkrow[:], [[P, 16]], base=0, channel_multiplier=0, allow_small_or_imprecise_dtypes=True)
            nc.gpsimd.iota(token[:], [[P, NTILES]], base=0, channel_multiplier=1, allow_small_or_imprecise_dtypes=True)
            nc.gpsimd.memset(trif[:], 1.0).then_inc(tri_done, 1)
            pool.wait_ge(tri_done, 1)
            nc.gpsimd.affine_select(out=trif[:], in_=trif[:], compare_op=ALU.is_gt, fill=0.0,
                                    base=0, pattern=[[1, P]], channel_multiplier=-1).then_inc(iota_done, 1)
            pool.wait_ge(row_ready, 1)
            for n in range(3, NA, 4):
                if n >= RING:
                    pool.wait_ge(onehot_used, (n - RING) // 4 + 1)
                i = n % NTILES
                nc.gpsimd.tensor_scalar(at_blk[:, n % RING], blk[:], blkf[:, n:n + 1], token[:, i:i + 1],
                                        ALU.is_equal, ALU.mult).then_inc(fourth_ready, 1)

        @block.scalar
        def _(act):
            act.wait_ge(group_in, 1)
            nc.scalar.activation(g4[1][:], g4[0][:], ACT.Exp).then_inc(group_exp, 1)
            act.wait_ge(expert_in, 1)
            nc.scalar.activation(e8[2][:], e8[1][:], ACT.Exp)
            nc.scalar.activation(t16[5][:], t16[4][:], ACT.Exp).then_inc(expert_exp, 1)

        @block.tensor
        def _(pe):
            pe.wait_ge(hot_ready, 1)
            flat = lambda a: a.rearrange("p t e -> p (t e)")
            nc.tensor.matmul(pr[:], tri[:], flat(hot[:]), start=True, stop=False)
            nc.tensor.matmul(pr[:], one16[:], flat(cum[:, 0:NTILES]), start=False, stop=True)
            nc.tensor.matmul(pc[:, 0:NE], one16[:], cum[:, NTILES], start=True, stop=True).then_inc(rank_ready, 1)
            for n in range(NA):
                if n % 4 == 0:
                    pe.wait_ge(onehot_ready, n // 4 * 3 + 3)
                    pe.wait_ge(fourth_ready, n // 4 + 1)
                last = nc.tensor.matmul(pi[:, 0:TAB], at_row[:, n % RING], at_blk[:, n % RING], start=(n == 0), stop=(n == NA - 1))
                if n % 4 == 3:
                    last.then_inc(onehot_used, 1)

        @block.vector
        def _(dve):
            V = nc.vector
            L = Chain(dve, dve_step).link
            bc = lambda a, n: a.unsqueeze(2).to_broadcast([P, a.shape[1], n])
            dve.wait_ge(iota_done, 1)
            L(V.tensor_copy(tri[:], trif[:]))
            L(V.tensor_copy(one16[:], c.ones[:]))

            def first_max(vals, best, diff, cand, index, onehot, n):
                L(V.tensor_reduce(best[:], vals, axis=AX.X, op=ALU.max))
                ins = V.tensor_tensor(diff[:], vals, bc(best[:], n), ALU.subtract)
                L(ins)
                L(V.tensor_scalar(cand[:], diff[:], 0.0, -64.0, ALU.is_ge, ALU.mult))
                L(V.tensor_tensor(cand[:], cand[:], lane[:, 0:n].unsqueeze(1).to_broadcast([P, NTILES, n]), ALU.add))
                L(V.tensor_reduce(index[:], cand[:], axis=AX.X, op=ALU.min))
                L(V.tensor_tensor(onehot[:], cand[:], bc(index[:], n), ALU.is_equal))

            gl = c.logits[:, :, 0:NG]
            first_max(gl, t16[0], g4[0], g4[1], t16[1], g4[2], NG)
            dve.sem_inc(group_in, 1)
            dve.wait_ge(group_exp, 1)
            L(V.tensor_reduce(t16[2][:], g4[1][:], axis=AX.X, op=ALU.add))
            L(V.reciprocal(t16[2][:], t16[2][:]))
            el = c.logits[:, :, NG:NR].rearrange("p t (g e) -> p t g e", g=NG)
            b4 = big[0][:].rearrange("p t (g e) -> p t g e", g=NG)
            L(V.tensor_tensor(b4, el, g4[2][:].unsqueeze(3).to_broadcast([P, NTILES, NG, NEG]), ALU.mult))
            L(V.tensor_reduce(e8[0][:], big[0][:].rearrange("p t (g e) -> p t e g", g=NG), axis=AX.X, op=ALU.add))
            first_max(e8[0][:], t16[3], e8[1], e8[2], t16[1], e8[3], NEG)
            L(V.scalar_tensor_tensor(out=e8[0][:], in0=e8[3][:], scalar=-BIG, in1=e8[0][:], op0=ALU.mult, op1=ALU.add))
            first_max(e8[0][:], t16[6], e8[5], e8[2], t16[1], e8[4], NEG)
            L(V.tensor_tensor(t16[4][:], t16[6][:], t16[3][:], ALU.subtract))
            dve.sem_inc(expert_in, 1)
            dve.wait_ge(expert_exp, 1)
            L(V.tensor_reduce(t16[7][:], e8[2][:], axis=AX.X, op=ALU.add))
            L(V.reciprocal(t16[7][:], t16[7][:]))
            L(V.tensor_tensor(t16[8][:], t16[5][:], t16[7][:], ALU.mult))
            L(V.tensor_tensor(t16[9][:], t16[8][:], t16[7][:], ALU.add))
            L(V.reciprocal(t16[9][:], t16[9][:]))
            L(V.tensor_tensor(t16[9][:], t16[9][:], t16[2][:], ALU.mult))
            L(V.tensor_tensor(c.weight[:, 0], t16[7][:], t16[9][:], ALU.mult))
            L(V.tensor_tensor(c.weight[:, 1], t16[8][:], t16[9][:], ALU.mult))
            for k in range(2):
                L(V.tensor_tensor(big[k][:].rearrange("p t (g e) -> p t g e", g=NG),
                                  g4[2][:].unsqueeze(3).to_broadcast([P, NTILES, NG, NEG]),
                                  e8[3 + k][:].unsqueeze(2).to_broadcast([P, NTILES, NG, NEG]), ALU.mult))
            L(V.tensor_tensor(hot[:], big[0][:], big[1][:], ALU.add))
            L(V.memset(cum[:, 0], 0.0))
            for i in range(NTILES):
                L(V.tensor_tensor(cum[:, i + 1], cum[:, i], hot[:, i], ALU.add))
            dve.sem_inc(hot_ready, 1)
            dve.wait_ge(rank_ready, 1)
            L(V.tensor_copy(x32[0][:], pc[:, 0:NE]))
            c3 = cmp_[:].rearrange("p a b -> p (a b)")[:, 0:NE * 16].rearrange("p (e m) -> p e m", e=NE)
            L(V.tensor_tensor(c3, bc(x32[0][:], 16), blkrow[:].unsqueeze(1).to_broadcast([P, NE, 16]), ALU.is_gt))
            L(V.tensor_reduce(x32[1][:], c3, axis=AX.X, op=ALU.add))
            L(V.tensor_tensor_scan(x32[2][:], c.ones[:, 0:NE], x32[1][:], 0.0, ALU.mult, ALU.add))
            L(V.tensor_scalar(c.block_end[:], x32[2][:], 2.0, 1.0, ALU.mult, ALU.add))
            L(V.tensor_tensor(x32[3][:], x32[2][:], x32[1][:], ALU.subtract))
            L(V.tensor_scalar(x32[3][:], x32[3][:], float(P), None, ALU.mult))
            L(V.tensor_tensor(big[2][:], pr[:].rearrange("p (t e) -> p t e", e=NE),
                              x32[3][:].unsqueeze(1).to_broadcast([P, NTILES, NE]), ALU.add))
            for k in range(2):
                L(V.tensor_tensor(big[3][:], big[2][:], big[k][:], ALU.mult))
                L(V.tensor_reduce(destf[:, k * NTILES:(k + 1) * NTILES], big[3][:], axis=AX.X, op=ALU.add))
            L(V.tensor_copy(c.dest[:].rearrange("p k t -> p (k t)"), destf[:]))
            di = c.dest[:].rearrange("p k t -> p (k t)")
            L(V.tensor_scalar(blki[:], di, 7, None, ALU.arith_shift_right))
            L(V.tensor_scalar(rowi[:], di, P - 1, None, ALU.bitwise_and))
            L(V.tensor_copy(blkf[:], blki[:]))
            L(V.tensor_copy(rowf[:], rowi[:]))
            dve.sem_inc(row_ready, 1)
            for n in range(0, NA, 4):
                if n >= RING:
                    dve.wait_ge(onehot_used, (n - RING) // 4 + 1)
                at = n % RING
                V.tensor_tensor(at_row[:, at:at + 4], lane[:].unsqueeze(1).to_broadcast([P, 4, P]),
                                bc(rowf[:, n:n + 4], P), ALU.is_equal)
                for j in range(3):
                    i = (n + j) % NTILES
                    V.tensor_scalar(at_blk[:, at + j], blk[:], blkf[:, n + j:n + j + 1], token[:, i:i + 1],
                                    ALU.is_equal, ALU.mult).then_inc(onehot_ready, 1)
            L(V.tensor_tensor(cmp_[:], x32[2][:].unsqueeze(1).to_broadcast([P, TAB, NE]), bc(blk[:], NE), ALU.is_le))
            L(V.tensor_reduce(etab[:], cmp_[:], axis=AX.X, op=ALU.add))
            L(V.tensor_scalar(etab[:], etab[:], float(NE - 1), None, ALU.min))
            L(V.scalar_tensor_tensor(out=c.expert_pair[:, 0:TAB - 1], in0=etab[:, 0:TAB - 1], scalar=float(NE), in1=etab[:, 1:TAB],
                                     op0=ALU.mult, op1=ALU.add))
            L(V.tensor_scalar(x32[0][:, 0:1], x32[2][:, NE - 1:NE], 1.0, None, ALU.add))
            L(V.tensor_copy(c.pairs[:], x32[0][:, 0:1]))
            L(V.tensor_scalar(c.pairs[:], c.pairs[:], 1, None, ALU.arith_shift_right))
            dve.wait_ge(onehot_used, NA // 4)
            L(V.tensor_copy(c.block_token[:], pi[:, 0:TAB]))


def load_expert(eng, ap, c, e, s):
    w = lambda name: ap[name][0][bass.ds(e, 1)].rearrange("a (k p) n -> p (a k) n", p=P)
    eng.dma_start(c.wgu[:, s, :, 0:FE], w("w_gate")).then_inc(c.w_in[s], 16)
    eng.dma_start(c.wgu[:, s, :, FE:2 * FE], w("w_up")).then_inc(c.w_in[s], 16)
    eng.dma_start(c.wd[:, s], w("w_down")).then_inc(c.w_in[s], 16)


def expert_phase(nc, ap, c):
    with ExitStack() as ctx:
        sb = lambda n, s, d=F32: ctx.enter_context(nc.sbuf_tensor(n, s, d))
        sem = lambda n: ctx.enter_context(nc.semaphore(n))
        psum = lambda n: ctx.enter_context(nc.psum_tensor(n, [P, 512], F32))
        xg = sb("xg", [P, 2, D])
        xT = sb("xTe", [P, KD, P])
        sg, hh = sb("sg", [P, FE]), sb("hh", [P, FE])
        hT = sb("hTe", [P, FE // P, P])
        yb = sb("yb", [P, 2, D])
        diag = sb("diag2", [P, KD, P])
        rows = sb("rows", [P, 2], I32)
        diag_ready, row_done = sem("diag2_ready"), sem("row2_done")
        pt = [psum("pt0"), psum("pt1")]
        pgate, pup, ph = psum("pgate"), psum("pup"), psum("ph")
        py = [psum("py0"), psum("py1")]
        experts_loaded = sem("experts_loaded")
        row_copied, xg_in = sem("row_copied"), [sem("xg_in0"), sem("xg_in1")]
        x_turned, xT_act, xT_dve = sem("x_turned"), sem("xT_act"), sem("xT_dve")
        gate_ready, up_ready, silu_ready, hh_ready = sem("gate_ready"), sem("up_ready"), sem("silu_ready"), sem("hh_ready")
        h_turned, hT_ready, y_ready, y_act, y_dve = sem("h_turned"), sem("hT_e"), sem("y_e"), sem("y_act"), sem("y_dve")
        y_stored = [sem("y_stored0"), sem("y_stored1")]
        pool_passed, sp_passed = sem("pool_passed_e"), sem("sp_passed_e")
        block = ctx.enter_context(nc.Block())

        def load_pairs(eng):
            return eng.value_load(c.pairs[0:1, 0:1], min_val=1, max_val=NBLK // 2)

        @block.sync
        def _(sp):
            def announce(s, turn):
                sp.wait_ge(c.w_in[s], 48 * turn)
                sp.sem_inc(experts_loaded, 1)

            def load_x1(n):
                sp.dma_start(c.x1_all[:, bass.ds(2 * n, 2)], ap["x1"][bass.ds(2 * n * P, 2 * P), :]
                             .rearrange("(t p) n -> p t n", p=P)).then_inc(c.x1_in, 16)

            for s in range(WSLOTS - 1):
                announce(s, 1)
            with sp.Fori(1, NE // WSLOTS) as g:
                for s in range(WSLOTS):
                    last = sp.value_load(c.block_end[0:1, bass.ds((g - 1) * WSLOTS + s, 1)], min_val=1, max_val=2 * NBLK + 1)
                    wait_apart(sp, y_ready, last, sp_passed)
                    load_expert(sp, ap, c, g * WSLOTS + s, s)
                    if s == 0:
                        announce(WSLOTS - 1, g)
                        load_x1(g - 1)
                    else:
                        announce(s - 1, g + 1)
            announce(WSLOTS - 1, NE // WSLOTS)
            load_x1(NE // WSLOTS - 1)

        @block.gpsimd
        def _(pool):
            def fetch(b, s, n):
                nc.gpsimd.tensor_copy(rows[:, s:s + 1], c.block_token[:, bass.ds(b, 1)]).then_inc(row_copied, 1)
                wait_apart(pool, row_copied, n, pool_passed)
                pool.indirect_dma_start(xg[:, s], None, ap["xn"], bass.IndirectOffsetOnAxis(rows[:, s:s + 1], 0)).then_inc(xg_in[s], 16)

            fetch(0, 0, 1)
            fetch(1, 1, 2)
            n_pairs = load_pairs(pool)
            with pool.Fori(0, n_pairs) as q:
                for s in range(2):
                    b = 2 * q + s
                    wait_apart(pool, x_turned, 2 * b + 2, pool_passed)
                    fetch(b + 2, s, b + 3)
                    pool.wait_ge(y_act, b + 1)
                    wait_apart(pool, y_dve, b + 1, pool_passed)
                    pool.dma_start(ap["y"][bass.ds(b * P, P), :], yb[:, s]).then_inc(y_stored[s], 16)
            for s in range(2):
                wait_apart(pool, y_stored[s], n_pairs * 16, pool_passed)
                wait_apart(pool, xg_in[s], n_pairs * 16 + 16, pool_passed)

        @block.tensor
        def _(pe):
            def turn_half(half, s):
                for j in range(4):
                    k = 4 * half + j
                    last = nc.tensor.transpose(pt[half][:, j * P:(j + 1) * P], xg[:, s, k * P:(k + 1) * P], c.ident[:])
                last.then_inc(x_turned, 1)

            def turn(s, times):
                pe.wait_ge(xg_in[s], 16 * times)
                turn_half(0, s)
                turn_half(1, s)

            def experts_of(b):
                both = pe.value_load(c.expert_pair[0:1, bass.ds(b, 1)], min_val=0, max_val=NE * NE - 1)
                return both // NE, both % NE

            def hidden_products(b, expert):
                pe.wait_ge(experts_loaded, expert + 1)
                pe.wait_ge(xT_act, b + 1)
                pe.wait_ge(xT_dve, b + 1)
                for out, cols, done in ((pgate, 0, gate_ready), (pup, FE, up_ready)):
                    for k in range(KD):
                        last = nc.tensor.matmul(out[:, 0:FE], xT[:, k, :],
                                                c.wgu[:, bass.ds(expert % WSLOTS, 1), k, cols:cols + FE].rearrange("p a n -> p (a n)"),
                                                start=(k == 0), stop=(k == KD - 1))
                    last.then_inc(done, 1)

            def down_products(b, expert):
                pe.wait_ge(hT_ready, b + 1)
                wait(pe, y_act, b)
                wait(pe, y_dve, b)
                for half in range(2):
                    for k in range(FE // P):
                        last = nc.tensor.matmul(py[half][:], hT[:, k, :],
                                                c.wd[:, bass.ds(expert % WSLOTS, 1), k, half * 512:(half + 1) * 512].rearrange("p a n -> p (a n)"),
                                                start=(k == 0), stop=(k == FE // P - 1))
                    last.then_inc(y_ready, 1)

            def finish(b, s, times):
                pe.wait_ge(xg_in[1 - s], 16 * times)
                turn_half(0, 1 - s)
                pe.wait_ge(hh_ready, b + 1)
                for k in range(FE // P):
                    last = nc.tensor.transpose(ph[:, k * P:(k + 1) * P], hh[:, k * P:(k + 1) * P], c.ident[:])
                last.then_inc(h_turned, 1)
                turn_half(1, 1 - s)
                expert, next_expert = experts_of(b)
                down_products(b, expert)
                hidden_products(b + 1, next_expert)

            pe.wait_ge(diag_ready, 1)
            for r in range(2):
                last = nc.tensor.matmul(py[r][:], c.ones[:], diag[:, 4 * r:4 * r + 4].rearrange("p a b -> p (a b)"), start=True, stop=True)
            last.then_inc(row_done, 1)
            pe.sem_inc(y_ready, 1)
            turn(0, 1)
            hidden_products(0, experts_of(0)[0])
            with pe.Fori(0, load_pairs(pe)) as q:
                for s in range(2):
                    finish(2 * q + s, s, q + 1 + s)

        @block.scalar
        def _(act):
            A = nc.scalar.activation

            def evacuate(b):
                act.wait_ge(x_turned, 2 * b + 1)
                wait(act, up_ready, b)
                for k in range(4):
                    last = A(xT[:, k, :], pt[0][:, k * P:(k + 1) * P], ACT.Identity, scale=c.scale2[:, k:k + 1], bias=c.shift2[:, k:k + 1])
                last.then_inc(xT_act, 1)

            evacuate(0)
            with act.Fori(0, load_pairs(act)) as q:
                for s in range(2):
                    b = 2 * q + s
                    act.wait_ge(gate_ready, b + 1)
                    act.wait_ge(hh_ready, b)
                    A(sg[:], pgate[:, 0:FE], ACT.Silu).then_inc(silu_ready, 1)
                    evacuate(b + 1)
                    act.wait_ge(y_ready, 2 * b + 2)
                    act.wait_ge(y_stored[s], q * 16)
                    A(yb[:, s, 0:512], py[0][:], ACT.Copy).then_inc(y_act, 1)

        @block.vector
        def _(dve):
            V = nc.vector

            def evacuate(b):
                dve.wait_ge(x_turned, 2 * b + 2)
                wait(dve, up_ready, b)
                for j in range(4):
                    k = 4 + j
                    last = V.tensor_scalar(xT[:, k, :], pt[1][:, j * P:(j + 1) * P], c.scale2[:, k:k + 1], c.shift2[:, k:k + 1], ALU.mult, ALU.add)
                last.then_inc(xT_dve, 1)

            for k in range(KD):
                last = V.tensor_scalar(diag[:, k], c.ident[:], c.gcol[:, KD + k:KD + k + 1], None, ALU.mult)
            last.then_inc(diag_ready, 1)
            dve.wait_ge(row_done, 1)
            for r in range(2):
                V.tensor_copy(c.grow2[:, r * 512:(r + 1) * 512], py[r][:])
            evacuate(0)
            with dve.Fori(0, load_pairs(dve)) as q:
                for s in range(2):
                    b = 2 * q + s
                    dve.wait_ge(silu_ready, b + 1)
                    dve.wait_ge(up_ready, b + 1)
                    dve.wait_ge(h_turned, b)
                    V.tensor_tensor(hh[:], pup[:, 0:FE], sg[:], ALU.mult).then_inc(hh_ready, 1)
                    dve.wait_ge(h_turned, b + 1)
                    dve.wait_ge(y_ready, 2 * b + 1)
                    V.tensor_copy(hT[:].rearrange("p a b -> p (a b)"), ph[:, 0:FE]).then_inc(hT_ready, 1)
                    evacuate(b + 1)
                    dve.wait_ge(y_ready, 2 * b + 3)
                    dve.wait_ge(y_stored[s], q * 16)
                    V.tensor_copy(yb[:, s, 512:D], py[1][:]).then_inc(y_dve, 1)


def combine_phase(nc, ap, c, out):
    with ExitStack() as ctx:
        sb = lambda n, s, d=F32: ctx.enter_context(nc.sbuf_tensor(n, s, d))
        sem = c.sem
        RING = 4
        ya, yb = sb("ya", [P, RING, D]), sb("yb2", [P, RING, D])
        junk = sb("junk", [P, D])
        rows = sb("rows2", [P, 2 * RING], I32)
        ss = sb("ss", [P, RING])
        row_copied = sem("row2_copied")
        ya_in, yb_in = [sem(f"ya_in{s}") for s in range(RING)], [sem(f"yb_in{s}") for s in range(RING)]
        out_stored = sem("out_stored")
        scaled, y_sum, act_step, rstd_ready, gated, out_ready = (
            sem("scaled"), sem("y_sum"), sem("act_step2"), sem("rstd_ready"), sem("gated"), sem("out_ready"))
        pool_passed, sp_passed = sem("pool_passed2"), sem("sp_passed2")
        block = ctx.enter_context(nc.Block())
        ROUNDS = NTILES // RING
        tile_of = lambda q, s: q * RING + s

        @block.gpsimd
        def _(pool):
            def fetch(q, s):
                i = tile_of(q, s)
                for k, (buf, done) in enumerate(((ya, ya_in), (yb, yb_in))):
                    at = 2 * s + k
                    nc.gpsimd.tensor_copy(rows[:, at:at + 1], c.dest[:, k, bass.ds(i, 1)]).then_inc(row_copied, 1)
                    wait_apart(pool, row_copied, 2 * i + k + 1, pool_passed)
                    pool.indirect_dma_start(buf[:, s], None, ap["y"], bass.IndirectOffsetOnAxis(rows[:, at:at + 1], 0)).then_inc(done[s], 16)

            for s in range(RING):
                fetch(0, s)
            with pool.Fori(1, ROUNDS) as q:
                for s in range(RING):
                    wait_apart(pool, out_ready, tile_of(q, s) - RING + 1, pool_passed)
                    fetch(q, s)

        @block.scalar
        def _(act):
            A = nc.scalar.activation

            def scale(q, s):
                act.wait_ge(ya_in[s], 16 * q + 16)
                A(ya[:, s], ya[:, s], ACT.Copy, scale=c.weight[:, 0, bass.ds(tile_of(q, s), 1)]).then_inc(scaled, 1)

            def rstd(q, s):
                i = tile_of(q, s)
                act.wait_ge(y_sum, i + 1)
                A(junk[:], ya[:, s], ACT.Square, accum_out=ss[:, s:s + 1]).then_inc(act_step, 1)
                act.wait_ge(act_step, 2 * i + 1)
                A(ss[:, s:s + 1], ss[:, s:s + 1], ACT.Ln, bias=c.epsc[:], scale=1.0 / D).then_inc(act_step, 1)
                act.wait_ge(act_step, 2 * i + 2)
                A(ss[:, s:s + 1], ss[:, s:s + 1], ACT.Exp, scale=-0.5).then_inc(rstd_ready, 1)

            act.preload_act_table_set("natural_log_exp_and_others")
            scale(0, 0)
            with act.Fori(0, ROUNDS - 1) as q:
                for s in range(RING):
                    scale(q + (s + 1) // RING, (s + 1) % RING)
                    rstd(q, s)
            for s in range(RING):
                if s < RING - 1:
                    scale(ROUNDS - 1, s + 1)
                rstd(ROUNDS - 1, s)

        @block.vector
        def _(dve):
            V = nc.vector

            def weigh(q, s):
                i = tile_of(q, s)
                dve.wait_ge(scaled, i + 1)
                dve.wait_ge(yb_in[s], 16 * q + 16)
                V.scalar_tensor_tensor(out=ya[:, s], in0=yb[:, s], scalar=c.weight[:, 1, bass.ds(i, 1)], in1=ya[:, s],
                                       op0=ALU.mult, op1=ALU.add).then_inc(y_sum, 1)

            def finish(q, s):
                i = tile_of(q, s)
                dve.wait_ge(rstd_ready, i + 1)
                V.scalar_tensor_tensor(out=ya[:, s], in0=ya[:, s], scalar=ss[:, s:s + 1], in1=c.grow2[:],
                                       op0=ALU.mult, op1=ALU.mult).then_inc(gated, 1)
                dve.wait_ge(gated, i + 1)
                x1 = c.x1_all[:, bass.ds(i, 1)].rearrange("p a n -> p (a n)")
                V.tensor_tensor(x1, x1, ya[:, s], ALU.add).then_inc(out_ready, 1)

            dve.wait_ge(c.x1_in, NTILES // 2 * 16)
            weigh(0, 0)
            with dve.Fori(0, ROUNDS - 1) as q:
                for s in range(RING):
                    weigh(q + (s + 1) // RING, (s + 1) % RING)
                    finish(q, s)
            for s in range(RING):
                if s < RING - 1:
                    weigh(ROUNDS - 1, s + 1)
                finish(ROUNDS - 1, s)

        @block.sync
        def _(sp):
            with sp.Fori(0, NTILES) as i:
                wait_apart(sp, out_ready, i + 1, sp_passed)
                sp.dma_start(out[bass.ds(i * P, P), :], c.x1_all[:, bass.ds(i, 1)].rearrange("p a n -> p (a n)")).then_inc(out_stored, 16)
            sp.wait_ge(out_stored, NTILES * 16)


INPUTS = ["x", "c", "w_ada", "b_ada", "g_pre_mix", "g_post_mix", "w_in", "dw_kernel", "dw_bias",
          "conv_ln_gain", "conv_ln_bias", "lb_logits", "rec_norm_gain", "w_out", "g_pre_ffn", "g_post_ffn",
          "w_router_group", "b_router_group", "w_router_expert", "b_router_expert", "w_gate", "w_up", "w_down"]


class Kept:
    pass


def build(nc, ap, out):
    c = Kept()
    with ExitStack() as ctx:
        sb = lambda n, s, d=F32: ctx.enter_context(nc.sbuf_tensor(n, s, d))
        c.ident, c.ones, c.causal = (sb(n, [P, P]) for n in ("ident", "ones", "causal"))
        c.cols = sb("cols", [P, NVEC])
        c.epsc = sb("epsc", [P, 1])
        c.scale1, c.shift1, c.scale2, c.shift2 = (sb(n, [P, KD]) for n in ("scale1", "shift1", "scale2", "shift2"))
        c.gcol = sb("gcol", [P, 2 * KD])
        c.logits = sb("logits", [P, NTILES, NR])
        ap["x1"] = nc.dram_tensor("x1_dram", (SEQ, D), F32, kind=DEBUG_KIND).ap()
        ap["xn"] = nc.dram_tensor("xn_dram", (SEQ, D), F32, kind=DEBUG_KIND).ap()
        ap["y"] = nc.dram_tensor("y_dram", (NBLK * P, D), F32, kind="Internal").ap()
        with ExitStack() as mix:
            mb = lambda n, s, d=F32: mix.enter_context(nc.sbuf_tensor(n, s, d))
            c.restart = mb("restart", [P, T])
            c.zeros = mb("zeros", [P, P])
            c.wroute = mb("wroute", [P, KD, NR])
            c.brow = mb("brow", [1, NR])
            c.taps = mb("taps", [P, NCH * CW])
            c.lb, c.oneless = mb("lb", [P, NCH]), mb("oneless", [P, NCH])
            c.grow = mb("grow", [P, D])
            c.state = mb("state", [P, 4, DC])
            c.scoreT = mb("scoreT", [P, 2, DC])
            mixer_phase(nc, ap, c)
        c.weight = sb("weight", [P, 2, NTILES])
        c.dest = sb("dest", [P, 2, NTILES], I32)
        c.block_token = sb("block_token", [P, TAB], I32)
        c.expert_pair = sb("expert_pair", [P, TAB], I32)
        c.block_end, c.pairs = sb("block_end", [P, NE], I32), sb("pairs", [P, 1], I32)
        c.sem = lambda n: ctx.enter_context(nc.semaphore(n))
        c.wgu = sb("wgu", [P, WSLOTS, KD, 2 * FE])
        c.wd = sb("wd", [P, WSLOTS, FE // P, D])
        c.w_in = [ctx.enter_context(nc.semaphore(f"w_in{i}")) for i in range(WSLOTS)]
        c.x1_all, c.grow2 = sb("x1_all", [P, NTILES, D]), sb("grow2", [P, D])
        c.x1_in = ctx.enter_context(nc.semaphore("x1_in"))
        routing_phase(nc, ap, c)
        expert_phase(nc, ap, c)
        combine_phase(nc, ap, c, out[0])


DEBUG_KIND = "Internal"


def kernel(**inputs):
    import numpy as np
    import concourse.bacc as bacc
    from concourse.bass_utils import run_bass_kernel_spmd

    nc = bacc.Bacc("TRN2", target_bir_lowering=False, num_devices=1)
    arrays, ap = {}, {}
    for name in INPUTS:
        a = np.ascontiguousarray(inputs[name])
        arrays[f"{name}_in"] = a
        ap[name] = nc.dram_tensor(f"{name}_in", a.shape, mybir.dt.from_np(a.dtype), kind="ExternalInput").ap()
    out = nc.dram_tensor("out", (1, SEQ, D), F32, kind="ExternalOutput").ap()
    build(nc, ap, out)
    r = run_bass_kernel_spmd(nc, [arrays], core_ids=[0])
    return r.results[0]["out"]
```

```python
import concourse.bass as bass
from concourse import mybir
from contextlib import ExitStack

F32 = mybir.dt.float32
F32R = mybir.dt.float32r
I32 = mybir.dt.int32
U32 = mybir.dt.uint32
BF16 = mybir.dt.bfloat16
ALU = mybir.AluOpType
ACT = mybir.ActivationFunctionType
AX = mybir.AxisListType

P = 128
D = 1024
KD = D // P
SEQ = 2048
DC = 512
NCH = DC // P
NH = 4
CW = 31
HALO = CW - 1
T = 512
NB = SEQ // T
NT = T // P
CH = 64
NTILES = SEQ // P
NG, NEG = 4, 8
NE = NG * NEG
FE = 256
NR = NG + NE
EPS = 1e-6
NBLK = 64
MINBLK = 2 * SEQ // P
WSLOTS = 4
TAB = NBLK + 2

VEC = {}
_at = 0
for _name, _n in (("c", 8), ("b_ada", 48), ("g_pre_mix", 8), ("g_post_mix", 8), ("g_pre_ffn", 8),
                  ("g_post_ffn", 8), ("dw_bias", 4), ("conv_ln_gain", 4), ("conv_ln_bias", 4),
                  ("lb_logits", 8), ("rec_norm_gain", 1)):
    VEC[_name] = (_at, _at + _n)
    _at += _n
NVEC = _at


def wait(eng, sem, value):
    if isinstance(value, int) and value <= 0:
        return
    eng.wait_ge(sem, value)


def wait_apart(eng, sem, value, passed):
    eng.wait_ge(sem, value)
    eng.sem_inc(passed, 1)


class Chain:

    def __init__(self, eng, sem, base=0):
        self.eng, self.sem, self.base, self.n = eng, sem, base, 0

    def step(self, ins):
        ins.then_inc(self.sem, 1)
        self.n += 1

    def sync(self):
        wait(self.eng, self.sem, self.base + self.n)

    def link(self, ins):
        self.step(ins)
        self.sync()


def mixer_phase(nc, ap, c):
    with ExitStack() as ctx:
        sb = lambda n, s, d=F32: ctx.enter_context(nc.sbuf_tensor(n, s, d))
        sem = lambda n: ctx.enter_context(nc.semaphore(n))
        col = lambda n, k: c.cols[:, VEC[n][0] + k:VEC[n][0] + k + 1]

        def overlaid(name, shape):
            with nc.sbuf_tensor(name, shape, F32) as values:
                pass
            return values, sb(name + "_operand", shape, F32R)

        hT_high = sb("hT_high", [P, KD, T], F32R)
        hT, hT_rest = overlaid("hT", [P, KD, T])
        NSLOT = 3
        win, win_rest = overlaid("win", [P, NSLOT, 2 * D])
        tiles, win_high = overlaid("tiles", [P, 2, 2 * D])
        piece_view = lambda w: w.rearrange("p (k n) -> p k n", k=KD)
        xt = win[:, 2].rearrange("p (a n) -> p a n", a=2)
        yt = tiles[:, 0].rearrange("p (a n) -> p a n", a=2)
        xres = tiles[:, 1].rearrange("p (a n) -> p a n", a=2)
        wo = sb("wo", [P, KD, D])
        u_all = sb("u", [P, NCH * (HALO + T)])
        u = u_all[:].rearrange("p (k n) -> p k n", k=NCH)
        gs = u_all[:, 0:NT * DC].rearrange("p (i n) -> p i n", i=NT)
        halo = sb("halo", [P, NCH, HALO])
        cv = sb("cv", [P, NCH, T])
        yT = sb("yT", [P, KD, T])
        heads_buf = sb("heads_buf", [P, 4, NH * T])
        by_head = lambda m: heads_buf[:, m].rearrange("p (h n) -> p h n", h=NH)
        qd, ki, ke = by_head(0), by_head(1), by_head(2)
        v = heads_buf[:, 3].rearrange("p (i n) -> p i n", i=NT)
        ob = sb("ob", [P, NT, DC])
        scr = sb("scr", [P, D])
        tmp = sb("tmp", [P, 512])
        decay = sb("decay", [P, NH, T // CH])
        sums = sb("sums", [P, 48])
        early = c.logits[:].rearrange("p t n -> p (t n)")
        cond, mod, lbt = early[:, 0:KD], early[:, KD:7 * KD], early[:, 7 * KD:7 * KD + 4 * NCH].rearrange("p (a n) -> p a n", a=4)
        bank = [ctx.enter_context(nc.psum_tensor(f"bank{i}", [P, 512], F32)) for i in range(4)]
        pS = ctx.enter_context(nc.psum_tensor("pS", [P, 512], F32))
        pO = ctx.enter_context(nc.psum_tensor("pO", [P, 512], F32))
        pD = ctx.enter_context(nc.psum_tensor("pD", [P, 512], F32))
        pT = ctx.enter_context(nc.psum_tensor("pT", [P, 512], F32))

        vec_in, mask_step, turned, cols_ready, cond_ready = (
            sem(n) for n in ("vec_in", "mask_step", "turned", "cols_ready", "cond_ready"))
        lb_in = sem("lb_in")
        ada_in = [sem(f"ada_in{i}") for i in range(4)] + [sem(f"ada_late_in{i}") for i in range(2)]
        route_in, act_passed = sem("route_in"), sem("act_passed")
        ada_used, ada_cols_done, scale1_ready, mod_ready = (
            sem(n) for n in ("ada_used", "ada_cols_done", "scale1_ready", "mod_ready"))
        mod_step, diag_ready, row_done = (
            sem(n) for n in ("mod_step", "diag_ready", "row_done"))
        x_in = [sem("x_in0"), sem("x_in1")]
        win_in = [sem(f"win_in{i}") for i in range(NSLOT)]
        wo_in = sem("wo_in")
        res_in = [sem("res_in0"), sem("res_in1")]
        x_rstd, x_normed, xT_ready, hT_ready = sem("x_rstd"), sem("x_normed"), sem("xT_ready"), sem("hT_ready")
        hT_raw, hT_split, high_ready, rest_ready = (sem("hT_raw0"), sem("hT_raw1")), sem("hT_split"), sem("high_ready"), sem("rest_ready")
        proj_ready = sem("proj_ready")
        gate_sig, u_ready = sem("gate_sig"), sem("u_ready")
        q_parts, g_parts, v_ready = sem("q_parts"), sem("g_parts"), sem("v_ready")
        forget_ready, logf_ready, b_ready = sem("forget_ready"), sem("logf_ready"), sem("b_ready")
        exp_ready, exp_used = sem("exp_ready"), sem("exp_used")
        y_ready, y_rstd, x1_ready, x1_rstd, xn_ready = sem("y_ready"), sem("y_rstd"), sem("x1_ready"), sem("x1_rstd"), sem("xn_ready")
        y_cleared = sem("y_cleared")
        pool_passed, dve_passed, sp_passed = sem("pool_passed"), sem("dve_passed"), sem("sp_passed")
        rT_ready, rin_ready, logit_ready, logit_saved = sem("rT_ready"), sem("rin_ready"), sem("logit_ready"), sem("logit_saved")
        x1_stored, xn_stored = [sem("x1_stored0"), sem("x1_stored1")], [sem("xn_stored0"), sem("xn_stored1")]
        mean_ready, centred, squared, var_ready, ln_rstd, ln_normed, ln_sig, ln_out = (
            sem(n) for n in ("mean_ready", "centred", "squared", "var_ready", "ln_rstd", "ln_normed", "ln_sig", "ln_out"))
        score_ready, masked, keT_psum, keT_ready = sem("score_ready"), sem("masked"), sem("keT_psum"), sem("keT_ready")
        dstate_ready, state_ready, o_ready, o_saved = sem("dstate_ready"), sem("state_ready"), sem("o_ready"), sem("o_saved")
        o_squared, o_ms, o_rstd, o_gated = sem("o_squared"), sem("o_ms"), sem("o_rstd"), sem("o_gated")
        oT_psum, yT_rec, yT_conv = sem("oT_psum"), sem("yT_rec"), sem("yT_conv")
        a_norm, a_out, a_ln = (sem(n) for n in ("a_norm", "a_out", "a_ln"))
        conv_step, v_head, y_normed, v_rec, v_ln, g_done, diff_ready = (
            sem(n) for n in ("conv_step", "v_head", "y_normed", "v_rec", "v_ln", "g_done", "diff_ready"))
        CLEARS = (3, 3, 2, 0)
        assert sum(CLEARS) * NB == NBLK - MINBLK
        CONV_STEPS, MASK_STEPS = NCH * CW + 2 * NCH, 10
        block = ctx.enter_context(nc.Block())

        x_d, x1_d, xn_d = ap["x"][0], ap["x1"], ap["xn"]
        w_d = ap["w_in"][0].rearrange("(k p) n -> p k n", p=P)
        NPIECE = 12
        GATE, Q, FG, VI, GG = DC, 2 * DC, 3 * DC, 4 * DC, 5 * DC
        PIECES = [((j * P, P), (GATE + j * P, P)) for j in range(NCH)]
        PIECES += [((Q + j * P, P), (FG + j * P, P)) for j in range(NH)]
        PIECES += [((VI + j * 256, 256),) for j in range(2)] + [((GG + j * 256, 256),) for j in range(2)]
        AU = 2 * NPIECE

        MODS, ADA_PIECES = 6, 12
        ada_slot = [wo[:, 0:4], wo[:, 4:8]] + [heads_buf[:, 2 * i:2 * i + 2].rearrange("p a (b n) -> p (a b) n", n=D) for i in range(2)]
        slot_of = lambda p: p if p < 4 else p % 2
        ada_load = lambda p: (ada_in[p], 16) if p < 4 else (ada_in[4 + p % 2], 16 * (p // 2 - 1))
        ada_acc = [yT[:, 2 * (m % 4):2 * (m % 4) + 2].rearrange("p a n -> p (a n)") for m in range(MODS)]
        diag = [yT[:, 4], yT[:, 5]]

        def load_ada(eng, p):
            m, half = p // 2, p % 2
            eng.dma_start(ada_slot[slot_of(p)], ap["w_ada"][0, half * 512:(half + 1) * 512, m * D:(m + 1) * D]
                          .rearrange("(k p) n -> p k n", p=P)).then_inc(ada_load(p)[0], 16)

        def load_vectors(eng, part):
            if part == 0:
                eng.dma_start(scr[0:CW, 0:DC], ap["dw_kernel"][0]).then_inc(vec_in, 16)
            for name in list(VEC)[part::2]:
                a, b = VEC[name]
                eng.dma_start(tmp[a:b, 0:P], ap[name].rearrange("a (k p) -> (a k) p", p=P)).then_inc(vec_in, 16)

        def win_bytes(t, j):
            per_block = sum(16 * len(PIECES[i]) for i in range(NPIECE) if i % NSLOT == j % NSLOT)
            return t * per_block + sum(16 * len(PIECES[i]) for i in range(j + 1) if i % NSLOT == j % NSLOT)

        STEPS = [("y", 0, 0), ("mean",), ("y", 0, 1), ("y", 1, 0), ("var",), ("A", 0), ("y", 1, 1), ("B", 0), ("r", 0), ("O", 0),
                 ("A", 1), ("B", 1), ("l", 0), ("O", 1),
                 ("A", 2), ("y", 2, 0), ("B", 2), ("r", 1), ("O", 2),
                 ("A", 3), ("y", 2, 1), ("B", 3), ("l", 1), ("O", 3),
                 ("y", 3, 0), ("y", 3, 1), ("r", 2), ("T", 0), ("T", 1), ("l", 2), ("oT", 0), ("oT", 1),
                 ("r", 3), ("oT", 2), ("oT", 3), ("l", 3), ("T", 2), ("T", 3)]
        USES = {"y": 1, "r": 2, "l": 1, "T": 2}

        TAIL = [("y", 0, 0), ("y", 0, 1), ("y", 1, 0), ("y", 1, 1), ("r", 0), ("y", 2, 0), ("y", 2, 1), ("l", 0), ("r", 1),
                ("y", 3, 0), ("y", 3, 1), ("l", 1), ("r", 2), ("l", 2), ("r", 3), ("l", 3)]
        tail_bank = [pS, pO, pD, pT] + bank

        def stage_units(kinds, steps=STEPS):
            return [(s[0], s[1], s[2] if s[0] == "y" else h) for s in steps if s[0] in kinds for h in range(USES.get(s[0], 0))]

        def stage_banks(mix, out, nxt):
            units = stage_units(kinds_of(out, nxt), STEPS if mix else TAIL)
            return {unit: bank[n % 4] if mix else tail_bank[n % 8] for n, unit in enumerate(units)}

        def reader(kind, i, half, t):
            if kind == "T":
                return hT_raw[half], t * NT + i + 1
            if kind == "y":
                return y_normed, t * 2 * NT + 2 * i + half + 1
            if kind == "r":
                return rin_ready, t * 2 * NT + 2 * i + half + 1
            if kind == "l":
                return logit_saved, t * NT + i + 1
            n = i
            if n < 8:
                return u_ready, t * NCH + n // 2 + 1
            if n < 16:
                return q_parts, (t * NH + (n - 8) // 2) * 3 + 2 + n % 2
            if n < 20:
                return v_ready, t * 4 + (n - 16) + 1
            return g_parts, t * 4 + (n - 20) + 1

        def kinds_of(out, nxt):
            return ("y", "r", "l") * out + ("T",) * nxt

        @block.sync
        def _(sp):
            def load_x(t, i):
                wait(sp, xT_ready, t * 2 * NT + 2 * (i - 2) + 2)
                sp.sem_inc(sp_passed, 1)
                sp.dma_start(xt[:, i % 2], x_d[bass.ds(t * T + i * P, P), :]).then_inc(x_in[i % 2], 16)

            def load_piece(t, j):
                wait(sp, proj_ready, t * AU + 2 * (j - NSLOT) + 2)
                sp.sem_inc(sp_passed, 1)
                at = 0
                for a, n in PIECES[j]:
                    sp.dma_start(piece_view(win[:, j % NSLOT])[:, :, at:at + n], w_d[:, :, a:a + n]).then_inc(win_in[j % NSLOT], 16)
                    at += n

            def load_next(t):
                wait(sp, proj_ready, t * AU)
                for i in range(2):
                    load_x(t, i)
                for j in range(2):
                    load_piece(t, j)
                for i in range(2, NT):
                    load_x(t, i)
                sp.wait_ge(xT_ready, (t + 1) * 2 * NT)
                load_piece(t, 2)

            load_vectors(sp, 0)
            for i in range(2):
                load_x(0, i)
            for p in range(4):
                load_ada(sp, p)
            for j in range(2):
                load_piece(0, j)
            for i in range(2, NT):
                load_x(0, i)
            sp.wait_ge(xT_ready, 2 * NT)
            load_piece(0, 2)
            with sp.Fori(0, NB - 1) as t:
                for j in range(NSLOT, NPIECE):
                    load_piece(t, j)
                load_next(t + 1)
            for j in range(NSLOT, NPIECE):
                load_piece(NB - 1, j)

        @block.gpsimd
        def _(pool):
            def load_residual(t, i):
                pool.dma_start(xres[:, i % 2], x_d[bass.ds(t * T + i * P, P), :]).then_inc(res_in[i % 2], 16)

            def store(t, projected):
                wait_apart(pool, proj_ready, projected * AU, pool_passed)
                if isinstance(t, int):
                    pool.wait_ge(rT_ready, t * 2 * NT)
                    for s in xn_stored:
                        pool.wait_ge(s, t * 32)
                for i in range(2):
                    load_residual(t, i)
                for i in range(NT):
                    rows = bass.ds(t * T + i * P, P)
                    wait_apart(pool, x1_ready, t * NT + i + 1, pool_passed)
                    pool.dma_start(x1_d[rows, :], yt[:, i % 2]).then_inc(x1_stored[i % 2], 16)
                    wait_apart(pool, xn_ready, t * NT + i + 1, pool_passed)
                    pool.dma_start(xn_d[rows, :], xres[:, i % 2]).then_inc(xn_stored[i % 2], 16)
                    for m in range(sum(CLEARS[:i]), sum(CLEARS[:i + 1])):
                        b = MINBLK + t * sum(CLEARS) + m
                        pool.dma_start(ap["y"][bass.ds(b * P, P), :].rearrange("p (a n) -> p a n", n=64),
                                       c.zeros[:].unsqueeze(1).to_broadcast([P, D // 64, 64])).then_inc(y_cleared, 16)
                    if i < 2:
                        wait_apart(pool, rT_ready, t * 2 * NT + 2 * i + 2, pool_passed)
                        wait_apart(pool, xn_stored[i % 2], t * 32 + 16, pool_passed)
                        load_residual(t, i + 2)

            ch = Chain(pool, mask_step)
            ch.step(nc.gpsimd.memset(c.ident[:], 0.0))
            ch.step(nc.gpsimd.memset(c.ones[:], 1.0))
            ch.step(nc.gpsimd.memset(c.causal[:], 1.0))
            ch.step(nc.gpsimd.memset(c.restart[:], 1.0))
            ch.step(nc.gpsimd.memset(c.epsc[:], EPS))
            ch.sync()
            ch.step(nc.gpsimd.affine_select(out=c.ident[:], in_=c.ident[:], compare_op=ALU.not_equal, fill=1.0,
                                            base=0, pattern=[[-1, P]], channel_multiplier=1))
            ch.step(nc.gpsimd.affine_select(out=c.causal[:], in_=c.causal[:], compare_op=ALU.is_ge, fill=0.0,
                                            base=0, pattern=[[1, P]], channel_multiplier=-1))
            ch.sync()
            ch.step(nc.gpsimd.memset(c.causal[0:CH, CH:P], 0.0))
            ch.step(nc.gpsimd.memset(c.restart[:].rearrange("p (n k) -> p n k", k=CH)[:, :, 0:1], 0.0))
            ch.step(nc.gpsimd.memset(c.zeros[:], 0.0))
            ch.sync()
            assert ch.n == MASK_STEPS
            pool.dma_start(c.wroute[:, :, 0:NG], ap["w_router_group"][0].rearrange("(k p) n -> p k n", p=P),
                           allow_slow_non_contiguous=True).then_inc(route_in, 16)
            pool.dma_start(c.wroute[:, :, NG:NR],
                           ap["w_router_expert"][0].rearrange("(k p) n -> p k n", p=P)).then_inc(route_in, 16)
            pool.dma_start(c.brow[0:1, 0:NG], ap["b_router_group"]).then_inc(route_in, 16)
            pool.dma_start(c.brow[0:1, NG:NR], ap["b_router_expert"]).then_inc(route_in, 16)
            for p in range(4, ADA_PIECES):
                pool.wait_ge(ada_used, p - 3 if p < 6 else p - 1)
                load_ada(pool, p)
            pool.wait_ge(ada_used, ADA_PIECES)
            pool.dma_start(wo[:], ap["w_out"][0].rearrange("(k p) n -> p k n", p=P)).then_inc(wo_in, 16)
            with pool.Fori(0, NB - 1) as t:
                store(t, t + 2)
            store(NB - 1, NB)
            pool.wait_ge(y_cleared, (NBLK - MINBLK) * 16)
            for s in x1_stored + xn_stored:
                pool.wait_ge(s, NB * 32)

        @block.tensor
        def _(pe):
            def ring(units, before, banks=bank):
                size = len(banks)
                for n in range(len(units)):
                    if n >= size:
                        wait(pe, *reader(*units[n - size]))
                    elif before and n >= size - 4:
                        wait(pe, *reader(*before[n - size + 4]))
                    yield banks[n % size]

            def turn_in(t, i, banks):
                pe.wait_ge(x_normed, t * NT + i + 1)
                for half in range(2):
                    out = next(banks)
                    for j in range(4):
                        k = half * 4 + j
                        last = nc.tensor.transpose(out[:, j * P:(j + 1) * P], xt[:, i % 2, k * P:(k + 1) * P], c.ident[:])
                    last.then_inc(xT_ready, 1)

            def ada_columns(m):
                out = pT if m < 4 else bank[3]
                pe.wait_ge(ada_used, 2 * m + 2)
                for j in range(KD):
                    last = nc.tensor.matmul(out[:, m * KD + j:m * KD + j + 1], ada_acc[m][:, j * P:(j + 1) * P],
                                            c.ones[:, 0:1], start=True, stop=True)
                last.then_inc(ada_cols_done, 1)

            def project(t, with_ada=False):
                banks = ring([("A", n, 0, t) for n in range(AU)], [("T", 2 + n // 2, n % 2, t) for n in range(4)])
                for j in range(NPIECE):
                    high, rest = piece_view(win_high[:, j % 2]), piece_view(win_rest[:, j % NSLOT])
                    pe.wait_ge(rest_ready, t * NPIECE + j + 1)
                    if j == 0:
                        pe.wait_ge(hT_ready, (t + 1) * NT)
                    for half in range(2):
                        out = next(banks)
                        if j < 8:
                            cols = slice(half * P, (half + 1) * P)
                            for k in range(KD):
                                nc.tensor.matmul(out[:], high[:, k, cols], hT_high[:, k, :], start=(k == 0), stop=False)
                                nc.tensor.matmul(out[:], high[:, k, cols], hT_rest[:, k, :], start=False, stop=False)
                                last = nc.tensor.matmul(out[:], rest[:, k, cols], hT_high[:, k, :], start=False, stop=(k == KD - 1))
                        else:
                            for s in range(2):
                                tok = slice((2 * half + s) * P, (2 * half + s + 1) * P)
                                to = out[:, s * 256:(s + 1) * 256]
                                for k in range(KD):
                                    nc.tensor.matmul(to, hT_high[:, k, tok], high[:, k, :], start=(k == 0), stop=False)
                                    nc.tensor.matmul(to, hT_high[:, k, tok], rest[:, k, :], start=False, stop=False)
                                    last = nc.tensor.matmul(to, hT_rest[:, k, tok], high[:, k, :], start=False, stop=(k == KD - 1))
                        last.then_inc(proj_ready, 1)
                    if with_ada and j in (6, 9):
                        ada_columns(j // 3)

            def y_half(t, i, half, banks):
                if i == 0 and half == 0:
                    pe.wait_ge(wo_in, 16)
                    pe.wait_ge(yT_rec, (t + 1) * NT)
                    pe.wait_ge(yT_conv, (t + 1) * NCH)
                out = next(banks)
                for k in range(KD):
                    last = nc.tensor.matmul(out[:], yT[:, k, i * P:(i + 1) * P], wo[:, k, half * 512:(half + 1) * 512],
                                            start=(k == 0), stop=(k == KD - 1))
                last.then_inc(y_ready, 1)

            def router_turn(t, i, banks):
                pe.wait_ge(xn_ready, t * NT + i + 1)
                for half in range(2):
                    out = next(banks)
                    for j in range(4):
                        k = half * 4 + j
                        last = nc.tensor.transpose(out[:, j * P:(j + 1) * P], xres[:, i % 2, k * P:(k + 1) * P], c.ident[:])
                    last.then_inc(rT_ready, 1)

            def logits(t, i, banks):
                pe.wait_ge(rin_ready, t * 2 * NT + 2 * i + 2)
                out = next(banks)
                for k in range(KD):
                    nc.tensor.matmul(out[:, 0:NR], yt[:, i % 2, k * P:(k + 1) * P], c.wroute[:, k, :], start=(k == 0), stop=False)
                nc.tensor.matmul(out[:, 0:NR], c.ones[0:1, :], c.brow[:], start=False, stop=True).then_inc(logit_ready, 1)

            def mean(t):
                pe.wait_ge(conv_step, (t + 1) * CONV_STEPS)
                wait(pe, masked, t * NT)
                for k in range(NCH):
                    last = nc.tensor.matmul(pS[:], c.ones[:], cv[:, k, :], start=(k == 0), stop=(k == NCH - 1))
                last.then_inc(mean_ready, 1)

            def variance(t):
                wait(pe, o_saved, t * NT)
                for k in range(NCH):
                    pe.wait_ge(squared, t * NCH + k + 1)
                    last = nc.tensor.matmul(pO[:], c.ones[:], hT[:, k, :], start=(k == 0), stop=(k == NCH - 1))
                last.then_inc(var_ready, 1)

            def scores(t, i):
                tok = slice(i * P, (i + 1) * P)
                if i == 0:
                    pe.wait_ge(exp_used, (t + 1) * 3 * NH)
                    pe.wait_ge(centred, (t + 1) * NCH)
                    if isinstance(t, int) and t == 0:
                        pe.wait_ge(mod_ready, 1)
                    wait(pe, yT_rec, t * NT)
                else:
                    pe.wait_ge(masked, t * NT + i)
                for h in range(NH):
                    last = nc.tensor.matmul(pS[:, h * P:(h + 1) * P], ki[:, h, tok], qd[:, h, tok], start=True, stop=True)
                last.then_inc(score_ready, 1)
                if i > 0:
                    pe.wait_ge(state_ready, t * 2 * NT + 2 * i)
                for h in range(NH):
                    last = nc.tensor.transpose(pT[:, h * P:(h + 1) * P], ke[:, h, tok], c.ident[:])
                last.then_inc(keT_psum, 1)

            def state_sums(t, i):
                pe.wait_ge(keT_ready, t * NT + i + 1)
                if i == 0:
                    pe.wait_ge(v_ready, (t + 1) * 4)
                for s, out in ((0, pD), (1, pT)):
                    rows = slice(s * CH, (s + 1) * CH)
                    for h in range(NH):
                        last = nc.tensor.matmul(out[:, h * P:(h + 1) * P], scr[rows, (i % 2) * 512 + h * P:(i % 2) * 512 + (h + 1) * P],
                                                v[rows, i, h * P:(h + 1) * P], start=True, stop=True)
                    last.then_inc(dstate_ready, 1)

            def outputs(t, i):
                pe.wait_ge(masked, t * NT + i + 1)
                pe.wait_ge(state_ready, t * 2 * NT + 2 * i + 1)
                if i == 0:
                    pe.wait_ge(ln_rstd, t + 1)
                else:
                    pe.wait_ge(o_saved, t * NT + i)
                for h in range(NH):
                    hc = slice(h * P, (h + 1) * P)
                    nc.tensor.matmul(pO[:, hc], c.scoreT[:, i % 2, hc], v[:, i, hc], start=True, stop=False, skip_group_check=True)
                    for s in range(2):
                        at = i * P + s * CH
                        last = nc.tensor.matmul(pO[s * CH:(s + 1) * CH, hc], qd[:, h, at:at + CH],
                                                c.state[:, (2 * i + s) % 4, hc], start=False, stop=(s == 1), skip_group_check=True)
                last.then_inc(o_ready, 1)

            def turn_outputs(t, i):
                if i == 0:
                    pe.wait_ge(o_gated, t + 1)
                if i >= 2:
                    pe.wait_ge(yT_rec, t * NT + i - 1)
                out = (pT, pD)[i % 2]
                for h in range(NH):
                    last = nc.tensor.transpose(out[:, h * P:(h + 1) * P], ob[:, i, h * P:(h + 1) * P], c.ident[:])
                last.then_inc(oT_psum, 1)

            def last_modulation():
                for n in range(AU - 4, AU):
                    pe.wait_ge(*reader("A", n, 0, 0))
                ada_columns(4)
                ada_columns(5)
                for r in range(2):
                    pe.wait_ge(diag_ready, r + 1)
                    nc.tensor.matmul(bank[r][:], c.ones[:], diag[r], start=True, stop=True).then_inc(row_done, 1)
                pe.wait_ge(route_in, 64)
                for k in range(KD):
                    last = nc.tensor.matmul(bank[2][0:1, 0:NR], c.shift2[:, k:k + 1], c.wroute[:, k, :],
                                            start=(k == 0), stop=(k == KD - 1))
                last.then_inc(row_done, 1)
                pe.wait_ge(mod_ready, 2)

            def steps(t, mix, out, nxt, before, after_outputs=None):
                block_of_kind = {"T": t + 1, "y": t - 1, "r": t - 1, "l": t - 1}
                order = STEPS if mix else TAIL
                banks = ring([(k, i, h, block_of_kind[k]) for k, i, h in stage_units(kinds_of(out, nxt), order)], before,
                             bank if mix else tail_bank)
                for kind, *at in order:
                    if kind in ("y", "r", "l"):
                        if out:
                            {"y": y_half, "r": router_turn, "l": logits}[kind](t - 1, *at, banks)
                    elif kind == "T":
                        if nxt:
                            turn_in(t + 1, *at, banks)
                    elif mix:
                        {"mean": mean, "var": variance, "A": scores, "B": state_sums, "O": outputs, "oT": turn_outputs}[kind](t, *at)
                        if after_outputs and (kind, *at) == ("O", NT - 1):
                            after_outputs()

            after_project = lambda t: [("A", AU - 4 + n, 0, t) for n in range(4)]

            pe.wait_ge(mask_step, MASK_STEPS)
            pe.wait_ge(vec_in, 16 * (len(VEC) + 1))
            nc.tensor.transpose(pS[:, 0:NVEC], tmp[0:NVEC, 0:P], c.ident[0:NVEC, 0:NVEC])
            for k in range(NCH):
                last = nc.tensor.transpose(pO[:, k * CW:(k + 1) * CW], scr[0:CW, k * P:(k + 1) * P], c.ident[0:CW, 0:CW])
            last.then_inc(turned, 1)
            first = ring([("T", n // 2, n % 2, 0) for n in range(2 * NT)], None)
            turn_in(0, 0, first)
            turn_in(0, 1, first)
            ada_columns(0)
            ada_columns(1)
            turn_in(0, 2, first)
            turn_in(0, 3, first)
            project(0, with_ada=True)
            steps(0, True, False, True, after_project(0), last_modulation)
            with pe.Fori(1, NB - 1) as t:
                project(t)
                steps(t, True, True, True, after_project(t))
            project(NB - 1)
            steps(NB - 1, True, True, False, after_project(NB - 1))
            ended = [(k, i, h, NB - 2) for k, i, h in stage_units(kinds_of(True, False))[-4:]]
            steps(NB, False, True, False, ended)

        @block.scalar
        def _(act):
            A = nc.scalar.activation
            logs = lambda: act.preload_act_table_set("natural_log_exp_and_others")

            def x_sums(t, i, junk):
                ch = Chain(act, a_norm, t * 2 * NT + 2 * i)
                act.wait_ge(x_in[i % 2], t * 32 + 16 * (i // 2 + 1))
                ch.link(A(junk, xt[:, i % 2], ACT.Square, accum_out=sums[:, i:i + 1]))
                ch.link(A(sums[:, i:i + 1], sums[:, i:i + 1], ACT.Ln, bias=c.epsc[:], scale=1.0 / D))
                A(sums[:, i:i + 1], sums[:, i:i + 1], ACT.Exp, scale=-0.5).then_inc(x_rstd, 1)

            def modulate(t, i, out):
                act.wait_ge(xT_ready, t * 2 * NT + 2 * i + 1)
                tok = slice(i * P, (i + 1) * P)
                for k in range(4):
                    last = A(hT[:, k, tok], out[:, k * P:(k + 1) * P], ACT.Identity,
                             scale=c.scale1[:, k:k + 1], bias=c.shift1[:, k:k + 1])
                last.then_inc(hT_raw[0], 1)
                for half in range(2):
                    act.wait_ge(hT_raw[half], t * NT + i + 1)
                A(hT_high[:, :, tok], hT[:, :, tok], ACT.Copy).then_inc(hT_split, 1)

            def split_piece(t, j, before=None):
                act.wait_ge(win_in[j % NSLOT], win_bytes(t, j))
                if j >= 2:
                    act.wait_ge(proj_ready, t * AU + 2 * (j - 2) + 2)
                elif before is not None and j == 0:
                    act.wait_ge(logit_ready, (before + 1) * NT)
                    for s in range(2):
                        act.wait_ge(x1_stored[s], (before + 1) * 32)
                        act.wait_ge(xn_stored[s], (before + 1) * 32)
                A(win_high[:, j % 2], win[:, j % NSLOT], ACT.Copy).then_inc(high_ready, 1)

            def gates(t):
                for j in range(NCH):
                    act.wait_ge(proj_ready, t * AU + 2 * j + 2)
                    if j == 0:
                        wait(act, yT_conv, t * NCH)
                    A(cv[:, j], bank[(2 * j + 1) % 4][:], ACT.Sigmoid).then_inc(gate_sig, 1)
                    split_piece(t, j + 2)
                for h in range(NH):
                    n = 8 + 2 * h
                    act.wait_ge(proj_ready, t * AU + n + 1)
                    if h == 0:
                        wait(act, o_ready, t * NT)
                        wait(act, keT_psum, t * NT)
                    A(ke[:, h], bank[n % 4][:], ACT.Sigmoid).then_inc(q_parts, 1)
                    A(qd[:, h], bank[n % 4][:], ACT.Copy).then_inc(q_parts, 1)
                    act.wait_ge(proj_ready, t * AU + n + 2)
                    A(ki[:, h], bank[(n + 1) % 4][:], ACT.Sigmoid).then_inc(q_parts, 1)
                    split_piece(t, NCH + h + 2)
                for j in range(2):
                    for half in range(2):
                        n = 16 + 2 * j + half
                        act.wait_ge(proj_ready, t * AU + n + 1)
                        src = bank[n % 4][:].rearrange("p (a b) -> p a b", a=2)
                        A(v[:, 2 * half:2 * half + 2, j * 256:(j + 1) * 256], src, ACT.Copy).then_inc(v_ready, 1)
                    split_piece(t, 10 + j)
                for j in range(2):
                    for half in range(2):
                        n = 20 + 2 * j + half
                        act.wait_ge(proj_ready, t * AU + n + 1)
                        if n == 20:
                            wait(act, oT_psum, t * NT)
                        src = bank[n % 4][:].rearrange("p (a b) -> p a b", a=2)
                        cols = slice(j * 256, (j + 1) * 256)
                        A(ob[:, 2 * half:2 * half + 2, cols], src, ACT.Copy).then_inc(g_parts, 1)
                act.wait_ge(g_parts, (t + 1) * 4)
                act.wait_ge(conv_step, (t + 1) * CONV_STEPS)
                A(gs, ob[:], ACT.Silu).then_inc(g_done, 1)

            def heads(t):
                grow_, shrink = scr[:, 0:T], scr[:, T:2 * T]
                act.sem_inc(act_passed, 1)
                logs()
                for h in range(NH):
                    act.wait_ge(v_head, t * 2 * NH + 2 * h + 2)
                    A(ki[:, h], ki[:, h], ACT.Ln).then_inc(logf_ready, 1)
                for h in range(NH):
                    n = t * NH + h
                    act.wait_ge(b_ready, n + 1)
                    if h > 0:
                        act.wait_ge(exp_used, 3 * n - 1)
                    A(grow_, ki[:, h], ACT.Exp).then_inc(exp_ready, 1)
                    A(decay[:, h], ki[:, h, CH - 1::CH], ACT.Exp).then_inc(exp_ready, 1)
                    A(shrink, ki[:, h], ACT.Exp, scale=-1.0).then_inc(exp_ready, 1)
                    act.wait_ge(diff_ready, n + 1)
                    A(tmp[:], tmp[:], ACT.Exp).then_inc(exp_ready, 1)

            def y_sums(t, i, places):
                ch = Chain(act, a_out, t * 7 * NT + 7 * i)
                if i == 0:
                    act.wait_ge(proj_ready, min(t + 2, NB) * AU if isinstance(t, int) else (t + 2) * AU)
                s = sums[:, 8 + 2 * (i % 2):10 + 2 * (i % 2)]
                r = sums[:, 12 + i % 2:13 + i % 2]
                wait(act, x1_ready, t * NT + max(i - 1, 0))
                wait(act, logit_ready, t * NT + max(i - 1, 0))
                for half in range(2):
                    act.wait_ge(y_ready, t * 2 * NT + 2 * i + half + 1)
                    ch.link(A(yt[:, i % 2, half * 512:(half + 1) * 512], places["y", i, half][:], ACT.Square,
                              accum_out=s[:, half:half + 1]))
                ch.link(A(r, s[:, 0:1], ACT.Identity, bias=s[:, 1:2]))
                ch.link(A(r, r, ACT.Ln, bias=c.epsc[:], scale=1.0 / D))
                A(r, r, ACT.Exp, scale=-0.5).then_inc(y_rstd, 1)

            def x1_sums(t, i):
                ch = Chain(act, a_out, t * 7 * NT + 7 * i + 4)
                r = sums[:, 14 + i % 2:15 + i % 2]
                act.wait_ge(x1_ready, t * NT + i + 1)
                for half in range(2):
                    cols = slice(half * 512, (half + 1) * 512)
                    ch.link(A(xres[:, i % 2, cols], yt[:, i % 2, cols], ACT.Square, accum_out=sums[:, 16 + half:17 + half]))
                ch.link(A(r, sums[:, 16:17], ACT.Identity, bias=sums[:, 17:18]))
                A(r, r, ACT.Ln, bias=c.epsc[:], scale=1.0 / D).then_inc(x1_rstd, 1)
                act.wait_ge(x1_rstd, (t * NT + i) * 2 + 1)
                A(r, r, ACT.Exp, scale=-0.5).then_inc(x1_rstd, 1)

            def router_in(t, i, places):
                act.wait_ge(x1_stored[i % 2], t * 32 + 16 * (i // 2 + 1))
                for half in range(2):
                    act.wait_ge(rT_ready, t * 2 * NT + 2 * i + half + 1)
                    A(yt[:, i % 2, half * 512:(half + 1) * 512], places["r", i, half][:], ACT.Copy).then_inc(rin_ready, 1)

            def squares(t):
                act.wait_ge(centred, (t + 1) * NCH)
                act.wait_ge(proj_ready, (t + 1) * AU)
                for k in range(NCH):
                    A(hT[:, k, :], cv[:, k], ACT.Square).then_inc(squared, 1)

            def variance(t):
                act.wait_ge(var_ready, t + 1)
                A(hT[:, 4, :], pO[:], ACT.Ln, bias=c.epsc[:], scale=1.0 / DC).then_inc(a_ln, 1)
                act.wait_ge(a_ln, 2 * t + 1)
                A(hT[:, 4, :], hT[:, 4, :], ACT.Exp, scale=-0.5).then_inc(ln_rstd, 1)

            def conv_gate(t):
                for k in range(NCH):
                    act.wait_ge(ln_normed, t * NCH + k + 1)
                    A(hT[:, k, :], cv[:, k], ACT.Sigmoid, scale=col("conv_ln_gain", k), bias=col("conv_ln_bias", k)).then_inc(ln_sig, 1)
                logs()

            def save_keys(t, i):
                act.wait_ge(keT_psum, t * NT + i + 1)
                if i >= 2:
                    act.wait_ge(dstate_ready, t * 2 * NT + 2 * (i - 1))
                A(scr[:, (i % 2) * 512:(i % 2 + 1) * 512], pT[:], ACT.Copy).then_inc(keT_ready, 1)

            def square_outputs(t, i):
                act.wait_ge(o_saved, t * NT + i + 1)
                wait(act, o_ms, t * NT + i)
                A(tmp[:], ob[:, i], ACT.Square).then_inc(o_squared, 1)

            def outputs_rstd(t):
                ch = Chain(act, a_ln, 2 * t + 1)
                act.wait_ge(o_ms, (t + 1) * NT)
                ch.link(A(sums[:, 32:48], sums[:, 32:48], ACT.Ln, bias=c.epsc[:], scale=1.0 / P))
                A(sums[:, 32:48], sums[:, 32:48], ACT.Exp, scale=-0.5).then_inc(o_rstd, 1)

            def save_turned(t, i):
                act.wait_ge(oT_psum, t * NT + i + 1)
                A(yT[:, NH:, i * P:(i + 1) * P], (pT, pD)[i % 2][:].rearrange("p (h n) -> p h n", h=NH), ACT.Copy,
                  scale=col("rec_norm_gain", 0)).then_inc(yT_rec, 1)

            ORDER = [("sq",), ("ysum", 0), ("var",), ("key", 0), ("x1sum", 0), ("ysum", 1), ("rin", 0), ("osq", 0), ("key", 1),
                     ("x1sum", 1), ("osq", 1), ("xsum", 0), ("xsum", 1), ("key", 2), ("gate",), ("rin", 1), ("osq", 2), ("key", 3),
                     ("ysum", 2), ("x1sum", 2), ("osq", 3), ("orstd",), ("ysum", 3), ("x1sum", 3), ("rin", 2), ("T", 0), ("T", 1),
                     ("turned", 0), ("turned", 1), ("rin", 3), ("xsum", 2), ("xsum", 3), ("turned", 2), ("turned", 3), ("split", 0),
                     ("T", 2), ("T", 3), ("split", 1)]

            TAIL_ORDER = [("ysum", 0), ("x1sum", 0), ("ysum", 1), ("rin", 0), ("x1sum", 1), ("ysum", 2), ("rin", 1), ("x1sum", 2),
                          ("ysum", 3), ("rin", 2), ("x1sum", 3), ("rin", 3)]

            def steps(t, mix, out, nxt):
                places = stage_banks(mix, out, nxt)
                for kind, *at in (ORDER if mix else TAIL_ORDER):
                    if kind in ("ysum", "x1sum", "rin"):
                        if out:
                            if kind == "x1sum":
                                x1_sums(t - 1, *at)
                            else:
                                {"ysum": y_sums, "rin": router_in}[kind](t - 1, *at, places)
                    elif kind == "xsum":
                        if nxt:
                            if at[0] == 2:
                                act.wait_ge(dstate_ready, (t + 1) * 2 * NT)
                            x_sums(t + 1, *at, hT[:, 5:7, :].rearrange("p a n -> p (a n)") if at[0] < 2 else scr[:])
                    elif kind == "T":
                        if nxt:
                            if at[0] == 0:
                                act.wait_ge(ln_out, (t + 1) * NCH)
                            modulate(t + 1, *at, places["T", at[0], 0])
                    elif kind == "split":
                        if nxt:
                            split_piece(t + 1, *at, before=t - 1 if out else None)
                    elif mix:
                        {"sq": squares, "var": variance, "key": save_keys, "gate": conv_gate, "osq": square_outputs,
                         "orstd": outputs_rstd, "turned": save_turned}[kind](t, *at)

            load_vectors(act, 1)
            act.wait_ge(cols_ready, 1)
            A(cond[:], c.cols[:, VEC["c"][0]:VEC["c"][1]], ACT.Silu).then_inc(cond_ready, 1)
            logs()
            act.wait_ge(lb_in, 1)
            A(lbt[:, 1:3], lbt[:, 1:3], ACT.Exp).then_inc(cond_ready, 1)
            x_sums(0, 0, scr[:])
            x_sums(0, 1, scr[:])
            split_piece(0, 0)
            split_piece(0, 1)
            act.wait_ge(scale1_ready, 1)
            for i in range(NT):
                modulate(0, i, bank[2 * (i % 2)])
                if i < 2:
                    x_sums(0, i + 2, scr[:])
            gates(0)
            heads(0)
            steps(0, True, False, True)
            with act.Fori(1, NB - 1) as t:
                gates(t)
                heads(t)
                steps(t, True, True, True)
            gates(NB - 1)
            heads(NB - 1)
            steps(NB - 1, True, True, False)
            steps(NB, False, True, False)

        @block.vector
        def _(dve):
            V = nc.vector

            def norm_in(t, i):
                dve.wait_ge(x_rstd, t * NT + i + 1)
                V.tensor_scalar(xt[:, i % 2], xt[:, i % 2], sums[:, i:i + 1], None, ALU.mult).then_inc(x_normed, 1)

            def ada_sums(m, halves=(0, 1)):
                for half in halves:
                    p = 2 * m + half
                    dve.wait_ge(*ada_load(p))
                    for k in range(4):
                        w, factor = ada_slot[slot_of(p)][:, k], cond[:, 4 * half + k:4 * half + k + 1]
                        if half == 0 and k == 0:
                            ins = V.tensor_scalar(ada_acc[m], w, factor, None, ALU.mult)
                        else:
                            mod_chain.sync()
                            ins = V.scalar_tensor_tensor(out=ada_acc[m], in0=w, scalar=factor, in1=ada_acc[m],
                                                         op0=ALU.mult, op1=ALU.add)
                        mod_chain.step(ins)
                    mod_chain.sync()
                    dve.sem_inc(ada_used, 1)

            def modulate(t, i, out):
                dve.wait_ge(xT_ready, t * 2 * NT + 2 * i + 2)
                for j in range(4):
                    k = 4 + j
                    last = V.tensor_scalar(hT[:, k, i * P:(i + 1) * P], out[:, j * P:(j + 1) * P],
                                           c.scale1[:, k:k + 1], c.shift1[:, k:k + 1], ALU.mult, ALU.add)
                last.then_inc(hT_raw[1], 1)

            def rest_of_input(t, i):
                dve.wait_ge(hT_split, t * NT + i + 1)
                tok = slice(i * P, (i + 1) * P)
                V.tensor_tensor(hT_rest[:, :, tok], hT[:, :, tok], hT_high[:, :, tok].bitcast(F32),
                                ALU.subtract).then_inc(hT_ready, 1)

            def rest_of_piece(t, j):
                dve.wait_ge(high_ready, t * NPIECE + j + 1)
                V.tensor_tensor(win_rest[:, j % NSLOT], win[:, j % NSLOT], win_high[:, j % 2].bitcast(F32), ALU.subtract).then_inc(rest_ready, 1)

            def conv(t, with_ada=False):
                ch = Chain(dve, conv_step, t * CONV_STEPS)
                done = {}

                def gated(j):
                    dve.wait_ge(gate_sig, t * NCH + j + 1)
                    V.tensor_tensor(u[:, j, HALO:], bank[(2 * j) % 4][:], cv[:, j], ALU.mult).then_inc(u_ready, 1)

                def taps(pair, w0, w1):
                    for w in range(w0, w1):
                        for j in pair:
                            if w == 0:
                                dve.wait_ge(u_ready, t * NCH + j + 1)
                            tap = c.taps[:, j * CW + w:j * CW + w + 1]
                            if w == 0:
                                ins = V.tensor_scalar(cv[:, j], u[:, j, 0:T], tap, col("dw_bias", j), ALU.mult, ALU.add)
                            else:
                                dve.wait_ge(conv_step, done[j])
                                ins = V.scalar_tensor_tensor(out=cv[:, j], in0=u[:, j, w:w + T], scalar=tap, in1=cv[:, j],
                                                             op0=ALU.mult, op1=ALU.add)
                            ch.step(ins)
                            done[j] = ch.base + ch.n

                for k in range(NCH):
                    src = c.zeros[:, 0:HALO] if isinstance(t, int) and t == 0 else halo[:, k]
                    ch.step(V.tensor_copy(u[:, k, 0:HALO], src))
                ch.sync()
                gated(0)
                rest_of_piece(t, 2)
                gated(1)
                rest_of_piece(t, 3)
                taps((0, 1), 0, 5)
                gated(2)
                taps((0, 1), 5, 7)
                rest_of_piece(t, 4)
                if with_ada:
                    ada_sums(2, (0,))
                taps((0, 1), 7, 11)
                gated(3)
                taps((0, 1), 11, 13)
                rest_of_piece(t, 5)
                if with_ada:
                    ada_sums(2, (1,))
                taps((0, 1), 13, 19)
                rest_of_piece(t, 6)
                if with_ada:
                    ada_sums(3, (0,))
                taps((0, 1), 19, 25)
                rest_of_piece(t, 7)
                if with_ada:
                    ada_sums(3, (1,))
                taps((0, 1), 25, CW)
                rest_of_piece(t, 8)
                taps((2, 3), 0, 6)
                rest_of_piece(t, 9)
                taps((2, 3), 6, 11)
                head_gates(t)
                rest_of_piece(t, 10)
                taps((2, 3), 11, 17)
                rest_of_piece(t, 11)
                taps((2, 3), 17, CW)
                ch.sync()
                for k in range(NCH):
                    ch.step(V.tensor_copy(halo[:, k], u[:, k, T:T + HALO]))
                ch.sync()
                assert ch.n == CONV_STEPS, ch.n

            def head_gates(t):
                ch = Chain(dve, v_head, t * 2 * NH)
                for h in range(NH):
                    dve.wait_ge(q_parts, (t * NH + h) * 3 + 3)
                    V.tensor_scalar(ki[:, h], ki[:, h], c.oneless[:, h:h + 1], c.lb[:, h:h + 1], ALU.mult, ALU.add).then_inc(forget_ready, 1)
                    ch.step(V.tensor_tensor(qd[:, h], qd[:, h], ke[:, h], ALU.mult))
                    ch.sync()
                    dve.wait_ge(forget_ready, t * NH + h + 1)
                    ch.step(V.tensor_scalar(ke[:, h], ki[:, h], -1.0, 1.0, ALU.mult, ALU.add))

            def heads(t):
                grow_, shrink = scr[:, 0:T], scr[:, T:2 * T]
                for h in range(NH):
                    n = t * NH + h
                    dve.wait_ge(logf_ready, n + 1)
                    V.tensor_tensor_scan(ki[:, h], c.restart[:], ki[:, h], 0.0, ALU.mult, ALU.add).then_inc(b_ready, 1)
                for h in range(NH):
                    n = t * NH + h
                    dve.wait_ge(b_ready, n + 1)
                    if h > 0:
                        dve.wait_ge(exp_used, 3 * n)
                    b3 = ki[:, h].rearrange("p (n k) -> p n k", k=CH)
                    V.tensor_tensor(tmp[:].rearrange("p (n k) -> p n k", k=CH),
                                    b3[:, :, CH - 1:CH].to_broadcast([P, T // CH, CH]), b3, ALU.subtract).then_inc(diff_ready, 1)
                    dve.wait_ge(exp_ready, 4 * n + 2)
                    V.tensor_tensor(qd[:, h], qd[:, h], grow_, ALU.mult).then_inc(exp_used, 1)
                    dve.wait_ge(exp_ready, 4 * n + 3)
                    dve.wait_ge(diff_ready, n + 1)
                    V.tensor_tensor(ki[:, h], ke[:, h], shrink, ALU.mult).then_inc(exp_used, 1)
                    dve.wait_ge(exp_ready, 4 * n + 4)
                    dve.wait_ge(exp_used, 3 * n + 2)
                    V.tensor_tensor(ke[:, h], ke[:, h], tmp[:], ALU.mult).then_inc(exp_used, 1)

            def y_norm(t, i, places):
                dve.wait_ge(y_rstd, t * NT + i + 1)
                wait(dve, x1_stored[i % 2], t * 32 + 16 * (i // 2))
                for half in range(2):
                    cols = slice(half * 512, (half + 1) * 512)
                    V.scalar_tensor_tensor(out=yt[:, i % 2, cols], in0=places["y", i, half][:],
                                           scalar=sums[:, 12 + i % 2:13 + i % 2], in1=c.grow[:, cols],
                                           op0=ALU.mult, op1=ALU.mult).then_inc(y_normed, 1)
                dve.wait_ge(y_normed, t * 2 * NT + 2 * i + 2)
                dve.wait_ge(res_in[i % 2], t * 32 + 16 * (i // 2 + 1))
                V.tensor_tensor(yt[:, i % 2], yt[:, i % 2], xres[:, i % 2], ALU.add).then_inc(x1_ready, 1)

            def x1_norm(t, i):
                dve.wait_ge(x1_rstd, (t * NT + i + 1) * 2)
                V.tensor_scalar(xres[:, i % 2], yt[:, i % 2], sums[:, 14 + i % 2:15 + i % 2], None, ALU.mult).then_inc(xn_ready, 1)

            def save_logits(t, i, places):
                dve.wait_ge(logit_ready, t * NT + i + 1)
                V.tensor_copy(c.logits[:, bass.ds(t * NT + i, 1), :].rearrange("p a n -> p (a n)"),
                              places["l", i, 0][:, 0:NR]).then_inc(logit_saved, 1)

            def centre(t):
                dve.wait_ge(mean_ready, t + 1)
                for k in range(NCH):
                    V.scalar_tensor_tensor(out=cv[:, k], in0=pS[:], scalar=-1.0 / DC, in1=cv[:, k],
                                           op0=ALU.mult, op1=ALU.add).then_inc(centred, 1)

            def scale_conv(t):
                dve.wait_ge(ln_rstd, t + 1)
                for k in range(NCH):
                    V.tensor_tensor(cv[:, k], cv[:, k], hT[:, 4, :], ALU.mult).then_inc(ln_normed, 1)

            def conv_out(t):
                ch = Chain(dve, v_ln, t * NCH)
                for k in range(NCH):
                    dve.wait_ge(ln_sig, t * NCH + k + 1)
                    ch.step(V.tensor_scalar(cv[:, k], cv[:, k], col("conv_ln_gain", k), col("conv_ln_bias", k), ALU.mult, ALU.add))
                ch.sync()
                for k in range(NCH):
                    V.tensor_tensor(cv[:, k], cv[:, k], hT[:, k, :], ALU.mult).then_inc(ln_out, 1)

            def place_conv(t):
                wait(dve, y_ready, t * 2 * NT)
                dve.wait_ge(ln_out, (t + 1) * NCH)
                for k in range(NCH):
                    V.tensor_copy(yT[:, k, :], cv[:, k]).then_inc(yT_conv, 1)

            def mask(t, i):
                wait_apart(dve, score_ready, t * NT + i + 1, dve_passed)
                V.copy_predicated(c.scoreT[:, i % 2].rearrange("p (h n) -> p h n", h=NH),
                                  c.causal[:].bitcast(I32).unsqueeze(1).to_broadcast([P, NH, P]),
                                  pS[:].rearrange("p (h n) -> p h n", h=NH)).then_inc(masked, 1)

            def states(t, i):
                for s in range(2):
                    m = 2 * i + s
                    dve.wait_ge(dstate_ready, t * 2 * NT + m + 1)
                    wait(dve, state_ready, t * 2 * NT + m)
                    for h in range(NH):
                        hc = slice(h * P, (h + 1) * P)
                        last = V.scalar_tensor_tensor(out=c.state[:, (m + 1) % 4, hc], in0=c.state[:, m % 4, hc],
                                                      scalar=decay[:, h, m:m + 1], in1=(pD, pT)[s][:, hc], op0=ALU.mult, op1=ALU.add)
                    last.then_inc(state_ready, 1)

            def save_outputs(t, i):
                if i == 0:
                    dve.wait_ge(g_done, t + 1)
                dve.wait_ge(o_ready, t * NT + i + 1)
                V.tensor_copy(ob[:, i], pO[:]).then_inc(o_saved, 1)

            def output_squares(t, i):
                dve.wait_ge(o_squared, t * NT + i + 1)
                V.tensor_reduce(sums[:, 32 + 4 * i:36 + 4 * i], tmp[:].rearrange("p (h n) -> p h n", h=NH), axis=AX.X, op=ALU.add).then_inc(o_ms, 1)

            def gate_outputs(t):
                dve.wait_ge(o_rstd, t + 1)
                o3 = ob[:].rearrange("p i (h n) -> p (i h) n", h=NH)
                V.tensor_tensor(o3, o3, sums[:, 32:48].unsqueeze(2).to_broadcast([P, NT * NH, P]), ALU.mult).then_inc(v_rec, 1)
                dve.wait_ge(v_rec, t + 1)
                dve.wait_ge(g_done, t + 1)
                V.tensor_tensor(ob[:], ob[:], gs[:], ALU.mult).then_inc(o_gated, 1)

            ORDER = [("centre",), ("ynorm", 0), ("scale",), ("mask", 0), ("x1norm", 0), ("state", 0), ("ynorm", 1), ("osave", 0), ("oms", 0),
                     ("mask", 1), ("state", 1), ("x1norm", 1), ("logit", 0), ("osave", 1), ("oms", 1),
                     ("mask", 2), ("xnorm", 0), ("xnorm", 1), ("state", 2), ("osave", 2), ("conv",), ("oms", 2),
                     ("mask", 3), ("ynorm", 2), ("state", 3), ("x1norm", 2), ("logit", 1), ("osave", 3), ("oms", 3),
                     ("gate",), ("ynorm", 3), ("x1norm", 3), ("T", 0), ("T", 1), ("input", 0), ("input", 1), ("logit", 2), ("place",), ("xnorm", 2), ("xnorm", 3), ("logit", 3), ("T", 2), ("T", 3),
                     ("piece", 0), ("input", 2), ("input", 3), ("piece", 1)]

            TAIL_ORDER = [("ynorm", 0), ("x1norm", 0), ("ynorm", 1), ("x1norm", 1), ("logit", 0), ("ynorm", 2), ("x1norm", 2), ("logit", 1),
                          ("ynorm", 3), ("x1norm", 3), ("logit", 2), ("logit", 3)]

            def steps(t, mix, out, nxt, after={}):
                places = stage_banks(mix, out, nxt)
                for kind, *at in (ORDER if mix else TAIL_ORDER):
                    if kind in ("ynorm", "x1norm", "logit"):
                        if out:
                            if kind == "x1norm":
                                x1_norm(t - 1, *at)
                            else:
                                {"ynorm": y_norm, "logit": save_logits}[kind](t - 1, *at, places)
                    elif kind == "T":
                        if nxt:
                            if at[0] == 0:
                                dve.wait_ge(x_rstd, (t + 1) * NT + 2)
                            modulate(t + 1, *at, places["T", at[0], 1])
                    elif kind in ("xnorm", "input", "piece"):
                        if nxt:
                            {"xnorm": norm_in, "input": rest_of_input, "piece": rest_of_piece}[kind](t + 1, *at)
                    elif mix:
                        {"centre": centre, "scale": scale_conv, "mask": mask, "state": states, "osave": save_outputs,
                         "oms": output_squares, "conv": conv_out, "gate": gate_outputs, "place": place_conv}[kind](t, *at)
                    if (kind, *at) in after:
                        after[(kind, *at)]()

            cols = lambda n: c.cols[:, VEC[n][0]:VEC[n][1]]
            m_of = lambda i: mod[:, i * KD:(i + 1) * KD]

            def last_modulation():
                dve.wait_ge(ada_cols_done, MODS)
                mod_chain.link(V.tensor_tensor(mod[:, 4 * KD:], bank[3][:, 4 * KD:6 * KD], c.cols[:, VEC["b_ada"][0] + 4 * KD:VEC["b_ada"][1]], ALU.add))
                mod_chain.step(V.scalar_tensor_tensor(out=c.scale2[:], in0=m_of(4), scalar=1.0, in1=cols("g_pre_ffn"),
                                                      op0=ALU.add, op1=ALU.mult))
                mod_chain.step(V.tensor_copy(c.shift2[:], m_of(3)))
                mod_chain.step(V.tensor_tensor(c.gcol[:, 0:KD], m_of(2), cols("g_post_mix"), ALU.mult))
                mod_chain.link(V.tensor_tensor(c.gcol[:, KD:2 * KD], m_of(5), cols("g_post_ffn"), ALU.mult))
                for r in range(2):
                    for j in range(4):
                        k = 4 * r + j
                        last = V.tensor_scalar(diag[r][:, j * P:(j + 1) * P], c.ident[:], c.gcol[:, k:k + 1], None, ALU.mult)
                    last.then_inc(diag_ready, 1)
                for r in range(2):
                    dve.wait_ge(row_done, r + 1)
                    mod_chain.step(V.tensor_copy(c.grow[:, r * 512:(r + 1) * 512], bank[r][:]))
                dve.wait_ge(row_done, 3)
                mod_chain.step(V.tensor_tensor(c.brow[:], c.brow[:], bank[2][0:1, 0:NR], ALU.add))
                for k in range(KD):
                    mod_chain.step(V.tensor_scalar(c.wroute[:, k, :], c.wroute[:, k, :], c.scale2[:, k:k + 1], None, ALU.mult))
                mod_chain.sync()
                dve.sem_inc(mod_ready, 1)

            ch = mod_chain = Chain(dve, mod_step)
            ch.step(V.memset(c.state[:], 0.0))
            ch.step(V.memset(c.scoreT[:], 0.0))
            dve.wait_ge(turned, 1)
            ch.step(V.tensor_copy(c.taps[:], pO[:, 0:NCH * CW]))
            ch.step(V.tensor_copy(c.cols[:], pS[:, 0:NVEC]))
            ch.sync()
            dve.sem_inc(cols_ready, 1)
            lb0 = VEC["lb_logits"][0]
            l0, l1 = c.cols[:, lb0:lb0 + NCH], c.cols[:, lb0 + NCH:lb0 + 2 * NCH]
            ch.link(V.tensor_tensor(lbt[:, 0], l0, l1, ALU.max))
            ch.step(V.tensor_tensor(lbt[:, 1], l0, lbt[:, 0], ALU.subtract))
            ch.link(V.tensor_tensor(lbt[:, 2], l1, lbt[:, 0], ALU.subtract))
            dve.sem_inc(lb_in, 1)
            dve.wait_ge(cond_ready, 2)
            ch.link(V.tensor_tensor(lbt[:, 3], lbt[:, 1], lbt[:, 2], ALU.add))
            ch.link(V.reciprocal(lbt[:, 0], lbt[:, 3]))
            ch.link(V.tensor_tensor(c.lb[:], lbt[:, 1], lbt[:, 0], ALU.mult))
            ch.step(V.tensor_scalar(c.oneless[:], c.lb[:], -1.0, 1.0, ALU.mult, ALU.add))
            norm_in(0, 0)
            norm_in(0, 1)
            ada_sums(0)
            ada_sums(1)
            dve.wait_ge(ada_cols_done, 2)
            mod_chain.link(V.tensor_tensor(mod[:, 0:2 * KD], pT[:, 0:2 * KD], c.cols[:, VEC["b_ada"][0]:VEC["b_ada"][0] + 2 * KD], ALU.add))
            mod_chain.step(V.scalar_tensor_tensor(out=c.scale1[:], in0=m_of(1), scalar=1.0, in1=cols("g_pre_mix"),
                                                  op0=ALU.add, op1=ALU.mult))
            mod_chain.link(V.tensor_copy(c.shift1[:], m_of(0)))
            dve.sem_inc(scale1_ready, 1)
            modulate(0, 0, bank[1])
            modulate(0, 1, bank[3])
            norm_in(0, 2)
            norm_in(0, 3)
            rest_of_piece(0, 0)
            rest_of_piece(0, 1)
            modulate(0, 2, bank[1])
            modulate(0, 3, bank[3])
            for i in range(NT):
                rest_of_input(0, i)
            conv(0, with_ada=True)
            heads(0)
            dve.wait_ge(ada_cols_done, 4)
            mod_chain.link(V.tensor_tensor(mod[:, 2 * KD:4 * KD], pT[:, 2 * KD:4 * KD],
                                           c.cols[:, VEC["b_ada"][0] + 2 * KD:VEC["b_ada"][0] + 4 * KD], ALU.add))
            dve.sem_inc(mod_ready, 1)
            steps(0, True, False, True, {("osave", 0): lambda: ada_sums(4, (0,)), ("osave", 1): lambda: ada_sums(4, (1,)),
                                         ("osave", 2): lambda: ada_sums(5, (0,)), ("oms", 2): lambda: ada_sums(5, (1,)),
                                         ("osave", 3): last_modulation})
            with dve.Fori(1, NB - 1) as t:
                conv(t)
                heads(t)
                steps(t, True, True, True)
            conv(NB - 1)
            heads(NB - 1)
            steps(NB - 1, True, True, False)
            steps(NB, False, True, False)


def routing_phase(nc, ap, c):
    with ExitStack() as ctx:
        sb = lambda n, s, d=F32: ctx.enter_context(nc.sbuf_tensor(n, s, d))
        sem = lambda n: ctx.enter_context(nc.semaphore(n))
        BIG = 1e30
        NA = 2 * NTILES
        lane, blk = sb("lane", [P, P]), sb("blk", [P, TAB])
        token, blkrow = sb("token", [P, NTILES]), sb("blkrow", [P, 16])
        tri, one16 = sb("tri16", [P, P], BF16), sb("one16", [P, P], BF16)
        trif = sb("trif", [P, P])
        t16 = [sb(f"t16_{i}", [P, NTILES]) for i in range(12)]
        g4 = [sb(f"g4_{i}", [P, NTILES, NG]) for i in range(3)]
        e8 = [sb(f"e8_{i}", [P, NTILES, NEG]) for i in range(6)]
        big = [sb(f"big{i}", [P, NTILES, NE]) for i in range(4)]
        hot = sb("hot", [P, NTILES, NE], BF16)
        cum = sb("cum", [P, NTILES + 1, NE], BF16)
        x32 = [sb(f"x32_{i}", [P, NE]) for i in range(4)]
        cmp_ = sb("cmp", [P, TAB, NE])
        destf, rowi, blki = sb("destf", [P, NA]), sb("rowi", [P, NA], I32), sb("blki", [P, NA], I32)
        rowf, blkf = sb("rowf", [P, NA]), sb("blkf", [P, NA])
        RING = 8
        at_row, at_blk = sb("at_row", [P, RING, P]), sb("at_blk", [P, RING, TAB])
        etab = sb("etab", [P, TAB])
        pr = ctx.enter_context(nc.psum_tensor("prank", [P, 512], F32))
        pc = ctx.enter_context(nc.psum_tensor("pcount", [P, 512], F32))
        pi = ctx.enter_context(nc.psum_tensor("pindex", [P, 512], F32))
        iota_done, tri_done, dve_step = sem("iota_done"), sem("tri_done"), sem("route_step")
        group_in, group_exp, expert_in, expert_exp = sem("group_in"), sem("group_exp"), sem("expert_in"), sem("expert_exp")
        row_ready, onehot_ready, fourth_ready = sem("row_ready"), sem("onehot_ready"), sem("fourth_ready")
        hot_ready, rank_ready, onehot_used = sem("hot_ready"), sem("rank_ready"), sem("onehot_used")
        block = ctx.enter_context(nc.Block())

        @block.sync
        def _(sp):
            for e in range(WSLOTS):
                load_expert(sp, ap, c, e, e)

        @block.gpsimd
        def _(pool):
            io = lambda out, n, **k: nc.gpsimd.iota(out, [[1, n]], base=0, allow_small_or_imprecise_dtypes=True, **k)
            io(lane[:], P, channel_multiplier=0)
            io(blk[:], TAB, channel_multiplier=0)
            nc.gpsimd.iota(blkrow[:], [[P, 16]], base=0, channel_multiplier=0, allow_small_or_imprecise_dtypes=True)
            nc.gpsimd.iota(token[:], [[P, NTILES]], base=0, channel_multiplier=1, allow_small_or_imprecise_dtypes=True)
            nc.gpsimd.memset(trif[:], 1.0).then_inc(tri_done, 1)
            pool.wait_ge(tri_done, 1)
            nc.gpsimd.affine_select(out=trif[:], in_=trif[:], compare_op=ALU.is_gt, fill=0.0,
                                    base=0, pattern=[[1, P]], channel_multiplier=-1).then_inc(iota_done, 1)
            pool.wait_ge(row_ready, 1)
            for n in range(3, NA, 4):
                if n >= RING:
                    pool.wait_ge(onehot_used, (n - RING) // 4 + 1)
                i = n % NTILES
                nc.gpsimd.tensor_scalar(at_blk[:, n % RING], blk[:], blkf[:, n:n + 1], token[:, i:i + 1],
                                        ALU.is_equal, ALU.mult).then_inc(fourth_ready, 1)

        @block.scalar
        def _(act):
            act.wait_ge(group_in, 1)
            nc.scalar.activation(g4[1][:], g4[0][:], ACT.Exp).then_inc(group_exp, 1)
            act.wait_ge(expert_in, 1)
            nc.scalar.activation(e8[2][:], e8[1][:], ACT.Exp)
            nc.scalar.activation(t16[5][:], t16[4][:], ACT.Exp).then_inc(expert_exp, 1)

        @block.tensor
        def _(pe):
            pe.wait_ge(hot_ready, 1)
            flat = lambda a: a.rearrange("p t e -> p (t e)")
            nc.tensor.matmul(pr[:], tri[:], flat(hot[:]), start=True, stop=False)
            nc.tensor.matmul(pr[:], one16[:], flat(cum[:, 0:NTILES]), start=False, stop=True)
            nc.tensor.matmul(pc[:, 0:NE], one16[:], cum[:, NTILES], start=True, stop=True).then_inc(rank_ready, 1)
            for n in range(NA):
                if n % 4 == 0:
                    pe.wait_ge(onehot_ready, n // 4 * 3 + 3)
                    pe.wait_ge(fourth_ready, n // 4 + 1)
                last = nc.tensor.matmul(pi[:, 0:TAB], at_row[:, n % RING], at_blk[:, n % RING], start=(n == 0), stop=(n == NA - 1))
                if n % 4 == 3:
                    last.then_inc(onehot_used, 1)

        @block.vector
        def _(dve):
            V = nc.vector
            L = Chain(dve, dve_step).link
            bc = lambda a, n: a.unsqueeze(2).to_broadcast([P, a.shape[1], n])
            dve.wait_ge(iota_done, 1)
            L(V.tensor_copy(tri[:], trif[:]))
            L(V.tensor_copy(one16[:], c.ones[:]))

            def first_max(vals, best, diff, cand, index, onehot, n):
                L(V.tensor_reduce(best[:], vals, axis=AX.X, op=ALU.max))
                L(V.tensor_tensor(diff[:], vals, bc(best[:], n), ALU.subtract))
                L(V.tensor_scalar(cand[:], diff[:], 0.0, -64.0, ALU.is_ge, ALU.mult))
                L(V.tensor_tensor(cand[:], cand[:], lane[:, 0:n].unsqueeze(1).to_broadcast([P, NTILES, n]), ALU.add))
                L(V.tensor_reduce(index[:], cand[:], axis=AX.X, op=ALU.min))
                L(V.tensor_tensor(onehot[:], cand[:], bc(index[:], n), ALU.is_equal))

            gl = c.logits[:, :, 0:NG]
            first_max(gl, t16[0], g4[0], g4[1], t16[1], g4[2], NG)
            dve.sem_inc(group_in, 1)
            dve.wait_ge(group_exp, 1)
            L(V.tensor_reduce(t16[2][:], g4[1][:], axis=AX.X, op=ALU.add))
            L(V.reciprocal(t16[2][:], t16[2][:]))
            el = c.logits[:, :, NG:NR].rearrange("p t (g e) -> p t g e", g=NG)
            b4 = big[0][:].rearrange("p t (g e) -> p t g e", g=NG)
            L(V.tensor_tensor(b4, el, g4[2][:].unsqueeze(3).to_broadcast([P, NTILES, NG, NEG]), ALU.mult))
            L(V.tensor_reduce(e8[0][:], big[0][:].rearrange("p t (g e) -> p t e g", g=NG), axis=AX.X, op=ALU.add))
            first_max(e8[0][:], t16[3], e8[1], e8[2], t16[1], e8[3], NEG)
            L(V.scalar_tensor_tensor(out=e8[0][:], in0=e8[3][:], scalar=-BIG, in1=e8[0][:], op0=ALU.mult, op1=ALU.add))
            first_max(e8[0][:], t16[6], e8[5], e8[2], t16[1], e8[4], NEG)
            L(V.tensor_tensor(t16[4][:], t16[6][:], t16[3][:], ALU.subtract))
            dve.sem_inc(expert_in, 1)
            dve.wait_ge(expert_exp, 1)
            L(V.tensor_reduce(t16[7][:], e8[2][:], axis=AX.X, op=ALU.add))
            L(V.reciprocal(t16[7][:], t16[7][:]))
            L(V.tensor_tensor(t16[8][:], t16[5][:], t16[7][:], ALU.mult))
            L(V.tensor_tensor(t16[9][:], t16[8][:], t16[7][:], ALU.add))
            L(V.reciprocal(t16[9][:], t16[9][:]))
            L(V.tensor_tensor(t16[9][:], t16[9][:], t16[2][:], ALU.mult))
            L(V.tensor_tensor(c.weight[:, 0], t16[7][:], t16[9][:], ALU.mult))
            L(V.tensor_tensor(c.weight[:, 1], t16[8][:], t16[9][:], ALU.mult))
            for k in range(2):
                L(V.tensor_tensor(big[k][:].rearrange("p t (g e) -> p t g e", g=NG),
                                  g4[2][:].unsqueeze(3).to_broadcast([P, NTILES, NG, NEG]),
                                  e8[3 + k][:].unsqueeze(2).to_broadcast([P, NTILES, NG, NEG]), ALU.mult))
            L(V.tensor_tensor(hot[:], big[0][:], big[1][:], ALU.add))
            L(V.memset(cum[:, 0], 0.0))
            for i in range(NTILES):
                L(V.tensor_tensor(cum[:, i + 1], cum[:, i], hot[:, i], ALU.add))
            dve.sem_inc(hot_ready, 1)
            dve.wait_ge(rank_ready, 1)
            L(V.tensor_copy(x32[0][:], pc[:, 0:NE]))
            c3 = cmp_[:].rearrange("p a b -> p (a b)")[:, 0:NE * 16].rearrange("p (e m) -> p e m", e=NE)
            L(V.tensor_tensor(c3, bc(x32[0][:], 16), blkrow[:].unsqueeze(1).to_broadcast([P, NE, 16]), ALU.is_gt))
            L(V.tensor_reduce(x32[1][:], c3, axis=AX.X, op=ALU.add))
            L(V.tensor_tensor_scan(x32[2][:], c.ones[:, 0:NE], x32[1][:], 0.0, ALU.mult, ALU.add))
            L(V.tensor_scalar(c.block_end[:], x32[2][:], 2.0, 1.0, ALU.mult, ALU.add))
            L(V.tensor_tensor(x32[3][:], x32[2][:], x32[1][:], ALU.subtract))
            L(V.tensor_scalar(x32[3][:], x32[3][:], float(P), None, ALU.mult))
            L(V.tensor_tensor(big[2][:], pr[:].rearrange("p (t e) -> p t e", e=NE),
                              x32[3][:].unsqueeze(1).to_broadcast([P, NTILES, NE]), ALU.add))
            for k in range(2):
                L(V.tensor_tensor(big[3][:], big[2][:], big[k][:], ALU.mult))
                L(V.tensor_reduce(destf[:, k * NTILES:(k + 1) * NTILES], big[3][:], axis=AX.X, op=ALU.add))
            L(V.tensor_copy(c.dest[:].rearrange("p k t -> p (k t)"), destf[:]))
            di = c.dest[:].rearrange("p k t -> p (k t)")
            L(V.tensor_scalar(blki[:], di, 7, None, ALU.arith_shift_right))
            L(V.tensor_scalar(rowi[:], di, P - 1, None, ALU.bitwise_and))
            L(V.tensor_copy(blkf[:], blki[:]))
            L(V.tensor_copy(rowf[:], rowi[:]))
            dve.sem_inc(row_ready, 1)
            for n in range(0, NA, 4):
                if n >= RING:
                    dve.wait_ge(onehot_used, (n - RING) // 4 + 1)
                at = n % RING
                V.tensor_tensor(at_row[:, at:at + 4], lane[:].unsqueeze(1).to_broadcast([P, 4, P]),
                                bc(rowf[:, n:n + 4], P), ALU.is_equal)
                for j in range(3):
                    i = (n + j) % NTILES
                    V.tensor_scalar(at_blk[:, at + j], blk[:], blkf[:, n + j:n + j + 1], token[:, i:i + 1],
                                    ALU.is_equal, ALU.mult).then_inc(onehot_ready, 1)
            L(V.tensor_tensor(cmp_[:], x32[2][:].unsqueeze(1).to_broadcast([P, TAB, NE]), bc(blk[:], NE), ALU.is_le))
            L(V.tensor_reduce(etab[:], cmp_[:], axis=AX.X, op=ALU.add))
            L(V.tensor_scalar(etab[:], etab[:], float(NE - 1), None, ALU.min))
            L(V.scalar_tensor_tensor(out=c.expert_pair[:, 0:TAB - 1], in0=etab[:, 0:TAB - 1], scalar=float(NE), in1=etab[:, 1:TAB],
                                     op0=ALU.mult, op1=ALU.add))
            L(V.tensor_scalar(x32[0][:, 0:1], x32[2][:, NE - 1:NE], 1.0, None, ALU.add))
            L(V.tensor_copy(c.pairs[:], x32[0][:, 0:1]))
            L(V.tensor_scalar(c.pairs[:], c.pairs[:], 1, None, ALU.arith_shift_right))
            dve.wait_ge(onehot_used, NA // 4)
            L(V.tensor_copy(c.block_token[:], pi[:, 0:TAB]))


def load_expert(eng, ap, c, e, s):
    w = lambda name: ap[name][0][bass.ds(e, 1)].rearrange("a (k p) n -> p (a k) n", p=P)
    eng.dma_start(c.wgu[:, s, :, 0:FE], w("w_gate")).then_inc(c.w_in[s], 16)
    eng.dma_start(c.wgu[:, s, :, FE:2 * FE], w("w_up")).then_inc(c.w_in[s], 16)
    eng.dma_start(c.wd[:, s], w("w_down")).then_inc(c.w_in[s], 16)


def expert_phase(nc, ap, c):
    with ExitStack() as ctx:
        sb = lambda n, s, d=F32: ctx.enter_context(nc.sbuf_tensor(n, s, d))
        sem = lambda n: ctx.enter_context(nc.semaphore(n))
        psum = lambda n: ctx.enter_context(nc.psum_tensor(n, [P, 512], F32))
        xg = sb("xg", [P, 2, D])
        xT = sb("xTe", [P, KD, P])
        sg, hh = sb("sg", [P, FE]), sb("hh", [P, FE])
        hT = sb("hTe", [P, FE // P, P])
        yb = sb("yb", [P, 2, D])
        diag = sb("diag2", [P, KD, P])
        rows = sb("rows", [P, 2], I32)
        diag_ready, row_done = sem("diag2_ready"), sem("row2_done")
        pt = [psum("pt0"), psum("pt1")]
        pgate, pup, ph = psum("pgate"), psum("pup"), psum("ph")
        py = [psum("py0"), psum("py1")]
        experts_loaded = sem("experts_loaded")
        row_copied, xg_in = sem("row_copied"), [sem("xg_in0"), sem("xg_in1")]
        x_turned, xT_act, xT_dve = sem("x_turned"), sem("xT_act"), sem("xT_dve")
        gate_ready, up_ready, silu_ready, hh_ready = sem("gate_ready"), sem("up_ready"), sem("silu_ready"), sem("hh_ready")
        h_turned, hT_ready, y_ready, y_act, y_dve = sem("h_turned"), sem("hT_e"), sem("y_e"), sem("y_act"), sem("y_dve")
        y_stored = [sem("y_stored0"), sem("y_stored1")]
        pool_passed, sp_passed = sem("pool_passed_e"), sem("sp_passed_e")
        block = ctx.enter_context(nc.Block())

        def load_pairs(eng):
            return eng.value_load(c.pairs[0:1, 0:1], min_val=1, max_val=NBLK // 2)

        @block.sync
        def _(sp):
            def announce(s, turn):
                sp.wait_ge(c.w_in[s], 48 * turn)
                sp.sem_inc(experts_loaded, 1)

            def load_x1(n):
                sp.dma_start(c.x1_all[:, bass.ds(2 * n, 2)], ap["x1"][bass.ds(2 * n * P, 2 * P), :]
                             .rearrange("(t p) n -> p t n", p=P)).then_inc(c.x1_in, 16)

            for s in range(WSLOTS - 1):
                announce(s, 1)
            with sp.Fori(1, NE // WSLOTS) as g:
                for s in range(WSLOTS):
                    last = sp.value_load(c.block_end[0:1, bass.ds((g - 1) * WSLOTS + s, 1)], min_val=1, max_val=2 * NBLK + 1)
                    wait_apart(sp, y_ready, last, sp_passed)
                    load_expert(sp, ap, c, g * WSLOTS + s, s)
                    if s == 0:
                        announce(WSLOTS - 1, g)
                        load_x1(g - 1)
                    else:
                        announce(s - 1, g + 1)
            announce(WSLOTS - 1, NE // WSLOTS)
            load_x1(NE // WSLOTS - 1)

        @block.gpsimd
        def _(pool):
            def fetch(b, s, n):
                nc.gpsimd.tensor_copy(rows[:, s:s + 1], c.block_token[:, bass.ds(b, 1)]).then_inc(row_copied, 1)
                wait_apart(pool, row_copied, n, pool_passed)
                pool.indirect_dma_start(xg[:, s], None, ap["xn"], bass.IndirectOffsetOnAxis(rows[:, s:s + 1], 0)).then_inc(xg_in[s], 16)

            fetch(0, 0, 1)
            fetch(1, 1, 2)
            n_pairs = load_pairs(pool)
            with pool.Fori(0, n_pairs) as q:
                for s in range(2):
                    b = 2 * q + s
                    wait_apart(pool, x_turned, 2 * b + 2, pool_passed)
                    fetch(b + 2, s, b + 3)
                    pool.wait_ge(y_act, b + 1)
                    wait_apart(pool, y_dve, b + 1, pool_passed)
                    pool.dma_start(ap["y"][bass.ds(b * P, P), :], yb[:, s]).then_inc(y_stored[s], 16)
            for s in range(2):
                wait_apart(pool, y_stored[s], n_pairs * 16, pool_passed)
                wait_apart(pool, xg_in[s], n_pairs * 16 + 16, pool_passed)

        @block.tensor
        def _(pe):
            def turn_half(half, s):
                for j in range(4):
                    k = 4 * half + j
                    last = nc.tensor.transpose(pt[half][:, j * P:(j + 1) * P], xg[:, s, k * P:(k + 1) * P], c.ident[:])
                last.then_inc(x_turned, 1)

            def turn(s, times):
                pe.wait_ge(xg_in[s], 16 * times)
                turn_half(0, s)
                turn_half(1, s)

            def experts_of(b):
                both = pe.value_load(c.expert_pair[0:1, bass.ds(b, 1)], min_val=0, max_val=NE * NE - 1)
                return both // NE, both % NE

            def hidden_products(b, expert):
                pe.wait_ge(experts_loaded, expert + 1)
                pe.wait_ge(xT_act, b + 1)
                pe.wait_ge(xT_dve, b + 1)
                for out, cols, done in ((pgate, 0, gate_ready), (pup, FE, up_ready)):
                    for k in range(KD):
                        last = nc.tensor.matmul(out[:, 0:FE], xT[:, k, :],
                                                c.wgu[:, bass.ds(expert % WSLOTS, 1), k, cols:cols + FE].rearrange("p a n -> p (a n)"),
                                                start=(k == 0), stop=(k == KD - 1))
                    last.then_inc(done, 1)

            def down_products(b, expert):
                pe.wait_ge(hT_ready, b + 1)
                wait(pe, y_act, b)
                wait(pe, y_dve, b)
                for half in range(2):
                    for k in range(FE // P):
                        last = nc.tensor.matmul(py[half][:], hT[:, k, :],
                                                c.wd[:, bass.ds(expert % WSLOTS, 1), k, half * 512:(half + 1) * 512].rearrange("p a n -> p (a n)"),
                                                start=(k == 0), stop=(k == FE // P - 1))
                    last.then_inc(y_ready, 1)

            def finish(b, s, times):
                pe.wait_ge(xg_in[1 - s], 16 * times)
                turn_half(0, 1 - s)
                pe.wait_ge(hh_ready, b + 1)
                for k in range(FE // P):
                    last = nc.tensor.transpose(ph[:, k * P:(k + 1) * P], hh[:, k * P:(k + 1) * P], c.ident[:])
                last.then_inc(h_turned, 1)
                turn_half(1, 1 - s)
                expert, next_expert = experts_of(b)
                down_products(b, expert)
                hidden_products(b + 1, next_expert)

            pe.wait_ge(diag_ready, 1)
            for r in range(2):
                last = nc.tensor.matmul(py[r][:], c.ones[:], diag[:, 4 * r:4 * r + 4].rearrange("p a b -> p (a b)"), start=True, stop=True)
            last.then_inc(row_done, 1)
            pe.sem_inc(y_ready, 1)
            turn(0, 1)
            hidden_products(0, experts_of(0)[0])
            with pe.Fori(0, load_pairs(pe)) as q:
                for s in range(2):
                    finish(2 * q + s, s, q + 1 + s)

        @block.scalar
        def _(act):
            A = nc.scalar.activation

            def evacuate(b):
                act.wait_ge(x_turned, 2 * b + 1)
                wait(act, up_ready, b)
                for k in range(4):
                    last = A(xT[:, k, :], pt[0][:, k * P:(k + 1) * P], ACT.Identity, scale=c.scale2[:, k:k + 1], bias=c.shift2[:, k:k + 1])
                last.then_inc(xT_act, 1)

            evacuate(0)
            with act.Fori(0, load_pairs(act)) as q:
                for s in range(2):
                    b = 2 * q + s
                    act.wait_ge(gate_ready, b + 1)
                    act.wait_ge(hh_ready, b)
                    A(sg[:], pgate[:, 0:FE], ACT.Silu).then_inc(silu_ready, 1)
                    evacuate(b + 1)
                    act.wait_ge(y_ready, 2 * b + 2)
                    act.wait_ge(y_stored[s], q * 16)
                    A(yb[:, s, 0:512], py[0][:], ACT.Copy).then_inc(y_act, 1)

        @block.vector
        def _(dve):
            V = nc.vector

            def evacuate(b):
                dve.wait_ge(x_turned, 2 * b + 2)
                wait(dve, up_ready, b)
                for j in range(4):
                    k = 4 + j
                    last = V.tensor_scalar(xT[:, k, :], pt[1][:, j * P:(j + 1) * P], c.scale2[:, k:k + 1], c.shift2[:, k:k + 1], ALU.mult, ALU.add)
                last.then_inc(xT_dve, 1)

            for k in range(KD):
                last = V.tensor_scalar(diag[:, k], c.ident[:], c.gcol[:, KD + k:KD + k + 1], None, ALU.mult)
            last.then_inc(diag_ready, 1)
            dve.wait_ge(row_done, 1)
            for r in range(2):
                V.tensor_copy(c.grow2[:, r * 512:(r + 1) * 512], py[r][:])
            evacuate(0)
            with dve.Fori(0, load_pairs(dve)) as q:
                for s in range(2):
                    b = 2 * q + s
                    dve.wait_ge(silu_ready, b + 1)
                    dve.wait_ge(up_ready, b + 1)
                    dve.wait_ge(h_turned, b)
                    V.tensor_tensor(hh[:], pup[:, 0:FE], sg[:], ALU.mult).then_inc(hh_ready, 1)
                    dve.wait_ge(h_turned, b + 1)
                    dve.wait_ge(y_ready, 2 * b + 1)
                    V.tensor_copy(hT[:].rearrange("p a b -> p (a b)"), ph[:, 0:FE]).then_inc(hT_ready, 1)
                    evacuate(b + 1)
                    dve.wait_ge(y_ready, 2 * b + 3)
                    dve.wait_ge(y_stored[s], q * 16)
                    V.tensor_copy(yb[:, s, 512:D], py[1][:]).then_inc(y_dve, 1)


def combine_phase(nc, ap, c, out):
    with ExitStack() as ctx:
        sb = lambda n, s, d=F32: ctx.enter_context(nc.sbuf_tensor(n, s, d))
        sem = c.sem
        RING = 4
        ya, yb = sb("ya", [P, RING, D]), sb("yb2", [P, RING, D])
        junk = sb("junk", [P, D])
        rows = sb("rows2", [P, 2 * RING], I32)
        ss = sb("ss", [P, RING])
        row_copied = sem("row2_copied")
        ya_in, yb_in = [sem(f"ya_in{s}") for s in range(RING)], [sem(f"yb_in{s}") for s in range(RING)]
        out_stored = sem("out_stored")
        scaled, y_sum, act_step, rstd_ready, gated, out_ready = (
            sem("scaled"), sem("y_sum"), sem("act_step2"), sem("rstd_ready"), sem("gated"), sem("out_ready"))
        pool_passed, sp_passed = sem("pool_passed2"), sem("sp_passed2")
        block = ctx.enter_context(nc.Block())
        ROUNDS = NTILES // RING
        tile_of = lambda q, s: q * RING + s

        @block.gpsimd
        def _(pool):
            def fetch(q, s):
                i = tile_of(q, s)
                for k, (buf, done) in enumerate(((ya, ya_in), (yb, yb_in))):
                    at = 2 * s + k
                    nc.gpsimd.tensor_copy(rows[:, at:at + 1], c.dest[:, k, bass.ds(i, 1)]).then_inc(row_copied, 1)
                    wait_apart(pool, row_copied, 2 * i + k + 1, pool_passed)
                    pool.indirect_dma_start(buf[:, s], None, ap["y"], bass.IndirectOffsetOnAxis(rows[:, at:at + 1], 0)).then_inc(done[s], 16)

            for s in range(RING):
                fetch(0, s)
            with pool.Fori(1, ROUNDS) as q:
                for s in range(RING):
                    wait_apart(pool, out_ready, tile_of(q, s) - RING + 1, pool_passed)
                    fetch(q, s)

        @block.scalar
        def _(act):
            A = nc.scalar.activation

            def scale(q, s):
                act.wait_ge(ya_in[s], 16 * q + 16)
                A(ya[:, s], ya[:, s], ACT.Copy, scale=c.weight[:, 0, bass.ds(tile_of(q, s), 1)]).then_inc(scaled, 1)

            def rstd(q, s):
                i = tile_of(q, s)
                act.wait_ge(y_sum, i + 1)
                A(junk[:], ya[:, s], ACT.Square, accum_out=ss[:, s:s + 1]).then_inc(act_step, 1)
                act.wait_ge(act_step, 2 * i + 1)
                A(ss[:, s:s + 1], ss[:, s:s + 1], ACT.Ln, bias=c.epsc[:], scale=1.0 / D).then_inc(act_step, 1)
                act.wait_ge(act_step, 2 * i + 2)
                A(ss[:, s:s + 1], ss[:, s:s + 1], ACT.Exp, scale=-0.5).then_inc(rstd_ready, 1)

            act.preload_act_table_set("natural_log_exp_and_others")
            scale(0, 0)
            with act.Fori(0, ROUNDS - 1) as q:
                for s in range(RING):
                    scale(q + (s + 1) // RING, (s + 1) % RING)
                    rstd(q, s)
            for s in range(RING):
                if s < RING - 1:
                    scale(ROUNDS - 1, s + 1)
                rstd(ROUNDS - 1, s)

        @block.vector
        def _(dve):
            V = nc.vector

            def weigh(q, s):
                i = tile_of(q, s)
                dve.wait_ge(scaled, i + 1)
                dve.wait_ge(yb_in[s], 16 * q + 16)
                V.scalar_tensor_tensor(out=ya[:, s], in0=yb[:, s], scalar=c.weight[:, 1, bass.ds(i, 1)], in1=ya[:, s],
                                       op0=ALU.mult, op1=ALU.add).then_inc(y_sum, 1)

            def finish(q, s):
                i = tile_of(q, s)
                dve.wait_ge(rstd_ready, i + 1)
                V.scalar_tensor_tensor(out=ya[:, s], in0=ya[:, s], scalar=ss[:, s:s + 1], in1=c.grow2[:],
                                       op0=ALU.mult, op1=ALU.mult).then_inc(gated, 1)
                dve.wait_ge(gated, i + 1)
                x1 = c.x1_all[:, bass.ds(i, 1)].rearrange("p a n -> p (a n)")
                V.tensor_tensor(x1, x1, ya[:, s], ALU.add).then_inc(out_ready, 1)

            dve.wait_ge(c.x1_in, NTILES // 2 * 16)
            weigh(0, 0)
            with dve.Fori(0, ROUNDS - 1) as q:
                for s in range(RING):
                    weigh(q + (s + 1) // RING, (s + 1) % RING)
                    finish(q, s)
            for s in range(RING):
                if s < RING - 1:
                    weigh(ROUNDS - 1, s + 1)
                finish(ROUNDS - 1, s)

        @block.sync
        def _(sp):
            with sp.Fori(0, NTILES) as i:
                wait_apart(sp, out_ready, i + 1, sp_passed)
                sp.dma_start(out[bass.ds(i * P, P), :], c.x1_all[:, bass.ds(i, 1)].rearrange("p a n -> p (a n)")).then_inc(out_stored, 16)
            sp.wait_ge(out_stored, NTILES * 16)


INPUTS = ["x", "c", "w_ada", "b_ada", "g_pre_mix", "g_post_mix", "w_in", "dw_kernel", "dw_bias",
          "conv_ln_gain", "conv_ln_bias", "lb_logits", "rec_norm_gain", "w_out", "g_pre_ffn", "g_post_ffn",
          "w_router_group", "b_router_group", "w_router_expert", "b_router_expert", "w_gate", "w_up", "w_down"]


class Kept:
    pass


def build(nc, ap, out):
    c = Kept()
    with ExitStack() as ctx:
        sb = lambda n, s, d=F32: ctx.enter_context(nc.sbuf_tensor(n, s, d))
        c.ident, c.ones, c.causal = (sb(n, [P, P]) for n in ("ident", "ones", "causal"))
        c.cols = sb("cols", [P, NVEC])
        c.epsc = sb("epsc", [P, 1])
        c.scale1, c.shift1, c.scale2, c.shift2 = (sb(n, [P, KD]) for n in ("scale1", "shift1", "scale2", "shift2"))
        c.gcol = sb("gcol", [P, 2 * KD])
        c.logits = sb("logits", [P, NTILES, NR])
        ap["x1"] = nc.dram_tensor("x1_dram", (SEQ, D), F32, kind=DEBUG_KIND).ap()
        ap["xn"] = nc.dram_tensor("xn_dram", (SEQ, D), F32, kind=DEBUG_KIND).ap()
        ap["y"] = nc.dram_tensor("y_dram", (NBLK * P, D), F32, kind="Internal").ap()
        with ExitStack() as mix:
            mb = lambda n, s, d=F32: mix.enter_context(nc.sbuf_tensor(n, s, d))
            c.restart = mb("restart", [P, T])
            c.zeros = mb("zeros", [P, 64])
            c.wroute = mb("wroute", [P, KD, NR])
            c.brow = mb("brow", [1, NR])
            c.taps = mb("taps", [P, NCH * CW])
            c.lb, c.oneless = mb("lb", [P, NCH]), mb("oneless", [P, NCH])
            c.grow = mb("grow", [P, D])
            c.state = mb("state", [P, 4, DC])
            c.scoreT = mb("scoreT", [P, 2, DC])
            mixer_phase(nc, ap, c)
        c.weight = sb("weight", [P, 2, NTILES])
        c.dest = sb("dest", [P, 2, NTILES], I32)
        c.block_token = sb("block_token", [P, TAB], I32)
        c.expert_pair = sb("expert_pair", [P, TAB], I32)
        c.block_end, c.pairs = sb("block_end", [P, NE], I32), sb("pairs", [P, 1], I32)
        c.sem = lambda n: ctx.enter_context(nc.semaphore(n))
        c.wgu = sb("wgu", [P, WSLOTS, KD, 2 * FE])
        c.wd = sb("wd", [P, WSLOTS, FE // P, D])
        c.w_in = [ctx.enter_context(nc.semaphore(f"w_in{i}")) for i in range(WSLOTS)]
        c.x1_all, c.grow2 = sb("x1_all", [P, NTILES, D]), sb("grow2", [P, D])
        c.x1_in = ctx.enter_context(nc.semaphore("x1_in"))
        routing_phase(nc, ap, c)
        expert_phase(nc, ap, c)
        combine_phase(nc, ap, c, out[0])


DEBUG_KIND = "Internal"


def kernel(**inputs):
    import numpy as np
    import concourse.bacc as bacc
    from concourse.bass_utils import run_bass_kernel_spmd

    nc = bacc.Bacc("TRN2", target_bir_lowering=False, num_devices=1)
    arrays, ap = {}, {}
    for name in INPUTS:
        a = np.ascontiguousarray(inputs[name])
        arrays[f"{name}_in"] = a
        ap[name] = nc.dram_tensor(f"{name}_in", a.shape, mybir.dt.from_np(a.dtype), kind="ExternalInput").ap()
    out = nc.dram_tensor("out", (1, SEQ, D), F32, kind="ExternalOutput").ap()
    build(nc, ap, out)
    r = run_bass_kernel_spmd(nc, [arrays], core_ids=[0])
    return r.results[0]["out"]
```
